# Optimizing a Trainium2 kernel written in Bass

```python
import math
import jax, jax.numpy as jnp
from jax import lax
import numpy as np

D_MODEL = 2048
BATCH = 1
SEQ = 1024
DEPTH = 1

CHUNK = 64
N_MEM = 256
EPS = 1e-6
A_HEADS = 16
A_KV_HEADS = 2
A_HEAD_DIM = 64
WINDOW = 128
WINDOW_CHUNKS = WINDOW // CHUNK
A_WIDTH = A_HEADS * A_HEAD_DIM
B_HEADS = 4
B_HEAD_DIM = 128
B_WIDTH = B_HEADS * B_HEAD_DIM
IDX_HEADS = 4
IDX_DIM = 64
TOPK_MAX = 256
Q_BLOCK = 128
C_HEADS = 4
C_HEAD_DIM = 128
C_WIDTH = C_HEADS * C_HEAD_DIM
MIX_WIDTH = A_WIDTH + B_WIDTH + C_WIDTH
N_BUCKETS = 32
MAX_DISTANCE = 1024
N_BIAS_HEADS = A_HEADS + B_HEADS
SPLIT_SIZES = (A_WIDTH, A_KV_HEADS * A_HEAD_DIM, A_KV_HEADS * A_HEAD_DIM,
               B_WIDTH, B_WIDTH, B_WIDTH,
               IDX_HEADS * IDX_DIM, IDX_DIM, IDX_HEADS,
               C_WIDTH, MIX_WIDTH)
IN_WIDTH = sum(SPLIT_SIZES)

kernel_name = "hybrid_chunk_causal_swa_dsa_memory_block"

def rms_norm(x, g):
    xf = x.astype(jnp.float32)
    y = xf * lax.rsqrt(jnp.mean(xf * xf, axis=-1, keepdims=True) + EPS)
    return (y * g.astype(jnp.float32)).astype(x.dtype)

def t5_bucket(rel):
    nb = N_BUCKETS // 2
    max_exact = nb // 2
    side = jnp.where(rel > 0, nb, 0)
    n = jnp.abs(rel)
    nf = jnp.maximum(n, max_exact).astype(jnp.float32)
    large = max_exact + (jnp.log(nf / max_exact) / math.log(MAX_DISTANCE / max_exact)
                         * (nb - max_exact)).astype(jnp.int32)
    large = jnp.minimum(large, nb - 1)
    return side + jnp.where(n < max_exact, n, large)

def sliding_window_sink_attention(q, k, v, sinks, rel_bias):
    b, s = q.shape[0], q.shape[1]
    nc = s // CHUNK
    grp = A_HEADS // A_KV_HEADS
    pad = WINDOW_CHUNKS * CHUNK
    nk = (WINDOW_CHUNKS + 1) * CHUNK
    qc = q.reshape(b, nc, CHUNK, A_KV_HEADS, grp, A_HEAD_DIM)

    def band(t):
        tp = jnp.pad(t, ((0, 0), (pad, 0), (0, 0), (0, 0)))
        tp = tp.reshape(b, nc + WINDOW_CHUNKS, CHUNK, A_KV_HEADS, A_HEAD_DIM)
        return jnp.concatenate([tp[:, j:j + nc] for j in range(WINDOW_CHUNKS + 1)], axis=2)

    kb, vb = band(k), band(v)
    logits = jnp.einsum('bcqgrd,bckgd->bcgrqk', qc, kb).astype(jnp.float32) * (A_HEAD_DIM ** -0.5)
    rel = jnp.arange(nk)[None, :] - pad - jnp.arange(CHUNK)[:, None]
    bias = rel_bias[t5_bucket(rel)][..., :A_HEADS].astype(jnp.float32)
    bias = jnp.transpose(bias, (2, 0, 1)).reshape(A_KV_HEADS, grp, CHUNK, nk)
    kpos = (jnp.arange(nc)[:, None] - WINDOW_CHUNKS) * CHUNK + jnp.arange(nk)[None, :]
    valid = (kpos >= 0)[:, None, None, None, :]
    logits = jnp.where(valid, logits + bias, -jnp.inf)
    sink = sinks.astype(jnp.float32).reshape(A_KV_HEADS, grp, 1, 1)
    m = jnp.maximum(jnp.max(logits, axis=-1, keepdims=True), sink)
    p = jnp.exp(logits - m)
    denom = jnp.sum(p, axis=-1, keepdims=True) + jnp.exp(sink - m)
    probs = (p / denom).astype(v.dtype)
    out = jnp.einsum('bcgrqk,bckgd->bcqgrd', probs, vb)
    return out.reshape(b, s, A_WIDTH)

def indexed_sparse_attention(q, k, v, iq, ik, iw, rel_bias):
    b, s = q.shape[0], q.shape[1]
    topk = min(TOPK_MAX, s // 4)
    nqb = s // Q_BLOCK
    kchunk = jnp.arange(s) // CHUNK
    gather = jax.vmap(lambda t, i: t[i])

    def to_blocks(t):
        return jnp.moveaxis(t.reshape((b, nqb, Q_BLOCK) + t.shape[2:]), 1, 0)

    qpos_blocks = jnp.arange(s, dtype=jnp.int32).reshape(nqb, Q_BLOCK)

    def block(args):
        qb, iqb, iwb, qpos = args
        qchunk = qpos // CHUNK
        sc = jax.nn.relu(jnp.einsum('bqhd,bsd->bqhs', iqb, ik).astype(jnp.float32) * (IDX_DIM ** -0.5))
        isc = jnp.einsum('bqh,bqhs->bqs', iwb.astype(jnp.float32) * (IDX_HEADS ** -0.5), sc)
        adm = kchunk[None, :] <= qchunk[:, None]
        isc = jnp.where(adm[None], isc, -jnp.inf)
        _, idx = lax.top_k(isc, topk)
        kg = gather(k, idx)
        vg = gather(v, idx)
        logits = jnp.einsum('bqhd,bqkhd->bqhk', qb, kg).astype(jnp.float32) * (B_HEAD_DIM ** -0.5)
        rel = idx - qpos[None, :, None]
        bias = rel_bias[t5_bucket(rel)][..., A_HEADS:A_HEADS + B_HEADS].astype(jnp.float32)
        logits = logits + jnp.moveaxis(bias, -1, 2)
        valid = (idx // CHUNK) <= qchunk[None, :, None]
        logits = jnp.where(valid[:, :, None, :], logits, -jnp.inf)
        probs = jax.nn.softmax(logits, axis=-1).astype(v.dtype)
        return jnp.einsum('bqhk,bqkhd->bqhd', probs, vg)

    out = lax.map(block, (to_blocks(q), to_blocks(iq), to_blocks(iw), qpos_blocks))
    return jnp.moveaxis(out, 0, 1).reshape(b, s, B_WIDTH)

def memory_cross_attention(q, mk, mv):
    b, s = q.shape[0], q.shape[1]
    logits = jnp.einsum('bshd,bmhd->bhsm', q, mk).astype(jnp.float32) * (C_HEAD_DIM ** -0.5)
    probs = jax.nn.softmax(logits, axis=-1).astype(mv.dtype)
    return jnp.einsum('bhsm,bmhd->bshd', probs, mv).reshape(b, s, C_WIDTH)

def setup_inputs(seed: int = 0) -> dict:
    key = jax.random.key(seed)
    ks = jax.random.split(key, 10)
    f32 = jnp.float32
    x = jax.random.normal(ks[0], (BATCH, SEQ, D_MODEL), f32)
    mem = jax.random.normal(ks[1], (BATCH, N_MEM, D_MODEL), f32)
    g_norm = 1.0 + 0.01 * jax.random.normal(ks[2], (DEPTH, D_MODEL), f32)
    w_in = jax.random.normal(ks[3], (DEPTH, D_MODEL, IN_WIDTH), f32) * D_MODEL ** -0.5
    sinks = jax.random.normal(ks[4], (DEPTH, A_HEADS), f32)
    rel_bias = 0.5 * jax.random.normal(ks[5], (N_BUCKETS, N_BIAS_HEADS), f32)
    g_mem = 1.0 + 0.01 * jax.random.normal(ks[6], (DEPTH, D_MODEL), f32)
    w_mem_kv = jax.random.normal(ks[7], (DEPTH, D_MODEL, 2 * C_WIDTH), f32) * D_MODEL ** -0.5
    w_out = jax.random.normal(ks[8], (DEPTH, MIX_WIDTH, D_MODEL), f32) * MIX_WIDTH ** -0.5
    g_final = 1.0 + 0.01 * jax.random.normal(ks[9], (D_MODEL,), f32)
    return {"x": x, "mem": mem, "g_norm": g_norm, "w_in": w_in, "sinks": sinks,
            "rel_bias": rel_bias, "g_mem": g_mem, "w_mem_kv": w_mem_kv,
            "w_out": w_out, "g_final": g_final}

def reference(x, mem, g_norm, w_in, sinks, rel_bias, g_mem, w_mem_kv, w_out, g_final):
    b, s, _ = x.shape
    split_points = [int(p) for p in np.cumsum(SPLIT_SIZES)[:-1]]
    h = x
    for layer in range(DEPTH):
        hn = rms_norm(h, g_norm[layer])
        proj = hn @ w_in[layer]
        (aq, ak, av, bq, bk, bv, iq, ik, iw, cq, gate) = jnp.split(proj, split_points, axis=-1)
        oa = sliding_window_sink_attention(
            aq.reshape(b, s, A_HEADS, A_HEAD_DIM),
            ak.reshape(b, s, A_KV_HEADS, A_HEAD_DIM),
            av.reshape(b, s, A_KV_HEADS, A_HEAD_DIM),
            sinks[layer], rel_bias)
        ob = indexed_sparse_attention(
            bq.reshape(b, s, B_HEADS, B_HEAD_DIM),
            bk.reshape(b, s, B_HEADS, B_HEAD_DIM),
            bv.reshape(b, s, B_HEADS, B_HEAD_DIM),
            iq.reshape(b, s, IDX_HEADS, IDX_DIM), ik, iw, rel_bias)
        mkv = rms_norm(mem, g_mem[layer]) @ w_mem_kv[layer]
        mk, mv = jnp.split(mkv, [C_WIDTH], axis=-1)
        n_mem = mem.shape[1]
        oc = memory_cross_attention(
            cq.reshape(b, s, C_HEADS, C_HEAD_DIM),
            mk.reshape(b, n_mem, C_HEADS, C_HEAD_DIM),
            mv.reshape(b, n_mem, C_HEADS, C_HEAD_DIM))
        y = jnp.concatenate([oa, ob, oc], axis=-1) * jax.nn.silu(gate)
        h = h + y @ w_out[layer]
    return rms_norm(h, g_final)


_drawn_inputs = setup_inputs


def setup_inputs(seed=0):
    import zlib

    import numpy as np

    out = dict(_drawn_inputs(seed))
    spreads = {}
    factors = {'g_norm': 8.0, 'sinks': 8.0, 'g_mem': 8.0, 'g_final': 5.571}
    for name, (base, spread) in spreads.items():
        noise = np.random.default_rng([zlib.crc32(name.encode()), seed]).standard_normal(out[name].shape)
        drawn = base * np.exp(spread * noise) if base else spread * noise
        out[name] = __import__('jax').numpy.asarray(drawn.astype(out[name].dtype))
    for name, factor in factors.items():
        out[name] = (out[name] * factor).astype(out[name].dtype)
    return out
```

```python
import math
from contextlib import ExitStack

import concourse.bass as bass
from concourse import mybir

F32 = mybir.dt.float32
F32R = mybir.dt.float32r
BF16 = mybir.dt.bfloat16
ALU = mybir.AluOpType
ACT = mybir.ActivationFunctionType
AX = mybir.AxisListType

P = 128
SEQ, D = 1024, 2048
KT = D // P
NB = SEQ // P
NMEM = 256
EPS = 1e-6
CHUNK = 64
TOPK = 256
ROUNDS = TOPK // 8
NBUCKET, MAXDIST = 32, 1024
AH, BH, CH = 16, 4, 4
A_SCALE = 64 ** -0.5
BC_SCALE = 128 ** -0.5
MASKED = -3.0e38
TAKEN = -3.3e38
BELOW_MASKED = -3.2e38

C_AQ, C_AK, C_AV = 0, 1024, 1152
C_BQ, C_BK, C_BV = 1280, 1792, 2304
C_IQ, C_IK = 2816, 3072
C_CQ, C_GATE = 3140, 3652
IKW = 68

MEM_TILES = 8
T_AK, T_AV, T_IQ, T_IK, T_Q0 = 8, 9, 10, 12, 13
T_LOOP = 14
T_B = T_LOOP + 24
T_BHEAD = T_B + 2
T_ALL = T_BHEAD + 13
N_OUT = 4 * T_ALL
B_POS = [0, 3, 6, 10, 14, 18, 22, 26]


def bucket_edges():
    half, exact = NBUCKET // 2, NBUCKET // 4

    def bucket(rel):
        n = abs(rel)
        if n < exact:
            b = n
        else:
            b = min(half - 1, exact + int(math.log(n / exact) / math.log(MAXDIST / exact) * (half - exact)))
        return b + (half if rel > 0 else 0)

    out, first = [], -(SEQ - 1)
    for rel in range(-(SEQ - 1) + 1, P + 1):
        if rel == P or bucket(rel) != bucket(first):
            out.append((first, rel, bucket(first)))
            first = rel
    return out


def mix_tile(m):
    return m + 12 if m < 4 else m - 4


class Semaphores:

    def __init__(self, sem):
        self.const_loaded = sem("const_loaded")
        self.rb_loaded = sem("rb_loaded")
        self.rb_scaled = sem("rb_scaled")
        self.v_built = sem("v_built")
        self.va_stored = sem("va_stored")
        self.vb_stored = sem("vb_stored")
        self.ta_built = sem("ta_built")
        self.tb_built = sem("tb_built")
        self.ta_fill = sem("ta_fill")
        self.ta_done = sem("ta_done")
        self.ident_zero = sem("ident_zero")
        self.ident_ready = sem("ident_ready")
        self.zeroed = sem("zeroed")
        self.mem_loaded0 = sem("mem_loaded0")
        self.mem_loaded1 = sem("mem_loaded1")
        self.g_loaded = sem("g_loaded")
        self.sq_done = sem("sq_done")
        self.ms_done = sem("ms_done")
        self.rt_done = sem("rt_done")
        self.rstd_done = sem("rstd_done")
        self.normed = sem("normed")
        self.turned = sem("turned")
        self.tr_hi = sem("tr_hi")
        self.tr_lo = sem("tr_lo")
        self.w_high = sem("w_high")
        self.w_low = sem("w_low")
        self.w_used = sem("w_used")
        self.pg_free = sem("pg_free")
        self.pq_free = sem("pq_free")
        self.stage_ready = sem("stage_ready")
        self.v_turned = sem("v_turned")
        self.kz_copied = sem("kz_copied")
        self.kz_moved = sem("kz_moved")
        self.kz1_copied = sem("kz1_copied")
        self.kz1_moved = sem("kz1_moved")
        self.ikz_copied = sem("ikz_copied")
        self.ikz_moved = sem("ikz_moved")
        self.iwT_ready = sem("iwT_ready")
        self.iw_turned = sem("iw_turned")
        self.iw_ready = sem("iw_ready")
        self.idx_ready = sem("idx_ready")
        self.relu_ready = sem("relu_ready")
        self.idx_added = sem("idx_added")
        self.isc_done = sem("isc_done")
        self.isc_st0 = sem("isc_st0")
        self.isc_st1 = sem("isc_st1")
        self.mask_done = sem("mask_done")
        self.mask_stored = sem("mask_stored")
        self.W_loaded = sem("W_loaded")
        self.top_max = sem("top_max")
        self.top_out = sem("top_out")
        self.gate_exp = sem("gate_exp")
        self.gate_step = sem("gate_step")
        self.sg_ready = sem("sg_ready")
        self.biasA_loaded = sem("biasA_loaded")
        self.sink_ready = sem("sink_ready")
        self.memkv_ready = sem("memkv_ready")
        self.logits_ready = sem("logits_ready")
        self.S_biased = sem("S_biased")
        self.S_max = sem("S_max")
        self.neg_ready = sem("neg_ready")
        self.probs_ready = sem("probs_ready")
        self.recip_ready = sem("recip_ready")
        self.norm_ready = sem("norm_ready")
        self.pt_ready = sem("pt_ready")
        self.pt_copied = sem("pt_copied")
        self.ot_ready = sem("ot_ready")
        self.ot_copied = sem("ot_copied")
        self.yf_ready = sem("yf_ready")
        self.y_high = sem("y_high")
        self.y_low = sem("y_low")
        self.y_free = sem("y_free")
        self.biasB_loaded = sem("biasB_loaded")
        self.mask_ld0 = sem("mask_ld0")
        self.mask_ld1 = sem("mask_ld1")
        self.bpt_ready = sem("bpt_ready")
        self.bpt_copied = sem("bpt_copied")
        self.out_done = sem("out_done")
        self.fin_sum = sem("fin_sum")
        self.out_free = sem("out_free")
        self.sq_out = sem("sq_out")
        self.h_added = sem("h_added")
        self.fin_ms = sem("fin_ms")
        self.fin_rt = sem("fin_rt")
        self.fin_rstd = sem("fin_rstd")
        self.fin_done = sem("fin_done")
        self.out_stored = sem("out_stored")
        self.gf_loaded = sem("gf_loaded")


def hybrid_layer(nc, x, mem, g_norm, w_in, sinks, rel_bias, g_mem, w_mem_kv, w_out, g_final, out):
    ctx = ExitStack()
    with ctx:
        def dram(name, shape, dt=F32):
            return nc.dram_tensor(name, shape, dt, kind="Internal").ap()

        VA_LEN, VB_LEN = 384, 1152
        va_dram = dram("va_dram", (AH, VA_LEN))
        vb_dram = dram("vb_dram", (BH, VB_LEN))
        ta_dram = dram("ta_dram", (AH, P, 256))
        tb_dram = dram("tb_dram", (BH, P, SEQ))
        isc_dram = dram("isc_dram", (6, P, SEQ))
        mask_dram = dram("mask_dram", (7, P, SEQ), BF16)
        yhi_dram = dram("yhi_dram", (16, P, SEQ), F32R)
        ylo_dram = dram("ylo_dram", (16, P, SEQ), F32R)

        base = (nc.sbuf_base + 127) // 128 * 128
        end = [base]

        def at(name, shape, dt, offset):
            return nc.alloc_sbuf_tensor_at(name, shape, dt, offset=offset)

        def take(nbytes):
            end[0] += nbytes
            return end[0] - nbytes

        KB = 1024
        R1 = take(128 * KB)
        hn_hi = at("hn_hi", [P, KT, SEQ], F32R, R1)
        hn_lo = at("hn_lo", [P, KT, SEQ], F32R, R1 + 64 * KB)
        mem_raw = at("mem_raw", [P, 2, D], F32, R1 + 96 * KB)
        gmem_b = at("gmem_b", [P, D], F32, R1 + 112 * KB)
        y_hi = at("y_hi", [P, KT, SEQ], F32R, R1)
        y_lo = at("y_lo", [P, KT, SEQ], F32R, R1 + 64 * KB)
        R2 = take(24 * KB)
        w_raw = at("w_raw", [P, 4, 512], F32, R2)
        w_hi = at("w_hi", [P, 4, 512], F32R, R2 + 8 * KB)
        w_lo = at("w_lo", [P, 4, 512], F32R, R2 + 16 * KB)
        R3 = take(32 * KB)
        memT_hi = at("memT_hi", [P, KT, NMEM], F32R, R3)
        memT_lo = at("memT_lo", [P, KT, NMEM], F32R, R3 + 16 * KB)
        SA = at("SA", [P, 3, 2, 257], F32, R3)
        SB = at("SB", [P, 2, SEQ], F32, R3)
        acc = at("acc", [P, 2, SEQ], F32, R3)
        av_stage = at("av_stage", [P, SEQ], F32, R3)
        PT = at("PT", [P, SEQ], F32, R3 + 8 * KB)
        relu_s = at("relu_s", [P, 2, SEQ], F32, R3 + 8 * KB)
        W = at("W", [P, SEQ], F32, R3 + 12 * KB)
        iwT = at("iwT", [P, SEQ], F32, R3 + 12 * KB)
        bv_stage = at("bv_stage", [P, SEQ], F32, R3 + 12 * KB)
        oT = at("oT", [P, SEQ], F32, R3 + 16 * KB)
        yf = at("yf", [P, SEQ], F32, R3 + 20 * KB)
        iq = at("iq", [P, 2, SEQ], F32, R3 + 16 * KB)
        yhi_s = at("yhi_s", [P, SEQ], F32R, R3 + 24 * KB)
        ylo_s = at("ylo_s", [P, SEQ], F32R, R3 + 28 * KB)
        ikz = at("ikz", [P, 2, SEQ], F32, R3 + 24 * KB)
        h_res = at("h_res", [P, 4, D], F32, R3)
        R4 = take(16 * KB)
        x_raw = at("x_raw", [P, 2, D], F32, R4)
        q0 = at("q0", [P, SEQ], F32, R4)
        kz = at("kz", [P, 2, SEQ], F32, R4 + 4 * KB)
        q1 = at("q1", [P, SEQ], F32, R4 + 4 * KB)
        bk1 = at("bk1", [P, SEQ], F32, R4 + 8 * KB)
        ak = at("ak", [P, SEQ], F32, R4 + 12 * KB)
        biasB = at("biasB", [P, SEQ], F32, R4 + 12 * KB)
        x_res = at("x_res", [P, 4, 512], F32, R4)
        R5 = take(16 * KB)
        VA = at("VA", [AH, VA_LEN], F32, R5)
        VB = at("VB", [BH, VB_LEN], F32, R5 + 2 * KB)
        mk = at("mk", [P, CH, NMEM], F32, R5)
        bk0 = at("bk0", [P, SEQ], F32, R5)
        mv = at("mv", [P, 2, CH, P], F32, R5 + 4 * KB)
        bv0 = at("bv0", [P, NB, P], F32, R5 + 4 * KB)
        gx_b = at("gx_b", [P, D], F32, R5 + 8 * KB)
        av = at("av", [P, NB, P], F32, R5 + 8 * KB)
        bv1 = at("bv1", [P, NB, P], F32, R5 + 8 * KB)
        sg = at("sg", [P, SEQ], F32, R5 + 12 * KB)
        gf_b = at("gf_b", [P, D], F32, R5)
        R6 = take(6 * KB)
        biasA = at("biasA", [P, 2, 256], F32, R6)
        maskB = at("maskB", [P, 2, SEQ], BF16, R6)
        mask_s = at("mask_s", [P, SEQ], BF16, R6 + 4 * KB)
        mv_stage = at("mv_stage", [P, NMEM], F32, R6)
        mk_now = at("mk_now", [P, NMEM], F32, R6)
        mv_now = at("mv_now", [P, 2, P], F32, R6 + KB)
        sq_junk = at("sq_junk", [P, D], BF16, R6)
        ident = at("ident", [P, P], F32, take(512))
        sinks8 = at("sinks8", [P, AH], F32, take(64))
        sink_now = at("sink_now", [P, 2], F32, take(32))
        mx = at("mx", [P, NB, 2], F32, take(64))
        neg = at("neg", [P, NB, 2], F32, take(64))
        den = at("den", [P, NB, 2], F32, take(64))
        rec = at("rec", [P, NB, 2], F32, take(64))
        iw = at("iw", [P, NB, 4], F32, take(128))
        top8 = at("top8", [P, 8], F32, take(32))
        ssq = at("ssq", [P, 16], F32, take(64))
        rms = at("rms", [P, 16], F32, take(64))
        rstd = at("rstd", [P, 16], F32, take(64))
        pace = at("pace", [P, 1], F32, take(32))
        ssum = at("ssum", [P, 4], F32, take(32))
        ms = at("ms", [P, 4], F32, take(32))
        masked = at("masked", [CHUNK, CHUNK], F32, take(256))
        rbA = at("rbA", [AH, NBUCKET], F32, R5 + 7 * KB)
        rbB = at("rbB", [BH, NBUCKET], F32, R5 + 7 * KB + 128)
        assert end[0] <= nc.sbuf_usable_end, (end[0], nc.sbuf_usable_end)

        def pb(name):
            return ctx.enter_context(nc.psum_tensor(name, [P, 2, 512], F32))

        PG, PQ, L, TO = pb("PG"), pb("PQ"), pb("L"), pb("TO")
        PROJ = (PG, PQ)
        T, O = TO[:, 0, :], TO[:, 1, :]
        bank = [t[:, i, :] for t in (PG, PQ, L, TO) for i in range(2)]

        def wide(t):
            return t[:, :, :].rearrange("p a b -> p (a b)")

        s = Semaphores(lambda n: ctx.enter_context(nc.semaphore(n)))
        w_loaded = [ctx.enter_context(nc.semaphore(f"w_loaded{i}")) for i in range(4)]
        x_loaded = [ctx.enter_context(nc.semaphore(f"x_loaded{i}")) for i in range(2)]
        xres_loaded = [ctx.enter_context(nc.semaphore(f"xres_loaded{i}")) for i in range(4)]
        y_loaded = [ctx.enter_context(nc.semaphore(f"y_loaded{i}")) for i in range(16)]
        proj_free = (s.pg_free, s.pq_free)

        w_in_v = w_in[0].rearrange("(c k p) n -> c p k n", k=4, p=P)
        w_mem_v = w_mem_kv[0].rearrange("(c k p) n -> c p k n", k=4, p=P)
        x_v = x[0].rearrange("(t p) d -> t p d", p=P)
        mem_v = mem[0].rearrange("(t p) d -> t p d", p=P)
        out_v = out[0].rearrange("(t p) d -> t p d", p=P)
        w_out_v = w_out[0].rearrange("(m p) n -> m p n", p=P)

        block = ctx.enter_context(nc.Block())

        @block.sync
        def _(sp):
            def chunk(n, c, src, k=4, width=P, first=False):
                if not first:
                    sp.wait_ge(s.w_low, n - 3)
                dst = w_raw[:, c, 0:512].rearrange("p (k n) -> p k n", k=k)[:, :, 0:width]
                sp.dma_start(dst, src).then_inc(w_loaded[c], 16)

            def tile(t, view, col, width=P, first=False):
                for c in range(4):
                    chunk(4 * t + c, c, view[c, :, :, bass.ds(col, width)], width=width, first=first)

            with nc.allow_non_contiguous_dma(reason="a few hundred elements"):
                sp.dma_start(rbA[:, :], rel_bias[:, 0:AH].rearrange("n h -> h n")).then_inc(s.rb_loaded, 16)
                sp.dma_start(rbB[:, :], rel_bias[:, AH:AH + BH].rearrange("n h -> h n")).then_inc(s.rb_loaded, 16)
            sp.dma_start(sinks8[:, :], sinks[0:1, :].to_broadcast([P, AH])).then_inc(s.const_loaded, 16)
            sp.dma_start(gmem_b[:, :], g_mem[0:1, :].to_broadcast([P, D])).then_inc(s.g_loaded, 16)
            sp.dma_start(mem_raw[:, 0, :], mem_v[0]).then_inc(s.mem_loaded0, 16)
            sp.dma_start(mem_raw[:, 1, :], mem_v[1]).then_inc(s.mem_loaded1, 16)
            sp.dma_start(gx_b[:, :], g_norm[0:1, :].to_broadcast([P, D])).then_inc(s.g_loaded, 16)
            for e in range(2):
                sp.dma_start(x_raw[:, e, :], x_v[e]).then_inc(x_loaded[e], 16)
            tile(0, w_mem_v, 0, first=True)
            sp.wait_ge(s.v_built, 1)
            sp.dma_start(va_dram, VA[:, :]).then_inc(s.va_stored, 16)
            sp.dma_start(vb_dram, VB[:, :]).then_inc(s.vb_stored, 16)
            sp.wait_ge(s.va_stored, 16)
            skew = bass.AP(va_dram.tensor, va_dram.offset + P - 1, [[VA_LEN, AH], [-1, P], [1, 256]])
            sp.dma_start(ta_dram, skew).then_inc(s.ta_built, 16)
            sp.wait_ge(s.vb_stored, 16)
            skew = bass.AP(vb_dram.tensor, vb_dram.offset + P - 1, [[VB_LEN, BH], [-1, P], [1, SEQ]])
            sp.dma_start(tb_dram, skew).then_inc(s.tb_built, 16)
            with sp.Fori(0, NB // 2 - 1) as i:
                for e in range(2):
                    sp.wait_ge(s.turned, 8 + 8 * i + 4 * e + 4)
                    sp.dma_start(x_raw[:, e, :], x_v[2 * i + 2 + e]).then_inc(x_loaded[e], 16)
            sp.wait_ge(s.ta_built, 16)
            sp.wait_ge(s.ta_fill, 1)
            neg_src = masked[:, :].rearrange("p (o k) -> p o k", o=1).to_broadcast([CHUNK, AH, CHUNK])
            ta_w = ta_dram.rearrange("h p k -> p h k")
            sp.dma_start(ta_w[0:CHUNK, :, 192:256], neg_src).then_inc(s.ta_done, 16)
            sp.dma_start(ta_w[CHUNK:P, :, 0:CHUNK], neg_src).then_inc(s.ta_done, 16)

            with sp.Fori(1, MEM_TILES) as t:
                tile(t, w_mem_v, t * P)
            tile(T_AK, w_in_v, C_AK)
            tile(T_AV, w_in_v, C_AV)
            tile(T_IQ, w_in_v, C_IQ)
            tile(T_IQ + 1, w_in_v, C_IQ + P)
            tile(T_IK, w_in_v, C_IK, width=IKW)
            tile(T_Q0, w_in_v, C_CQ)
            with sp.Fori(0, 3) as i:
                tile(T_LOOP + 2 * i, w_in_v, C_GATE + 12 * P + i * P)
                tile(T_LOOP + 1 + 2 * i, w_in_v, C_CQ + P + i * P)
            tile(T_LOOP + 6, w_in_v, C_GATE + 15 * P)
            tile(T_LOOP + 7, w_in_v, C_AQ)
            with sp.Fori(0, 7) as i:
                tile(T_LOOP + 8 + 2 * i, w_in_v, C_GATE + i * P)
                tile(T_LOOP + 9 + 2 * i, w_in_v, C_AQ + P + i * P)
            tile(T_LOOP + 22, w_in_v, C_GATE + 7 * P)
            tile(T_LOOP + 23, w_in_v, C_BQ)
            tile(T_B, w_in_v, C_BK)
            tile(T_B + 1, w_in_v, C_BV)
            with sp.Fori(0, 3) as h:
                tile(T_BHEAD + 4 * h, w_in_v, C_GATE + 8 * P + h * P)
                tile(T_BHEAD + 4 * h + 1, w_in_v, C_BQ + P + h * P)
                tile(T_BHEAD + 4 * h + 2, w_in_v, C_BK + P + h * P)
                tile(T_BHEAD + 4 * h + 3, w_in_v, C_BV + P + h * P)
            tile(T_BHEAD + 12, w_in_v, C_GATE + 11 * P)

            def load_y(half, m):
                cols = slice(512 * half, 512 * half + 512)
                sp.dma_start(y_hi[:, m, cols].bitcast(F32), yhi_dram[m, :, cols].bitcast(F32)).then_inc(y_loaded[m], 16)
                sp.dma_start(y_lo[:, m, cols].bitcast(F32), ylo_dram[m, :, cols].bitcast(F32)).then_inc(y_loaded[m], 16)

            sp.wait_ge(s.w_used, 4 * T_ALL)
            sp.wait_ge(s.y_free, 32 * 16)
            for m in range(8):
                load_y(0, m)
            for c in range(4):
                chunk(N_OUT + c, c, w_out_v[mix_tile(c), :, 0:512], k=1, width=512)
            for m in range(8, 15):
                load_y(0, m)
            sp.wait_ge(s.y_free, 32 * 17)
            load_y(0, 15)

            def out_loads(q, col, half, first):
                for m in range(4 if first else 0, 16):
                    if m == 8:
                        for j in range(4):
                            if not first:
                                sp.wait_ge(s.out_free, 8 + 4 * (q - 1) + j + 1)
                            sp.dma_start(x_res[:, j, :], x_v[4 * half + j, :, bass.ds(col, 512)])\
                              .then_inc(xres_loaded[j], 16)
                    chunk(N_OUT + 16 * q + m, m % 4, w_out_v[mix_tile(m), :, bass.ds(col, 512)], k=1, width=512)

            out_loads(0, 0, 0, True)
            for m in range(16):
                load_y(1, m)
            sp.dma_start(gf_b[:, :], bass.AP(g_final.tensor, g_final.offset, [[0, P], [1, D]]))\
              .then_inc(s.gf_loaded, 16)
            with sp.Fori(0, 3) as n:
                out_loads(1 + n, n * 512 + 512, 0, False)
            with sp.Fori(1, 5) as n:
                out_loads(3 + n, n * 512 - 512, 1, False)

        @block.gpsimd
        def _(pool):
            pool.memset(ident[:, :], 0.0).then_inc(s.ident_zero, 1)
            pool.wait_ge(s.ident_zero, 1)
            pool.affine_select(out=ident[:, :], in_=ident[:, :], compare_op=ALU.not_equal, fill=1.0, base=0,
                               pattern=[[-1, P]], channel_multiplier=1).then_inc(s.ident_ready, 1)

            def low(n, c):
                pool.wait_ge(s.w_high, n + 1)
                pool.tensor_tensor(w_lo[:, c, :], w_raw[:, c, :], w_hi[:, c, :].bitcast(F32), ALU.subtract)\
                    .then_inc(s.w_low, 1)

            for n in range(3):
                low(n, n % 4)
            with pool.Fori(0, T_LOOP) as t:
                for c in range(4):
                    low(4 * t + c + 3, (c + 3) % 4)

            def normalise(g, b, kind):
                pool.wait_ge(s.recip_ready, g + 1)
                if kind == "A":
                    k0 = P if b == 0 else 0
                    for e in range(2):
                        v = SA[:, b % 3, e, k0:256]
                        last = pool.tensor_tensor(v, v, rec[:, b, e:e + 1].to_broadcast([P, 256 - k0]), ALU.mult)
                else:
                    w = NMEM if kind == "C" else P * (b + 1)
                    v = SA[:, b % 3, 0, 0:w] if kind == "C" else SB[:, b % 2, 0:w]
                    last = pool.tensor_tensor(v, v, rec[:, b, 0:1].to_broadcast([P, w]), ALU.mult)
                last.then_inc(s.norm_ready, 1)

            def gated(m, pg_count):
                pool.wait_ge(s.ot_copied, 8 * m + 8)
                pool.wait_ge(s.pg_free, pg_count)
                pool.tensor_tensor(yf[:, :], oT[:, :], sg[:, :], ALU.mult).then_inc(s.yf_ready, 1)

            def y_low(m):
                pool.wait_ge(s.y_high, m + 1)
                pool.tensor_tensor(ylo_s[:, :], yf[:, :], yhi_s[:, :].bitcast(F32), ALU.subtract)\
                    .then_inc(s.y_low, 1)

            def mix(m, kind):
                for slot in range(16):
                    if slot % 2 == 0:
                        low(4 * T_LOOP + 8 * m + slot // 2 + 3, (slot // 2 + 3) % 4)
                    if 1 <= slot <= 8:
                        normalise(8 * m + slot - 1, slot - 1, kind)
                    if slot == 13:
                        gated(m, m + 8)
                    if slot == 15:
                        y_low(m)

            with pool.Fori(0, 4) as m:
                mix(m, "C")
            with pool.Fori(4, 12) as m:
                mix(m, "A")
            for n in range(4 * T_B, 4 * T_BHEAD):
                low(n + 3, (n + 3) % 4)

            def head(h, slots):
                m = 12 + h
                for slot in range(32):
                    if slot % 2 == 0 and (slots == 32 or slot // 2 + 3 < 4):
                        low(4 * T_BHEAD + 16 * h + slot // 2 + 3, (slot // 2 + 3) % 4)
                    if slot - 1 in B_POS:
                        b = B_POS.index(slot - 1)
                        normalise(8 * m + b, b, "B")
                gated(m, 21 + 2 * h)
                y_low(m)

            with pool.Fori(0, 3) as h:
                head(h, 32)
            head(3, 8)
            with pool.Fori(N_OUT // 4, N_OUT // 4 + 32) as t:
                for c in range(4):
                    low(4 * t + c, c)

        isc_stored = (s.isc_st0, s.isc_st1)
        isc_width = [512, 512, 768, 768, 1024, 1024]

        def store_scores(act, b):
            act.wait_ge(s.isc_done, b - 1)
            w = isc_width[b - 2]
            act.dma_start(isc_dram[b - 2, :, 0:w], acc[:, b % 2, 0:w]).then_inc(isc_stored[b % 2], 16)

        @block.scalar
        def _(act):
            def norm_root(j, e, raw):
                act.activation(sq_junk[:, :], raw, ACT.Square, accum_out=ssq[:, e:e + 1]).then_inc(s.sq_done, 1)
                act.wait_ge(s.ms_done, j + 1)
                act.activation(rms[:, e:e + 1], ms[:, e:e + 1], ACT.Sqrt).then_inc(s.rt_done, 1)

            def norm_high(j, e, dst, col):
                for kg in range(4):
                    act.wait_ge(s.turned, 4 * j + kg + 1)
                    act.activation(dst[:, 4 * kg:4 * kg + 4, bass.ds(col, P)],
                                   bank[4 * e + kg].rearrange("p (k t) -> p k t", k=4), ACT.Copy).then_inc(s.tr_hi, 1)

            act.wait_ge(s.mem_loaded0, 16)
            norm_root(0, 0, mem_raw[:, 0, :])
            act.wait_ge(s.mem_loaded1, 16)
            norm_root(1, 1, mem_raw[:, 1, :])
            norm_high(0, 0, memT_hi, 0)
            act.wait_ge(x_loaded[0], 16)
            norm_root(2, 0, x_raw[:, 0, :])
            norm_high(1, 1, memT_hi, P)
            with act.Fori(0, 3) as i:
                act.wait_ge(x_loaded[1], 16 * i + 16)
                norm_root(2 * i + 3, 1, x_raw[:, 1, :])
                norm_high(2 * i + 2, 0, hn_hi, 2 * P * i)
                act.wait_ge(x_loaded[0], 16 * i + 32)
                norm_root(2 * i + 4, 0, x_raw[:, 0, :])
                norm_high(2 * i + 3, 1, hn_hi, 2 * P * i + P)
            act.wait_ge(x_loaded[1], 64)
            norm_root(9, 1, x_raw[:, 1, :])
            norm_high(8, 0, hn_hi, 6 * P)
            norm_high(9, 1, hn_hi, 7 * P)

            def high(t, c, first=False):
                act.wait_ge(w_loaded[c], 16 * t + 16)
                if not first:
                    act.wait_ge(s.w_used, 4 * t + c - 3)
                act.activation(w_hi[:, c, :], w_raw[:, c, :], ACT.Copy).then_inc(s.w_high, 1)

            def highs_ahead(t, c):
                if c == 0:
                    high(t, 3)
                else:
                    high(t + 1, c - 1)

            for c in range(3):
                high(0, c, first=True)

            def tile_highs(t):
                for c in range(4):
                    if isinstance(t, int) and t == 0 and c == 0:
                        high(0, 3, first=True)
                    else:
                        highs_ahead(t, c)

            for t in range(CH):
                tile_highs(t)
                if t == 0:
                    act.wait_ge(s.va_stored, 16)
                    act.wait_ge(s.vb_stored, 16)
                act.wait_ge(s.w_used, 4 * t + 4)
                act.activation(mk[:, t, :], PROJ[t % 2][:, 0, 0:NMEM], ACT.Copy).then_inc(proj_free[t % 2], 1)
            with act.Fori(0, 2) as i:
                for e in range(2):
                    tile_highs(4 + 2 * i + e)
                    act.wait_ge(s.w_used, 4 * (5 + 2 * i + e))
                    act.activation(mv_stage[:, :], PROJ[e][:, 0, 0:NMEM], ACT.Copy).then_inc(s.stage_ready, 1)
                    act.wait_ge(s.v_turned, 2 * i + e + 1)
                    act.activation(mv[:, :, bass.ds(2 * i + e, 1), :].rearrange("p k o d -> p k (o d)"),
                                   PROJ[e][:, 0, 0:NMEM].rearrange("p (k d) -> p k d", k=2), ACT.Copy)\
                       .then_inc(proj_free[e], 1)

            def values(t, stage, dst, count):
                p = PROJ[t % 2]
                act.wait_ge(s.w_used, 4 * t + 4)
                act.activation(stage[:, :], wide(p), ACT.Copy).then_inc(s.stage_ready, 1)
                act.wait_ge(s.v_turned, count)
                act.activation(dst[:, :, :].rearrange("p k d -> p (k d)"), wide(p), ACT.Copy)\
                   .then_inc(proj_free[t % 2], 1)

            tile_highs(T_AK)
            act.wait_ge(s.w_used, 4 * T_AK + 4)
            act.activation(kz[0:CHUNK, 0, :], wide(PG)[0:CHUNK, :], ACT.Copy)
            act.activation(ak[:, :], wide(PG), ACT.Copy).then_inc(s.pg_free, 1)
            act.wait_ge(s.pg_free, T_AK // 2 + 1)
            act.dma_start(kz[CHUNK:P, 1, :], ak[0:CHUNK, :]).then_inc(s.kz_moved, 16)
            tile_highs(T_AV)
            values(T_AV, av_stage, av, 5)
            for e in range(2):
                t = T_IQ + e
                tile_highs(t)
                act.wait_ge(s.w_used, 4 * t + 4)
                act.activation(iq[:, e, :], wide(PROJ[e]), ACT.Copy).then_inc(proj_free[e], 1)
            tile_highs(T_IK)
            act.wait_ge(s.w_used, 4 * T_IK + 4)
            act.activation(ikz[0:CHUNK, 0, :], wide(PG)[0:CHUNK, :], ACT.Copy).then_inc(s.ikz_copied, 1)
            act.activation(iwT[CHUNK:IKW, :], wide(PG)[CHUNK:IKW, :], ACT.Copy).then_inc(s.pg_free, 1)
            act.wait_ge(s.ikz_copied, 1)
            act.dma_start(ikz[CHUNK:P, 1, :], ikz[0:CHUNK, 0, :]).then_inc(s.ikz_moved, 16)

            act.wait_ge(s.iw_turned, 1)
            for slot in range(8):
                for u in range(3 * slot, 3 * slot + 3):
                    b = 2 + u // 4
                    act.wait_ge(s.idx_ready, u + 1)
                    if u >= 2:
                        act.wait_ge(s.idx_added, u - 1)
                    src = wide(L if u % 2 == 0 else TO)
                    act.activation(relu_s[:, u % 2, 0:P * (b + 1)], src[:, 0:P * (b + 1)], ACT.Relu, scale=0.125)\
                       .then_inc(s.relu_ready, 1)
                    if u % 4 == 1 and b > 2:
                        store_scores(act, b - 1)
                if slot % 2 == 0:
                    highs_ahead(T_Q0, slot // 2)
            store_scores(act, 7)
            act.wait_ge(s.w_used, 4 * T_Q0 + 4)
            act.activation(q0[:, :], wide(PQ), ACT.Copy).then_inc(s.pq_free, 1)
            act.wait_ge(s.isc_st0, 48)
            act.wait_ge(s.isc_st1, 48)

            def gate_exp(m, t):
                act.wait_ge(s.w_used, 4 * t + 4)
                act.activation(sg[:, :], wide(PG), ACT.Exp, scale=-1.0).then_inc(s.gate_exp, 1)

            def probs(g, b, kind):
                act.wait_ge(s.neg_ready, g + 1)
                if kind == "A":
                    k0 = P if b == 0 else 0
                    for e in range(2):
                        v = SA[:, b % 3, e, k0:257]
                        last = act.activation(v, v, ACT.Exp, scale=A_SCALE, bias=neg[:, b, e:e + 1],
                                              accum_out=den[:, b, e:e + 1])
                elif kind == "C":
                    last = act.activation(SA[:, b % 3, 0, 0:NMEM], L[:, b % 2, 0:NMEM], ACT.Exp, scale=BC_SCALE,
                                          bias=neg[:, b, 0:1], accum_out=den[:, b, 0:1])
                else:
                    v = SB[:, b % 2, 0:P * (b + 1)]
                    last = act.activation(v, v, ACT.Exp, scale=BC_SCALE, bias=neg[:, b, 0:1],
                                          accum_out=den[:, b, 0:1])
                last.then_inc(s.probs_ready, 1)

            def turned_probs(g, b, kind):
                act.wait_ge(s.pt_ready, g + 1)
                a, z = (0, 256) if kind == "C" else (256 if b == 0 else 0, 512)
                act.activation(PT[:, a:z], T[:, a:z], ACT.Copy).then_inc(s.pt_copied, 1)

            def head_out(g, b):
                act.wait_ge(s.ot_ready, g + 1)
                act.activation(oT[:, P * b:P * b + P], O[:, 0:P], ACT.Copy).then_inc(s.ot_copied, 1)

            def y_high(m):
                act.wait_ge(s.yf_ready, m + 1)
                act.wait_ge(s.y_free, 32 * m + 32)
                act.activation(yhi_s[:, :], yf[:, :], ACT.Copy).then_inc(s.y_high, 1)

            def y_row(dst, m):
                return dst[bass.ds(m, 1), :, :].rearrange("o p t -> (o p) t").bitcast(F32)

            def y_store(m):
                act.wait_ge(s.y_low, m + 1)
                act.dma_start(y_row(yhi_dram, m), yhi_s[:, :].bitcast(F32)).then_inc(s.y_free, 16)
                act.dma_start(y_row(ylo_dram, m), ylo_s[:, :].bitcast(F32)).then_inc(s.y_free, 16)

            def mix(m, kind, pair=None, width=0):
                for slot in range(17):
                    if slot == 0 and pair is not None:
                        act.wait_ge(s.mask_done, pair + 1)
                        act.dma_start(mask_dram[pair, :, 0:width], mask_s[:, 0:width]).then_inc(s.mask_stored, 16)
                        act.dma_start(W[:, 0:width], isc_dram[pair, :, 0:width]).then_inc(s.W_loaded, 16)
                    if slot == 0 and kind == "A":
                        act.wait_ge(s.ta_done, 32)
                        act.wait_ge(s.S_max, 8 * m)
                        act.dma_start(biasA[:, :, :], ta_dram[bass.ds(2 * (m - 4), 2), :, :]
                                      .rearrange("h p k -> p h k")).then_inc(s.biasA_loaded, 16)
                    if slot == 0 and kind == "C":
                        act.activation(mk_now[:, :], mk[:, bass.ds(m, 1), :].rearrange("p o n -> p (o n)"), ACT.Copy)
                        act.activation(mv_now[:, :, :], mv[:, :, bass.ds(m, 1), :].rearrange("p k o d -> p k (o d)"),
                                       ACT.Copy).then_inc(s.memkv_ready, 1)
                    if 4 <= slot <= 11:
                        turned_probs(8 * m + slot - 4, slot - 4, kind)
                    if 5 <= slot <= 12:
                        head_out(8 * m + slot - 5, slot - 5)
                    if 1 <= slot <= 8:
                        probs(8 * m + slot - 1, slot - 1, kind)
                    if slot % 2 == 0 and slot < 16:
                        c = slot // 2
                        highs_ahead(T_LOOP + 2 * m + c // 4, c % 4)
                    if slot == 8:
                        gate_exp(m, T_LOOP + 2 * m)
                    if slot == 14:
                        y_high(m)
                act.wait_ge(s.w_used, 4 * (T_LOOP + 2 * m + 2))
                act.activation(q0[:, :], wide(PQ), ACT.Copy).then_inc(s.pq_free, 1)
                y_store(m)

            for kind, lo, width in (("C", 0, 512), ("A", 2, 768), ("A", 4, 1024)):
                if lo == 4:
                    act.activation(kz[CHUNK:P, 1, :], ak[CHUNK:P, :], ACT.Copy).then_inc(s.kz1_copied, 1)
                    act.dma_start(kz[0:CHUNK, 0, :], ak[CHUNK:P, :]).then_inc(s.kz_moved, 16)
                if lo == 0:
                    act.wait_ge(s.kz_moved, 16)
                with act.Fori(lo, lo + 2) as pair:
                    mix(2 * pair, kind, pair, width)
                    mix(2 * pair + 1, kind)

            act.wait_ge(s.mask_done, 7)
            act.dma_start(mask_dram[6, :, :], mask_s[:, :]).then_inc(s.mask_stored, 16)
            tile_highs(T_B)
            act.wait_ge(s.w_used, 4 * T_B + 4)
            act.activation(bk0[:, :], wide(PG), ACT.Copy).then_inc(s.pg_free, 1)
            tile_highs(T_B + 1)
            values(T_B + 1, bv_stage, bv0, 6)
            act.wait_ge(s.mask_stored, 16 * 7)
            for h in range(BH):
                m = 12 + h

                def load_mask(b):
                    src = mask_dram[max(0, b - 1), :, P:3 * P] if b == 1 else mask_dram[max(0, b - 1), :, 0:P * (b + 1)]
                    act.dma_start(maskB[:, b % 2, 0:P * (b + 1)], src).then_inc((s.mask_ld0, s.mask_ld1)[b % 2], 16)

                act.wait_ge(s.S_max, 8 * m)
                if h == 0:
                    act.wait_ge(s.tb_built, 16)
                act.dma_start(biasB[:, :], tb_dram[h]).then_inc(s.biasB_loaded, 16)
                load_mask(0)
                load_mask(1)
                for slot in range(33):
                    for b in range(NB):
                        two = b >= 4
                        if slot == B_POS[b] + 4:
                            act.wait_ge(s.bpt_ready, 12 * h + (2 * b - 4 if two else b) + 1)
                            n = P * min(4, b + 1)
                            act.activation(PT[:, 0:n], T[:, 0:n], ACT.Copy).then_inc(s.bpt_copied, 1)
                        if slot == B_POS[b] + 5 and two:
                            act.wait_ge(s.bpt_ready, 12 * h + 2 * b - 4 + 2)
                            n = P * (b - 3)
                            act.activation(PT[:, 512:512 + n], T[:, 0:n], ACT.Copy).then_inc(s.bpt_copied, 1)
                        if slot == B_POS[b] + 6:
                            head_out(8 * m + b, b)
                        if slot == B_POS[b] + 1:
                            probs(8 * m + b, b, "B")
                            if b + 2 < NB:
                                load_mask(b + 2)
                    if slot % 2 == 0 and slot < 32 and (h < 3 or slot < 2):
                        c = slot // 2
                        highs_ahead(T_BHEAD + 4 * h + c // 4, c % 4)
                    if slot == 8:
                        gate_exp(m, T_BHEAD + 4 * h)
                    if slot == 16 and h < 3:
                        act.wait_ge(s.w_used, 4 * (T_BHEAD + 4 * h + 2))
                        act.activation((q0, q1)[(h + 1) % 2][:, :], wide(PQ), ACT.Copy).then_inc(s.pq_free, 1)
                    if slot == 24 and h < 3:
                        act.wait_ge(s.w_used, 4 * (T_BHEAD + 4 * h + 3))
                        act.activation((bk0, bk1)[(h + 1) % 2][:, :], wide(PG), ACT.Copy).then_inc(s.pg_free, 1)
                if h < 3:
                    values(T_BHEAD + 4 * h + 3, bv_stage, (bv0, bv1)[(h + 1) % 2], 7 + h)
                y_high(m)
                y_store(m)

            for c in range(3):
                high(T_ALL, c)

            def roots(half):
                act.wait_ge(s.fin_ms, half + 1)
                act.activation(rms[:, 0:4], ms[:, 0:4], ACT.Sqrt).then_inc(s.fin_rt, 1)

            def store_out(half):
                for j in range(4):
                    act.wait_ge(s.fin_done, 4 * half + j + 1)
                    act.dma_start(out_v[4 * half + j], h_res[:, j, :]).then_inc(s.out_stored, 16)

            def out_n(q, n, **more):
                for k in range(3, 16 if more.get("last") else 19):
                    high(T_ALL + 4 * q + k // 4, k % 4)
                    if k == 9 and more.get("between"):
                        store_out(0)
                for j in range(4):
                    act.wait_ge(s.out_free, 8 + 4 * q + j + 1)
                    act.activation(sq_junk[:, 512 * j:512 * j + 512], h_res[:, j, bass.ds(n * 512, 512)], ACT.Square,
                                   accum_out=ssq[:, bass.ds(4 * j + n, 1)]).then_inc(s.sq_out, 1)

            with act.Fori(0, 4) as n:
                out_n(n, n)
            roots(0)
            out_n(4, 0, between=True)
            with act.Fori(1, 3) as n:
                out_n(4 + n, n)
            out_n(7, 3, last=True)
            roots(1)
            store_out(1)
            act.wait_ge(s.out_stored, 16 * NB)

        @block.vector
        def _(dve):
            def carry():
                dve.memset(pace[:, :], 0.0)

            dve.memset(masked[:, :], MASKED).then_inc(s.ta_fill, 1)
            dve.wait_ge(s.rb_loaded, 32)
            dve.tensor_scalar(rbA[:, :], rbA[:, :], 1 / A_SCALE, None, ALU.mult)
            dve.tensor_scalar(rbB[:, :], rbB[:, :], 1 / BC_SCALE, None, ALU.mult).then_inc(s.rb_scaled, 1)
            dve.wait_ge(s.rb_scaled, 1)
            dve.memset(VA[:, VA_LEN - 1:VA_LEN], 0.0)
            dve.memset(VB[:, VB_LEN - 1:VB_LEN], 0.0)
            for first, last, r in bucket_edges():
                for V, rb, heads, zero in ((VA, rbA, AH, 255), (VB, rbB, BH, SEQ - 1)):
                    a, z = max(first + zero, 0), last + zero
                    if z > a:
                        ins = dve.tensor_copy(V[:, a:z], rb[:, r:r + 1].to_broadcast([heads, z - a]))
            ins.then_inc(s.v_built, 1)
            dve.memset(mask_s[CHUNK:P, :], 0.0)
            dve.memset(mask_s[0:CHUNK, 0:64], 0.0)
            dve.memset(mask_s[0:CHUNK, 64:128], MASKED)
            dve.memset(mask_s[0:CHUNK, 128:320], 0.0)
            dve.memset(mask_s[0:CHUNK, 320:384], MASKED)
            dve.memset(mask_s[0:CHUNK, 384:SEQ], 0.0).then_inc(s.mask_done, 1)

            def normed(j, e, raw, g):
                dve.wait_ge(s.sq_done, j + 1)
                dve.tensor_scalar(ms[:, e:e + 1], ssq[:, e:e + 1], 1.0 / D, EPS, ALU.mult, ALU.add)\
                   .then_inc(s.ms_done, 1)
                dve.wait_ge(s.rt_done, j + 1)
                dve.reciprocal(rstd[:, e:e + 1], rms[:, e:e + 1]).then_inc(s.rstd_done, 1)
                dve.wait_ge(s.rstd_done, j + 1)
                dve.scalar_tensor_tensor(out=raw, in0=raw, scalar=rstd[:, e:e + 1], in1=g, op0=ALU.mult,
                                         op1=ALU.mult).then_inc(s.normed, 1)

            def norm_low(j, e, hi, lo, col):
                for kg in range(4):
                    dve.wait_ge(s.tr_hi, 4 * j + kg + 1)
                    dve.tensor_tensor(lo[:, 4 * kg:4 * kg + 4, bass.ds(col, P)],
                                      bank[4 * e + kg].rearrange("p (k t) -> p k t", k=4),
                                      hi[:, 4 * kg:4 * kg + 4, bass.ds(col, P)].bitcast(F32), ALU.subtract)\
                       .then_inc(s.tr_lo, 1)

            dve.wait_ge(s.g_loaded, 32)
            normed(0, 0, mem_raw[:, 0, :], gmem_b[:, :])
            normed(1, 1, mem_raw[:, 1, :], gmem_b[:, :])
            norm_low(0, 0, memT_hi, memT_lo, 0)
            normed(2, 0, x_raw[:, 0, :], gx_b[:, :])
            norm_low(1, 1, memT_hi, memT_lo, P)
            with dve.Fori(0, 3) as i:
                normed(2 * i + 3, 1, x_raw[:, 1, :], gx_b[:, :])
                norm_low(2 * i + 2, 0, hn_hi, hn_lo, 2 * P * i)
                normed(2 * i + 4, 0, x_raw[:, 0, :], gx_b[:, :])
                norm_low(2 * i + 3, 1, hn_hi, hn_lo, 2 * P * i + P)
            normed(9, 1, x_raw[:, 1, :], gx_b[:, :])
            norm_low(8, 0, hn_hi, hn_lo, 6 * P)
            norm_low(9, 1, hn_hi, hn_lo, 7 * P)

            dve.wait_ge(s.const_loaded, 16)
            dve.tensor_scalar(sinks8[:, :], sinks8[:, :], 1 / A_SCALE, None, ALU.mult).then_inc(s.sink_ready, 1)

            dve.wait_ge(s.turned, 40)
            dve.memset(kz[CHUNK:P, 0, :], 0.0)
            dve.memset(kz[0:CHUNK, 1, :], 0.0).then_inc(s.zeroed, 1)
            dve.wait_ge(s.w_used, 4 * MEM_TILES)
            dve.memset(ikz[CHUNK:P, 0, :], 0.0)
            dve.memset(ikz[0:CHUNK, 1, :], 0.0).then_inc(s.zeroed, 1)

            dve.wait_ge(s.iw_turned, 1)
            dve.tensor_scalar(iw[:, :, :].rearrange("p b h -> p (b h)"), T[:, 0:4 * NB], 0.5, None, ALU.mult)\
               .then_inc(s.iw_ready, 1)
            dve.wait_ge(s.iw_ready, 1)
            for u in range(24):
                b, h = 2 + u // 4, u % 4
                w = P * (b + 1)
                dve.wait_ge(s.relu_ready, u + 1)
                if h == 0:
                    if b >= 4:
                        dve.wait_ge(isc_stored[b % 2], 16 * ((b - 2) // 2))
                    dve.tensor_scalar(acc[:, b % 2, 0:w], relu_s[:, u % 2, 0:w], iw[:, b, 0:1], 0.0,
                                      ALU.mult, ALU.add).then_inc(s.idx_added, 1)
                else:
                    dve.wait_ge(s.idx_added, u)
                    dve.scalar_tensor_tensor(out=acc[:, b % 2, 0:w], in0=relu_s[:, u % 2, 0:w],
                                             scalar=iw[:, b, h:h + 1], in1=acc[:, b % 2, 0:w],
                                             op0=ALU.mult, op1=ALU.add).then_inc(s.idx_added, 1)
                if h == 3:
                    dve.wait_ge(s.idx_added, u + 1)
                    if isc_width[b - 2] > w:
                        dve.memset(acc[:, b % 2, w:isc_width[b - 2]], MASKED)
                    if b == NB - 1:
                        dve.memset(acc[0:CHUNK, b % 2, w - CHUNK:w - 32], MASKED).then_inc(s.y_free, 32)
                        dve.memset(acc[0:CHUNK, b % 2, w - 32:w], MASKED).then_inc(s.isc_done, 1)
                    else:
                        dve.memset(acc[0:CHUNK, b % 2, w - CHUNK:w], MASKED).then_inc(s.isc_done, 1)

            def choose(m, slot, width, pair, second):
                if slot == 0 and not second:
                    dve.wait_ge(s.W_loaded, 16 * pair + 16)
                else:
                    dve.wait_ge(s.top_out, 16 * m + slot)
                carry()
                dve.max(top8[:, :], W[:, 0:width]).then_inc(s.top_max, 1)
                dve.wait_ge(s.top_max, 16 * m + slot + 1)
                carry()
                dve.match_replace(W[:, 0:width], top8[:, :], W[:, 0:width], TAKEN).then_inc(s.top_out, 1)
                if slot == 15 and second:
                    dve.wait_ge(s.top_out, 16 * m + 16)
                    dve.wait_ge(s.mask_stored, 16 * pair + 16)
                    dve.tensor_scalar(mask_s[:, 0:width], W[:, 0:width], BELOW_MASKED, MASKED, ALU.is_gt, ALU.mult)\
                       .then_inc(s.mask_done, 1)

            def negated(g, b, n, scale):
                dve.wait_ge(s.S_max, g + 1)
                dve.tensor_scalar(neg[:, b, 0:n], mx[:, b, 0:n], -scale, None, ALU.mult).then_inc(s.neg_ready, 1)

            def maxima(m, b, kind):
                g = 8 * m + b
                dve.wait_ge(s.logits_ready, g + 1)
                if kind == "C":
                    dve.tensor_reduce(mx[:, b, 0:1], L[:, b % 2, 0:NMEM], AX.X, ALU.max).then_inc(s.S_max, 1)
                    negated(g, b, 1, BC_SCALE)
                else:
                    k0 = P if b == 0 else 0
                    if b == 0:
                        dve.wait_ge(s.biasA_loaded, 16 * (m - 3))
                    dve.tensor_copy(SA[:, b % 3, :, 256:257].rearrange("p e o -> p (e o)"), sink_now[:, :])
                    for e in range(2):
                        last = dve.tensor_tensor_reduce(SA[:, b % 3, e, k0:256], L[:, b % 2, 256 * e + k0:256 * e + 256],
                                                        biasA[:, e, k0:256], 1.0, sink_now[:, e:e + 1], ALU.add,
                                                        ALU.max, mx[:, b, e:e + 1])
                    last.then_inc(s.S_max, 1)
                    negated(g, b, 2, A_SCALE)

            def reciprocals(g, b, n):
                dve.wait_ge(s.probs_ready, g + 1)
                dve.reciprocal(rec[:, b, 0:n], den[:, b, 0:n]).then_inc(s.recip_ready, 1)

            def silu(m):
                dve.wait_ge(s.gate_exp, m + 1)
                dve.tensor_scalar(sg[:, :], sg[:, :], 1.0, None, ALU.add).then_inc(s.gate_step, 1)
                dve.wait_ge(s.gate_step, 2 * m + 1)
                dve.reciprocal(sg[:, :], sg[:, :]).then_inc(s.gate_step, 1)
                dve.wait_ge(s.gate_step, 2 * m + 2)
                dve.tensor_tensor(sg[:, :], wide(PG), sg[:, :], ALU.mult).then_inc(s.pg_free, 1)

            def mix(m, kind, pair, second, width):
                if kind == "A":
                    dve.wait_ge(s.S_max, 8 * m)
                    dve.tensor_copy(sink_now[:, :], sinks8[:, bass.ds(2 * (m - 4), 2)]).then_inc(s.sink_ready, 1)
                    dve.wait_ge(s.sink_ready, m - 2)
                for slot in range(16):
                    if slot < 8:
                        maxima(m, slot, kind)
                    choose(m, slot, width, pair, second)
                    if 1 <= slot <= 8:
                        reciprocals(8 * m + slot - 1, slot - 1, 2 if kind == "A" else 1)
                    if slot == 9:
                        silu(m)

            for kind, lo, width in (("C", 0, 512), ("A", 2, 768), ("A", 4, 1024)):
                if lo == 2:
                    dve.wait_ge(s.sink_ready, 1)
                with dve.Fori(lo, lo + 2) as pair:
                    mix(2 * pair, kind, pair, False, width)
                    mix(2 * pair + 1, kind, pair, True, width)

            with dve.Fori(0, BH) as h:
                m = 12 + h
                for slot in range(32):
                    if slot in B_POS:
                        b = B_POS.index(slot)
                        g, w = 8 * m + b, P * (b + 1)
                        dve.wait_ge(s.logits_ready, g + 1)
                        if b == 0:
                            dve.wait_ge(s.biasB_loaded, 16 * h + 16)
                        dve.tensor_tensor(SB[:, b % 2, 0:w], wide(L)[:, 0:w], biasB[:, SEQ - w:SEQ], ALU.add)\
                           .then_inc(s.S_biased, 1)
                        dve.wait_ge(s.S_biased, 8 * h + b + 1)
                        dve.wait_ge((s.mask_ld0, s.mask_ld1)[b % 2], 64 * h + 16 * (b // 2) + 16)
                        carry()
                        dve.tensor_tensor_reduce(SB[:, b % 2, 0:w], SB[:, b % 2, 0:w], maskB[:, b % 2, 0:w], 1.0,
                                                 MASKED, ALU.add, ALU.max, mx[:, b, 0:1]).then_inc(s.S_max, 1)
                        negated(g, b, 1, BC_SCALE)
                    if slot - 1 in B_POS:
                        b = B_POS.index(slot - 1)
                        reciprocals(8 * m + b, b, 1)
                    if slot == 9:
                        silu(m)

            dve.wait_ge(s.ot_copied, 8 * 16)
            dve.memset(pace[:, :], 0.0).then_inc(s.out_free, 8)
            dve.wait_ge(s.y_free, 32 * 17)
            for half in range(2):
                if half == 1:
                    dve.wait_ge(s.out_stored, 64)
                with dve.Fori(0, 2) as i:
                    for e in range(2):
                        n = 2 * i + e
                        for j in range(4):
                            if j < 3:
                                dve.wait_ge(s.out_done, 12 * half + 3 * n + j + 1)
                            else:
                                dve.wait_ge(s.w_used, N_OUT + 64 * half + 16 * n + 16)
                            dve.wait_ge(xres_loaded[j], 64 * half + 16 * n + 16)
                            dve.tensor_tensor(h_res[:, j, bass.ds(n * 512, 512)], bank[4 * e + j], x_res[:, j, :],
                                              ALU.add).then_inc(s.out_free, 1)
                dve.wait_ge(s.sq_out, 16 * half + 16)
                dve.tensor_reduce(ssum[:, 0:4], ssq[:, :].rearrange("p (j n) -> p j n", j=4), AX.X, ALU.add)\
                   .then_inc(s.fin_sum, 1)
                dve.wait_ge(s.fin_sum, half + 1)
                dve.tensor_scalar(ms[:, 0:4], ssum[:, 0:4], 1.0 / D, EPS, ALU.mult, ALU.add).then_inc(s.fin_ms, 1)
                dve.wait_ge(s.fin_rt, half + 1)
                dve.reciprocal(rstd[:, 0:4], rms[:, 0:4]).then_inc(s.fin_rstd, 1)
                dve.wait_ge(s.fin_rstd, half + 1)
                dve.wait_ge(s.gf_loaded, 16)
                for j in range(4):
                    dve.scalar_tensor_tensor(out=h_res[:, j, :], in0=h_res[:, j, :], scalar=rstd[:, j:j + 1],
                                             in1=gf_b[:, :], op0=ALU.mult, op1=ALU.mult).then_inc(s.fin_done, 1)

        @block.tensor
        def _(pe):
            def turn(u, b, srcs, inc):
                for i, src in enumerate(srcs):
                    last = pe.transpose(b[:, P * i:P * i + P], src, ident[:, :])
                last.then_inc(inc, 1)

            def norm_turn(j, e, raw, first=False):
                pe.wait_ge(s.normed, j + 1)
                for kg in range(4):
                    if not first:
                        pe.wait_ge(s.tr_lo, 4 * j + kg - 7)
                    turn(0, bank[4 * e + kg], [raw[:, P * (4 * kg + i):P * (4 * kg + i) + P] for i in range(4)], s.turned)

            pe.wait_ge(s.ident_ready, 1)
            norm_turn(0, 0, mem_raw[:, 0, :], first=True)
            norm_turn(1, 1, mem_raw[:, 1, :], first=True)
            with pe.Fori(1, 5) as i:
                norm_turn(2 * i, 0, x_raw[:, 0, :])
                norm_turn(2 * i + 1, 1, x_raw[:, 1, :])
            pe.wait_ge(s.tr_lo, 40)

            def three(dst, hi, lo, rhs_hi, rhs_lo, start, stop):
                for d, r in zip(dst, rhs_hi):
                    pe.matmul(d, hi, r, start=start, stop=False)
                for d, r in zip(dst, rhs_lo):
                    pe.matmul(d, hi, r, start=False, stop=False)
                for d, r in zip(dst, rhs_hi):
                    last = pe.matmul(d, lo, r, start=False, stop=stop)
                return last

            def begin(t, e, half_t):
                if not (isinstance(t, int) and t < 2):
                    pe.wait_ge(proj_free[e], half_t)

            def mem_tile(t, e, half_t):
                begin(t, e, half_t)
                for c in range(4):
                    pe.wait_ge(s.w_low, 4 * t + c + 1)
                    for i in range(4):
                        k = 4 * c + i
                        last = three([PROJ[e][:, 0, 0:NMEM]], w_hi[:, c, P * i:P * i + P], w_lo[:, c, P * i:P * i + P],
                                     [memT_hi[:, k, :]], [memT_lo[:, k, :]], k == 0, k == 15)
                    last.then_inc(s.w_used, 1)

            def slot_of(t, e, half_t, j, width=P):
                if j == 0:
                    begin(t, e, half_t)
                c = j // 2
                if j % 2 == 0:
                    pe.wait_ge(s.w_low, 4 * t + c + 1)
                for k in (2 * j, 2 * j + 1):
                    i = k % 4
                    last = three([PROJ[e][0:width, half, :] for half in range(2)],
                                 w_hi[:, c, P * i:P * i + width], w_lo[:, c, P * i:P * i + width],
                                 [hn_hi[:, k, 512 * half:512 * half + 512] for half in range(2)],
                                 [hn_lo[:, k, 512 * half:512 * half + 512] for half in range(2)], k == 0, k == 15)
                if j % 2 == 1:
                    last.then_inc(s.w_used, 1)

            def turn_values(e, stage, count, n=NB):
                pe.wait_ge(s.stage_ready, count)
                p = wide(PROJ[e])
                for i in range(n):
                    last = pe.transpose(p[:, P * i:P * i + P], stage[:, P * i:P * i + P], ident[:, :])
                last.then_inc(s.v_turned, 1)

            for t in range(CH):
                mem_tile(t, t % 2, t // 2)
            with pe.Fori(2, 4) as i:
                for e in range(2):
                    mem_tile(2 * i + e, e, i)
                    turn_values(e, mv_stage, 2 * i + e - 3, n=2)

            for t in (T_AK, T_AV, T_IQ, T_IQ + 1):
                for j in range(8):
                    slot_of(t, t % 2, t // 2, j)
                if t == T_AV:
                    turn_values(1, av_stage, 5)
            for j in range(8):
                slot_of(T_IK, 0, T_IK // 2, j, width=P)
            pe.wait_ge(s.pg_free, T_IK // 2 + 1)
            for b in range(NB):
                last = pe.transpose(T[:, 4 * b:4 * b + 4], iwT[CHUNK:IKW, P * b:P * b + P], ident[CHUNK:IKW, CHUNK:IKW])
            last.then_inc(s.iw_turned, 1)
            for j in range(8):
                slot_of(T_Q0, 1, T_Q0 // 2, j)
                if j == 0:
                    pe.wait_ge(s.ikz_copied, 1)
                    pe.wait_ge(s.ikz_moved, 16)
                    pe.wait_ge(s.zeroed, 2)
                for u in range(3 * j, 3 * j + 3):
                    b, h = 2 + u // 4, u % 4
                    if u == 1:
                        pe.wait_ge(s.iw_ready, 1)
                    if u >= 2:
                        pe.wait_ge(s.relu_ready, u - 1)
                    dst = wide(L if u % 2 == 0 else TO)
                    for a in range(0, P * (b + 1), 512):
                        z = min(a + 512, P * (b + 1))
                        last = pe.matmul(dst[:, a:z], iq[:, h // 2, P * b:P * b + P], ikz[:, h % 2, a:z],
                                         start=True, stop=True)
                    last.then_inc(s.idx_ready, 1)

            def logits(m, b, kind):
                if kind == "C":
                    if b == 0:
                        pe.wait_ge(s.pq_free, m + 7)
                        pe.wait_ge(s.memkv_ready, m + 1)
                    if b >= 2:
                        pe.wait_ge(s.probs_ready, 8 * m + b - 1)
                    last = pe.matmul(L[:, b % 2, 0:NMEM], q0[:, P * b:P * b + P], mk_now[:, :], start=True, stop=True)
                else:
                    if b == 0:
                        pe.wait_ge(s.pq_free, m + 7)
                    if b >= 2:
                        pe.wait_ge(s.S_max, 8 * m + b - 1)
                    k0 = P if b == 0 else 0
                    a = P * (b - 1) + k0
                    dst = L[:, b % 2, :].rearrange("p (e k) -> p e k", e=2)[:, :, k0:256]
                    last = pe.matmul(dst, q0[:, P * b:P * b + P], kz[:, :, a:P * (b + 1)], start=True, stop=True)
                last.then_inc(s.logits_ready, 1)

            def turn_probs(m, b, kind):
                pe.wait_ge(s.norm_ready, 8 * m + b + 1)
                for kt in range(1 if kind == "A" and b == 0 else 0, 2):
                    for e in range(2 if kind == "A" else 1):
                        i = 2 * kt + e if kind == "A" else kt
                        last = pe.transpose(T[:, P * i:P * i + P], SA[:, b % 3, e, P * kt:P * kt + P], ident[:, :])
                last.then_inc(s.pt_ready, 1)

            def weigh(m, b, kind, group):
                pe.wait_ge(s.pt_copied, 8 * m + b + 1)
                if b >= 1:
                    pe.wait_ge(s.ot_copied, 8 * m + b)
                if kind == "C":
                    for kt in range(2):
                        last = pe.matmul(O[:, 0:P], mv_now[:, kt, :], PT[:, P * kt:P * kt + P], start=kt == 0, stop=kt == 1)
                else:
                    kts = (1,) if b == 0 else (0, 1)
                    for e in range(2):
                        for kt in kts:
                            i = 2 * kt + e
                            last = pe.matmul(O[CHUNK * e:CHUNK * e + CHUNK, 0:P],
                                             av[:, b - 1 + kt, CHUNK * group:CHUNK * group + CHUNK],
                                             PT[:, P * i:P * i + P], start=kt == kts[0], stop=kt == 1)
                last.then_inc(s.ot_ready, 1)

            def mix(m, kind, group):
                for slot in range(16):
                    t = T_LOOP + 2 * m + slot // 8
                    slot_of(t, slot // 8, m + 7, slot % 8)
                    if 4 <= slot <= 11:
                        weigh(m, slot - 4, kind, group)
                    if 3 <= slot <= 10:
                        turn_probs(m, slot - 3, kind)
                    if slot <= 7:
                        logits(m, slot, kind)

            with pe.Fori(0, 4) as m:
                mix(m, "C", 0)
            pe.wait_ge(s.kz_moved, 16)
            pe.wait_ge(s.zeroed, 1)
            with pe.Fori(4, 8) as m:
                mix(m, "A", 0)
            pe.wait_ge(s.kz1_copied, 1)
            pe.wait_ge(s.kz_moved, 32)
            with pe.Fori(8, 12) as m:
                mix(m, "A", 1)

            for t in (T_B, T_B + 1):
                for j in range(8):
                    slot_of(t, t % 2, t // 2, j)
            turn_values(1, bv_stage, 6)
            for h in range(BH):
                m = 12 + h
                q, bk, bv = (q0, q1)[h % 2], (bk0, bk1)[h % 2], (bv0, bv1)[h % 2]
                for slot in range(32):
                    if h < 3 or slot < 8:
                        t = T_BHEAD + 4 * h + slot // 8
                        slot_of(t, t % 2, t // 2, slot % 8)
                    for b in range(NB):
                        if slot == B_POS[b] + 5:
                            pe.wait_ge(s.bpt_copied, 12 * h + (2 * b - 2 if b >= 4 else b + 1))
                            if b >= 1:
                                pe.wait_ge(s.ot_copied, 8 * m + b)
                            else:
                                pe.wait_ge(s.pq_free, 20 + 2 * h)
                            for kt in range(b + 1):
                                last = pe.matmul(O[:, 0:P], bv[:, kt, :], PT[:, P * kt:P * kt + P], start=kt == 0, stop=kt == b)
                            last.then_inc(s.ot_ready, 1)
                    for b in range(4, NB):
                        if slot == B_POS[b] + 4:
                            pe.wait_ge(s.bpt_copied, 12 * h + 2 * b - 3)
                            for kt in range(4, b + 1):
                                last = pe.transpose(T[:, P * (kt - 4):P * (kt - 3)], SB[:, b % 2, P * kt:P * kt + P], ident[:, :])
                            last.then_inc(s.bpt_ready, 1)
                    for b in range(NB):
                        if slot == B_POS[b] + 3:
                            pe.wait_ge(s.norm_ready, 8 * m + b + 1)
                            for kt in range(min(4, b + 1)):
                                last = pe.transpose(T[:, P * kt:P * kt + P], SB[:, b % 2, P * kt:P * kt + P], ident[:, :])
                            last.then_inc(s.bpt_ready, 1)
                    if slot in B_POS:
                        b = B_POS.index(slot)
                        if b == 0:
                            pe.wait_ge(s.pq_free, 19 if h == 0 else 19 + 2 * h)
                            pe.wait_ge(s.pg_free, 20 + 2 * h)
                        for a in range(0, P * (b + 1), 512):
                            z = min(a + 512, P * (b + 1))
                            last = pe.matmul(wide(L)[:, a:z], q[:, P * b:P * b + P], bk[:, a:z], start=True, stop=True)
                        last.then_inc(s.logits_ready, 1)
                if h < 3:
                    turn_values(1, bv_stage, 7 + h)

            def out_tile(q, e, half):
                banks = [bank[4 * e + j] for j in range(4)]
                pe.wait_ge(s.out_free, 4 * q + 4)
                for k in range(16):
                    if half == 0 and e == 0:
                        pe.wait_ge(y_loaded[k], 32)
                    pe.wait_ge(s.w_low, N_OUT + 16 * q + k + 1)
                    c = k % 4
                    for j in range(4):
                        cols = slice(512 * half + P * j, 512 * half + P * j + P)
                        pe.matmul(banks[j], y_hi[:, k, cols], w_hi[:, c, :], start=k == 0, stop=False)
                        pe.matmul(banks[j], y_hi[:, k, cols], w_lo[:, c, :], start=False, stop=False)
                        last = pe.matmul(banks[j], y_lo[:, k, cols], w_hi[:, c, :], start=False, stop=k == 15)
                        if k == 15 and j < 3:
                            last.then_inc(s.out_done, 1)
                    last.then_inc(s.w_used, 1)

            for half in range(2):
                if half == 1:
                    for k in range(16):
                        pe.wait_ge(y_loaded[k], 64)
                with pe.Fori(0, 2) as i:
                    for e in range(2):
                        out_tile(4 * half + 2 * i + e, e, half)


_INS = ["x", "mem", "g_norm", "w_in", "sinks", "rel_bias", "g_mem", "w_mem_kv", "w_out", "g_final"]
_OUTS = [((1, SEQ, D), "float32")]


def kernel(**inputs):
    import numpy as _np
    import concourse.bacc as _bacc
    from concourse import mybir as _mybir
    from concourse.bass_utils import run_bass_kernel_spmd as _run

    nc = _bacc.Bacc("TRN2", target_bir_lowering=False, num_devices=1, dynamic_dma_scratch_size=256)
    arrays, args = {}, []
    for name in _INS:
        a = _np.ascontiguousarray(inputs[name])
        arrays[f"in_{name}_dram"] = a
        args.append(nc.dram_tensor(f"in_{name}_dram", a.shape, _mybir.dt.from_np(a.dtype), kind="ExternalInput").ap())
    for i, (shape, dtype) in enumerate(_OUTS):
        dt = _mybir.dt.from_np(_np.dtype(dtype))
        args.append(nc.dram_tensor(f"out_{i}_dram", shape, dt, kind="ExternalOutput").ap())
    hybrid_layer(nc, *args)
    r = _run(nc, [arrays], core_ids=[0])
    got = tuple(r.results[0][f"out_{i}_dram"] for i in range(len(_OUTS)))
    return got[0]
```

```python
import math
from contextlib import ExitStack

import concourse.bass as bass
from concourse import mybir

F32 = mybir.dt.float32
F32R = mybir.dt.float32r
BF16 = mybir.dt.bfloat16
ALU = mybir.AluOpType
ACT = mybir.ActivationFunctionType
AX = mybir.AxisListType

P = 128
SEQ, D = 1024, 2048
KT = D // P
NB = SEQ // P
NMEM = 256
EPS = 1e-6
CHUNK = 64
TOPK = 256
ROUNDS = TOPK // 8
NBUCKET, MAXDIST = 32, 1024
AH, BH, CH = 16, 4, 4
A_SCALE = 64 ** -0.5
BC_SCALE = 128 ** -0.5
MASKED = -3.0e38
TAKEN = -3.3e38
BELOW_MASKED = -3.2e38

C_AQ, C_AK, C_AV = 0, 1024, 1152
C_BQ, C_BK, C_BV = 1280, 1792, 2304
C_IQ, C_IK = 2816, 3072
C_CQ, C_GATE = 3140, 3652
IKW = 68

MEM_TILES = 8
T_AK, T_AV, T_IQ, T_IK, T_Q0 = 8, 9, 10, 12, 13
T_LOOP = 14
T_B = T_LOOP + 24
T_BHEAD = T_B + 2
T_ALL = T_BHEAD + 13
N_OUT = 4 * T_ALL
B_POS = [0, 3, 6, 10, 14, 18, 22, 26]
B_LAST = [0, 2, 4, 6, 9, 12, 15, 18]


def bucket_edges():
    half, exact = NBUCKET // 2, NBUCKET // 4

    def bucket(rel):
        n = abs(rel)
        if n < exact:
            b = n
        else:
            b = min(half - 1, exact + int(math.log(n / exact) / math.log(MAXDIST / exact) * (half - exact)))
        return b + (half if rel > 0 else 0)

    out, first = [], -(SEQ - 1)
    for rel in range(-(SEQ - 1) + 1, P + 1):
        if rel == P or bucket(rel) != bucket(first):
            out.append((first, rel, bucket(first)))
            first = rel
    return out


def mix_tile(m):
    return m + 12 if m < 4 else m - 4


class Semaphores:

    def __init__(self, sem):
        self.const_loaded = sem("const_loaded")
        self.rb_loaded = sem("rb_loaded")
        self.rb_scaled = sem("rb_scaled")
        self.v_built = sem("v_built")
        self.va_stored = sem("va_stored")
        self.vb_stored = sem("vb_stored")
        self.ta_built = sem("ta_built")
        self.tb_built = sem("tb_built")
        self.ta_fill = sem("ta_fill")
        self.ta_done = sem("ta_done")
        self.ident_zero = sem("ident_zero")
        self.ident_ready = sem("ident_ready")
        self.zeroed = sem("zeroed")
        self.mem_loaded0 = sem("mem_loaded0")
        self.mem_loaded1 = sem("mem_loaded1")
        self.g_loaded = sem("g_loaded")
        self.sq_done = sem("sq_done")
        self.ms_done = sem("ms_done")
        self.rt_done = sem("rt_done")
        self.rstd_done = sem("rstd_done")
        self.normed = sem("normed")
        self.turned = sem("turned")
        self.tr_hi = sem("tr_hi")
        self.tr_lo = sem("tr_lo")
        self.w_high = sem("w_high")
        self.w_low = sem("w_low")
        self.w_used = sem("w_used")
        self.pg_free = sem("pg_free")
        self.pq_free = sem("pq_free")
        self.stage_ready = sem("stage_ready")
        self.v_turned = sem("v_turned")
        self.kz_moved = sem("kz_moved")
        self.kz1_copied = sem("kz1_copied")
        self.kz1_moved = sem("kz1_moved")
        self.ikz_copied = sem("ikz_copied")
        self.ikz_moved = sem("ikz_moved")
        self.iwT_ready = sem("iwT_ready")
        self.iw_turned = sem("iw_turned")
        self.iw_ready = sem("iw_ready")
        self.idx_ready = sem("idx_ready")
        self.relu_ready = sem("relu_ready")
        self.idx_added = sem("idx_added")
        self.isc_done = sem("isc_done")
        self.isc_st0 = sem("isc_st0")
        self.isc_st1 = sem("isc_st1")
        self.mask_done = sem("mask_done")
        self.mask_stored = sem("mask_stored")
        self.W_loaded = sem("W_loaded")
        self.top_max = sem("top_max")
        self.top_out = sem("top_out")
        self.gate_exp = sem("gate_exp")
        self.gate_step = sem("gate_step")
        self.sg_ready = sem("sg_ready")
        self.biasA_loaded = sem("biasA_loaded")
        self.sink_ready = sem("sink_ready")
        self.memkv_ready = sem("memkv_ready")
        self.logits_ready = sem("logits_ready")
        self.S_biased = sem("S_biased")
        self.S_max = sem("S_max")
        self.neg_ready = sem("neg_ready")
        self.probs_ready = sem("probs_ready")
        self.recip_ready = sem("recip_ready")
        self.norm_ready = sem("norm_ready")
        self.pt_ready = sem("pt_ready")
        self.pt_copied = sem("pt_copied")
        self.ot_ready = sem("ot_ready")
        self.ot_copied = sem("ot_copied")
        self.yf_ready = sem("yf_ready")
        self.y_high = sem("y_high")
        self.y_low = sem("y_low")
        self.y_free = sem("y_free")
        self.biasB_loaded = sem("biasB_loaded")
        self.mask_ld0 = sem("mask_ld0")
        self.mask_ld1 = sem("mask_ld1")
        self.bpt_ready = sem("bpt_ready")
        self.bpt_copied = sem("bpt_copied")
        self.out_done = sem("out_done")
        self.fin_sum = sem("fin_sum")
        self.out_free = sem("out_free")
        self.sq_out = sem("sq_out")
        self.h_added = sem("h_added")
        self.fin_ms = sem("fin_ms")
        self.fin_rt = sem("fin_rt")
        self.fin_done = sem("fin_done")
        self.out_stored = sem("out_stored")
        self.gf_loaded = sem("gf_loaded")


def hybrid_layer(nc, x, mem, g_norm, w_in, sinks, rel_bias, g_mem, w_mem_kv, w_out, g_final, out):
    ctx = ExitStack()
    with ctx:
        def dram(name, shape, dt=F32):
            return nc.dram_tensor(name, shape, dt, kind="Internal").ap()

        VA_LEN, VB_LEN = 384, 1152
        va_dram = dram("va_dram", (AH, VA_LEN))
        vb_dram = dram("vb_dram", (BH, VB_LEN))
        ta_dram = dram("ta_dram", (AH, P, 256))
        tb_dram = dram("tb_dram", (BH, P, SEQ))
        isc_dram = dram("isc_dram", (6, P, SEQ))
        mask_dram = dram("mask_dram", (7, P, SEQ), BF16)
        yhi_dram = dram("yhi_dram", (16, P, SEQ), F32R)
        ylo_dram = dram("ylo_dram", (16, P, SEQ), F32R)

        base = (nc.sbuf_base + 127) // 128 * 128
        end = [base]

        def at(name, shape, dt, offset):
            return nc.alloc_sbuf_tensor_at(name, shape, dt, offset=offset)

        def take(nbytes):
            end[0] += nbytes
            return end[0] - nbytes

        KB = 1024
        R1 = take(128 * KB)
        hn_hi = at("hn_hi", [P, KT, SEQ], F32R, R1)
        hn_lo = at("hn_lo", [P, KT, SEQ], F32R, R1 + 64 * KB)
        mem_raw = at("mem_raw", [P, 2, D], F32, R1 + 96 * KB)
        gmem_b = at("gmem_b", [P, D], F32, R1 + 112 * KB)
        y_hi = at("y_hi", [P, KT, SEQ], F32R, R1)
        y_lo = at("y_lo", [P, KT, SEQ], F32R, R1 + 64 * KB)
        R2 = take(24 * KB)
        w_raw = at("w_raw", [P, 4, 512], F32, R2)
        w_hi = at("w_hi", [P, 4, 512], F32R, R2 + 8 * KB)
        w_lo = at("w_lo", [P, 4, 512], F32R, R2 + 16 * KB)
        R3 = take(32 * KB)
        memT_hi = at("memT_hi", [P, KT, NMEM], F32R, R3)
        memT_lo = at("memT_lo", [P, KT, NMEM], F32R, R3 + 16 * KB)
        SA = at("SA", [P, 3, 2, 257], F32, R3)
        SB = at("SB", [P, 2, SEQ], F32, R3)
        acc = at("acc", [P, 2, SEQ], F32, R3)
        av_stage = at("av_stage", [P, SEQ], F32, R3)
        PT = at("PT", [P, SEQ], F32, R3 + 8 * KB)
        relu_s = at("relu_s", [P, 2, SEQ], F32, R3 + 8 * KB)
        W = at("W", [P, SEQ], F32, R3 + 12 * KB)
        iwT = at("iwT", [P, SEQ], F32, R3 + 12 * KB)
        bv_stage = at("bv_stage", [P, SEQ], F32, R3 + 12 * KB)
        oT = at("oT", [P, SEQ], F32, R3 + 16 * KB)
        yf = at("yf", [P, SEQ], F32, R3 + 20 * KB)
        iq = at("iq", [P, 2, SEQ], F32, R3 + 16 * KB)
        yhi_s = at("yhi_s", [P, SEQ], F32R, R3 + 24 * KB)
        ylo_s = at("ylo_s", [P, SEQ], F32R, R3 + 28 * KB)
        ikz = at("ikz", [P, 2, SEQ], F32, R3 + 24 * KB)
        h_res = at("h_res", [P, 4, D], F32, R3)
        R4 = take(16 * KB)
        x_raw = at("x_raw", [P, 2, D], F32, R4)
        q0 = at("q0", [P, SEQ], F32, R4)
        kz = at("kz", [P, 2, SEQ], F32, R4 + 4 * KB)
        gate_last = at("gate_last", [P, SEQ], F32, R4)
        q1 = at("q1", [P, SEQ], F32, R4 + 4 * KB)
        bk1 = at("bk1", [P, SEQ], F32, R4 + 8 * KB)
        ak = at("ak", [P, SEQ], F32, R4 + 12 * KB)
        biasB = at("biasB", [P, SEQ], F32, R4 + 12 * KB)
        x_res = at("x_res", [P, 4, 512], F32, R4)
        R5 = take(16 * KB)
        VA = at("VA", [AH, VA_LEN], F32, R5)
        VB = at("VB", [BH, VB_LEN], F32, R5 + 2 * KB)
        mk = at("mk", [P, CH, NMEM], F32, R5)
        bk0 = at("bk0", [P, SEQ], F32, R5)
        mv = at("mv", [P, 2, CH, P], F32, R5 + 4 * KB)
        kz1 = at("kz1", [P, 2, SEQ], F32, R5)
        bv0 = at("bv0", [P, NB, P], F32, R5 + 4 * KB)
        gx_b = at("gx_b", [P, D], F32, R5 + 8 * KB)
        av = at("av", [P, NB, P], F32, R5 + 8 * KB)
        bv1 = at("bv1", [P, NB, P], F32, R5 + 8 * KB)
        sg = at("sg", [P, SEQ], F32, R5 + 12 * KB)
        gf_b = at("gf_b", [P, D], F32, R5)
        R6 = take(6 * KB)
        biasA = at("biasA", [P, 2, 256], F32, R6 + 2 * KB)
        maskB = at("maskB", [P, 2, SEQ], BF16, R6)
        mask_s = at("mask_s", [P, SEQ], BF16, R6 + 4 * KB)
        mv_stage = at("mv_stage", [P, NMEM], F32, R6)
        mk_now = at("mk_now", [P, NMEM], F32, R6)
        mv_now = at("mv_now", [P, 2, P], F32, R6 + KB)
        sq_junk = at("sq_junk", [P, D], BF16, R6)
        ident = at("ident", [P, P], F32, take(512))
        sinks8 = at("sinks8", [P, AH], F32, take(64))
        sink_now = at("sink_now", [P, 2], F32, take(32))
        mx = at("mx", [P, NB, 2], F32, take(64))
        neg = at("neg", [P, NB, 2], F32, take(64))
        den = at("den", [P, NB, 2], F32, take(64))
        rec = at("rec", [P, NB, 2], F32, take(64))
        iw = at("iw", [P, NB, 4], F32, take(128))
        top8 = at("top8", [P, 8], F32, take(32))
        ssq = at("ssq", [P, 16], F32, take(64))
        rms = at("rms", [P, 16], F32, take(64))
        rstd = at("rstd", [P, 16], F32, take(64))
        rfix = at("rfix", [P, 4], F32, take(32))
        pace = at("pace", [P, 1], F32, take(32))
        ssum = at("ssum", [P, 4], F32, take(32))
        ms = at("ms", [P, 4], F32, take(32))
        masked = at("masked", [CHUNK, CHUNK], F32, take(256))
        rbA = at("rbA", [AH, NBUCKET], F32, R5 + 7 * KB)
        rbB = at("rbB", [BH, NBUCKET], F32, R5 + 7 * KB + 128)
        assert end[0] <= nc.sbuf_usable_end, (end[0], nc.sbuf_usable_end)

        def pb(name):
            return ctx.enter_context(nc.psum_tensor(name, [P, 2, 512], F32))

        PG, PQ, L, TO = pb("PG"), pb("PQ"), pb("L"), pb("TO")
        PROJ = (PG, PQ)
        T, O = TO[:, 0, :], TO[:, 1, :]
        bank = [t[:, i, :] for t in (PG, PQ, L, TO) for i in range(2)]

        def wide(t):
            return t[:, :, :].rearrange("p a b -> p (a b)")

        s = Semaphores(lambda n: ctx.enter_context(nc.semaphore(n)))
        w_loaded = [ctx.enter_context(nc.semaphore(f"w_loaded{i}")) for i in range(4)]
        x_loaded = [ctx.enter_context(nc.semaphore(f"x_loaded{i}")) for i in range(2)]
        xres_loaded = [ctx.enter_context(nc.semaphore(f"xres_loaded{i}")) for i in range(4)]
        y_loaded = [ctx.enter_context(nc.semaphore(f"y_loaded{i}")) for i in range(15)]
        proj_free = (s.pg_free, s.pq_free)

        w_in_v = w_in[0].rearrange("(c k p) n -> c p k n", k=4, p=P)
        w_mem_v = w_mem_kv[0].rearrange("(c k p) n -> c p k n", k=4, p=P)
        x_v = x[0].rearrange("(t p) d -> t p d", p=P)
        mem_v = mem[0].rearrange("(t p) d -> t p d", p=P)
        out_v = out[0].rearrange("(t p) d -> t p d", p=P)
        w_out_v = w_out[0].rearrange("(m p) n -> m p n", p=P)

        block = ctx.enter_context(nc.Block())

        @block.sync
        def _(sp):
            def chunk(n, c, src, k=4, width=P, first=False):
                if not first:
                    sp.wait_ge(s.w_low, n - 3)
                dst = w_raw[:, c, 0:512].rearrange("p (k n) -> p k n", k=k)[:, :, 0:width]
                sp.dma_start(dst, src).then_inc(w_loaded[c], 16)

            def tile(t, view, col, width=P, first=False):
                for c in range(4):
                    chunk(4 * t + c, c, view[c, :, :, bass.ds(col, width)], width=width, first=first)

            with nc.allow_non_contiguous_dma(reason="a few hundred elements"):
                sp.dma_start(rbA[:, :], rel_bias[:, 0:AH].rearrange("n h -> h n")).then_inc(s.rb_loaded, 16)
                sp.dma_start(rbB[:, :], rel_bias[:, AH:AH + BH].rearrange("n h -> h n")).then_inc(s.rb_loaded, 16)
            sp.dma_start(sinks8[:, :], sinks[0:1, :].to_broadcast([P, AH])).then_inc(s.const_loaded, 16)
            sp.dma_start(gmem_b[:, :], g_mem[0:1, :].to_broadcast([P, D])).then_inc(s.g_loaded, 16)
            sp.dma_start(mem_raw[:, 0, :], mem_v[0]).then_inc(s.mem_loaded0, 16)
            sp.dma_start(mem_raw[:, 1, :], mem_v[1]).then_inc(s.mem_loaded1, 16)
            sp.dma_start(gx_b[:, :], g_norm[0:1, :].to_broadcast([P, D])).then_inc(s.g_loaded, 16)
            for e in range(2):
                sp.dma_start(x_raw[:, e, :], x_v[e]).then_inc(x_loaded[e], 16)
            tile(0, w_mem_v, 0, first=True)
            sp.wait_ge(s.v_built, 1)
            sp.dma_start(va_dram, VA[:, :]).then_inc(s.va_stored, 16)
            sp.dma_start(vb_dram, VB[:, :]).then_inc(s.vb_stored, 16)
            sp.wait_ge(s.va_stored, 16)
            skew = bass.AP(va_dram.tensor, va_dram.offset + P - 1, [[VA_LEN, AH], [-1, P], [1, 256]])
            sp.dma_start(ta_dram, skew).then_inc(s.ta_built, 16)
            sp.wait_ge(s.vb_stored, 16)
            skew = bass.AP(vb_dram.tensor, vb_dram.offset + P - 1, [[VB_LEN, BH], [-1, P], [1, SEQ]])
            sp.dma_start(tb_dram, skew).then_inc(s.tb_built, 16)
            with sp.Fori(0, NB // 2 - 1) as i:
                for e in range(2):
                    sp.wait_ge(s.turned, 8 + 8 * i + 4 * e + 4)
                    sp.dma_start(x_raw[:, e, :], x_v[2 * i + 2 + e]).then_inc(x_loaded[e], 16)
            sp.wait_ge(s.ta_built, 16)
            sp.wait_ge(s.ta_fill, 1)
            neg_src = masked[:, :].rearrange("p (o k) -> p o k", o=1).to_broadcast([CHUNK, AH, CHUNK])
            ta_w = ta_dram.rearrange("h p k -> p h k")
            sp.dma_start(ta_w[0:CHUNK, :, 192:256], neg_src).then_inc(s.ta_done, 16)
            sp.dma_start(ta_w[CHUNK:P, :, 0:CHUNK], neg_src).then_inc(s.ta_done, 16)

            with sp.Fori(1, MEM_TILES) as t:
                tile(t, w_mem_v, t * P)
            tile(T_AK, w_in_v, C_AK)
            tile(T_AV, w_in_v, C_AV)
            tile(T_IQ, w_in_v, C_IQ)
            tile(T_IQ + 1, w_in_v, C_IQ + P)
            tile(T_IK, w_in_v, C_IK, width=IKW)
            tile(T_Q0, w_in_v, C_CQ)
            with sp.Fori(0, 3) as i:
                tile(T_LOOP + 2 * i, w_in_v, C_GATE + 12 * P + i * P)
                tile(T_LOOP + 1 + 2 * i, w_in_v, C_CQ + P + i * P)
            tile(T_LOOP + 6, w_in_v, C_GATE + 15 * P)
            tile(T_LOOP + 7, w_in_v, C_AQ)
            sp.wait_ge(s.ta_done, 32)

            def window_bias(i):
                sp.wait_ge(s.S_max, 8 * i + 32)
                sp.dma_start(biasA[:, :, :], ta_dram[bass.ds(2 * i, 2), :, :].rearrange("h p k -> p h k"))\
                  .then_inc(s.biasA_loaded, 16)

            with sp.Fori(0, 7) as i:
                tile(T_LOOP + 8 + 2 * i, w_in_v, C_GATE + i * P)
                window_bias(i)
                tile(T_LOOP + 9 + 2 * i, w_in_v, C_AQ + P + i * P)
            tile(T_LOOP + 22, w_in_v, C_GATE + 7 * P)
            window_bias(7)
            tile(T_LOOP + 23, w_in_v, C_BQ)
            tile(T_B, w_in_v, C_BK)
            tile(T_B + 1, w_in_v, C_BV)
            with sp.Fori(0, 3) as h:
                tile(T_BHEAD + 4 * h, w_in_v, C_GATE + 8 * P + h * P)
                tile(T_BHEAD + 4 * h + 1, w_in_v, C_BQ + P + h * P)
                tile(T_BHEAD + 4 * h + 2, w_in_v, C_BK + P + h * P)
                tile(T_BHEAD + 4 * h + 3, w_in_v, C_BV + P + h * P)
            tile(T_BHEAD + 12, w_in_v, C_GATE + 11 * P)

            def load_y(half, m):
                cols = slice(512 * half, 512 * half + 512)
                sp.dma_start(y_hi[:, m, cols].bitcast(F32), yhi_dram[m, :, cols].bitcast(F32)).then_inc(y_loaded[m], 16)
                sp.dma_start(y_lo[:, m, cols].bitcast(F32), ylo_dram[m, :, cols].bitcast(F32)).then_inc(y_loaded[m], 16)

            def load_residual(q, col, half):
                for j in range(4):
                    if not (isinstance(q, int) and q == 0):
                        sp.wait_ge(s.out_free, 8 + 4 * (q - 1) + j + 1)
                    sp.dma_start(x_res[:, j, :], x_v[4 * half + j, :, bass.ds(col, 512)]).then_inc(xres_loaded[j], 16)

            def out_chunk(q, m, col):
                chunk(N_OUT + 16 * q + m, m % 4, w_out_v[mix_tile(m), :, bass.ds(col, 512)], k=1, width=512)

            for m in range(16):
                out_chunk(0, m, 0)
                if m in (0, 14):
                    sp.wait_ge(s.y_free, 32 * (15 if m == 0 else 16))
                if m < 15:
                    if m % 4 == 0:
                        sp.wait_ge(s.w_used, 4 * T_ALL - 4 + m // 4 + 1)
                    load_y(0, m)
            sp.wait_ge(s.logits_ready, 8 * 16)
            sp.wait_ge(s.sg_ready, 1)
            load_residual(0, 0, 0)

            def out_loads(q, col, half, y_from=15):
                for m in range(16):
                    if m == 8:
                        load_residual(q, col, half)
                    out_chunk(q, m, col)
                    if m % 2 == 0 and y_from + m // 2 < 15:
                        load_y(1, y_from + m // 2)

            out_loads(1, 512, 0, y_from=0)
            out_loads(2, 1024, 0, y_from=8)
            sp.dma_start(gf_b[:, :], bass.AP(g_final.tensor, g_final.offset, [[0, P], [1, D]]))\
              .then_inc(s.gf_loaded, 16)
            out_loads(3, 1536, 0)
            with sp.Fori(1, 5) as n:
                out_loads(3 + n, n * 512 - 512, 1)

        @block.gpsimd
        def _(pool):
            pool.memset(ident[:, :], 0.0).then_inc(s.ident_zero, 1)
            pool.wait_ge(s.ident_zero, 1)
            pool.affine_select(out=ident[:, :], in_=ident[:, :], compare_op=ALU.not_equal, fill=1.0, base=0,
                               pattern=[[-1, P]], channel_multiplier=1).then_inc(s.ident_ready, 1)

            def low(n, c):
                pool.wait_ge(s.w_high, n + 1)
                pool.tensor_tensor(w_lo[:, c, :], w_raw[:, c, :], w_hi[:, c, :].bitcast(F32), ALU.subtract)\
                    .then_inc(s.w_low, 1)

            for n in range(3):
                low(n, n % 4)
            with pool.Fori(0, T_LOOP) as t:
                for c in range(4):
                    low(4 * t + c + 3, (c + 3) % 4)

            def normalise(g, b, kind):
                pool.wait_ge(s.recip_ready, g + 1)
                if kind == "A":
                    k0 = P if b == 0 else 0
                    for e in range(2):
                        v = SA[:, b % 3, e, k0:256]
                        last = pool.tensor_tensor(v, v, rec[:, b, e:e + 1].to_broadcast([P, 256 - k0]), ALU.mult)
                else:
                    w = NMEM if kind == "C" else P * (b + 1)
                    v = SA[:, b % 3, 0, 0:w] if kind == "C" else SB[:, b % 2, 0:w]
                    last = pool.tensor_tensor(v, v, rec[:, b, 0:1].to_broadcast([P, w]), ALU.mult)
                last.then_inc(s.norm_ready, 1)

            def gated(m, pg_count):
                pool.wait_ge(s.ot_copied, 8 * m + 8)
                pool.wait_ge(s.pg_free, pg_count)
                pool.tensor_tensor(yf[:, :], oT[:, :], sg[:, :], ALU.mult).then_inc(s.yf_ready, 1)
                pool.wait_ge(s.y_free, 32 * m + 32)
                pool.tensor_tensor(yhi_s[:, :], oT[:, :], sg[:, :], ALU.mult).then_inc(s.y_high, 1)

            def y_low(m):
                pool.wait_ge(s.y_high, m + 1)
                pool.tensor_tensor(ylo_s[:, :], yf[:, :], yhi_s[:, :].bitcast(F32), ALU.subtract)\
                    .then_inc(s.y_low, 1)

            def mix(m, kind):
                for slot in range(16):
                    if slot % 2 == 0:
                        low(4 * T_LOOP + 8 * m + slot // 2 + 3, (slot // 2 + 3) % 4)
                    if 1 <= slot <= 8:
                        normalise(8 * m + slot - 1, slot - 1, kind)
                    if slot == 13:
                        gated(m, m + 8)
                    if slot == 15:
                        y_low(m)

            with pool.Fori(0, 4) as m:
                mix(m, "C")
            with pool.Fori(4, 12) as m:
                mix(m, "A")
            for n in range(4 * T_B, 4 * T_BHEAD):
                low(n + 3, (n + 3) % 4)

            def head(h, pos, last=False):
                m = 12 + h
                for slot in range(24 if last else 32):
                    if slot % 2 == 0 and slot < (8 if last else 32):
                        low(4 * T_BHEAD + 16 * h + slot // 2 + 3, (slot // 2 + 3) % 4)
                    if last and slot >= 8:
                        low(N_OUT + slot - 8 + 3, (slot - 8 + 3) % 4)
                    if slot - 1 in pos:
                        b = pos.index(slot - 1)
                        normalise(8 * m + b, b, "B")
                    if last and slot == 14:
                        y_last(0)
                if last:
                    y_last(1)
                else:
                    gated(m, 21 + 2 * h)
                    y_low(m)

            def y_last(half):
                cols = slice(512 * half, 512 * half + 512)
                pool.wait_ge(s.ot_copied, 8 * 15 + 4 + 4 * half)
                pool.wait_ge(s.sg_ready, 1)
                pool.tensor_tensor(yf[:, cols], oT[:, cols], sg[:, cols], ALU.mult).then_inc(s.yf_ready, 1)
                pool.wait_ge(s.y_high, 16 + half)
                pool.tensor_tensor(y_lo[:, 15, cols], yf[:, cols], y_hi[:, 15, cols].bitcast(F32), ALU.subtract)\
                    .then_inc(s.y_low, 1)

            with pool.Fori(0, BH - 1) as h:
                head(h, B_POS)
            head(BH - 1, B_LAST, last=True)
            low(N_OUT + 19, 3)
            with pool.Fori(N_OUT // 4 + 5, N_OUT // 4 + 32) as t:
                for c in range(4):
                    low(4 * t + c, c)

        isc_stored = (s.isc_st0, s.isc_st1)
        isc_width = [512, 512, 768, 768, 1024, 1024]

        def store_scores(act, b):
            act.wait_ge(s.isc_done, b - 1)
            w = isc_width[b - 2]
            act.dma_start(isc_dram[b - 2, :, 0:w], acc[:, b % 2, 0:w]).then_inc(isc_stored[b % 2], 16)

        @block.scalar
        def _(act):
            def norm_root(j, e, raw):
                act.activation(sq_junk[:, :], raw, ACT.Square, accum_out=ssq[:, e:e + 1]).then_inc(s.sq_done, 1)
                act.wait_ge(s.ms_done, j + 1)
                act.activation(rms[:, e:e + 1], ms[:, e:e + 1], ACT.Sqrt).then_inc(s.rt_done, 1)

            def norm_high(j, e, dst, col):
                for kg in range(4):
                    act.wait_ge(s.turned, 4 * j + kg + 1)
                    act.activation(dst[:, 4 * kg:4 * kg + 4, bass.ds(col, P)],
                                   bank[4 * e + kg].rearrange("p (k t) -> p k t", k=4), ACT.Copy).then_inc(s.tr_hi, 1)

            act.wait_ge(s.mem_loaded0, 16)
            norm_root(0, 0, mem_raw[:, 0, :])
            act.wait_ge(s.mem_loaded1, 16)
            norm_root(1, 1, mem_raw[:, 1, :])
            norm_high(0, 0, memT_hi, 0)
            act.wait_ge(x_loaded[0], 16)
            norm_root(2, 0, x_raw[:, 0, :])
            norm_high(1, 1, memT_hi, P)
            with act.Fori(0, 3) as i:
                act.wait_ge(x_loaded[1], 16 * i + 16)
                norm_root(2 * i + 3, 1, x_raw[:, 1, :])
                norm_high(2 * i + 2, 0, hn_hi, 2 * P * i)
                act.wait_ge(x_loaded[0], 16 * i + 32)
                norm_root(2 * i + 4, 0, x_raw[:, 0, :])
                norm_high(2 * i + 3, 1, hn_hi, 2 * P * i + P)
            act.wait_ge(x_loaded[1], 64)
            norm_root(9, 1, x_raw[:, 1, :])
            norm_high(8, 0, hn_hi, 6 * P)
            norm_high(9, 1, hn_hi, 7 * P)

            def high(t, c, first=False):
                act.wait_ge(w_loaded[c], 16 * t + 16)
                if not first:
                    act.wait_ge(s.w_used, 4 * t + c - 3)
                act.activation(w_hi[:, c, :], w_raw[:, c, :], ACT.Copy).then_inc(s.w_high, 1)

            def highs_ahead(t, c):
                if c == 0:
                    high(t, 3)
                else:
                    high(t + 1, c - 1)

            for c in range(3):
                high(0, c, first=True)

            def tile_highs(t):
                for c in range(4):
                    if isinstance(t, int) and t == 0 and c == 0:
                        high(0, 3, first=True)
                    else:
                        highs_ahead(t, c)

            for t in range(CH):
                tile_highs(t)
                if t == 0:
                    act.wait_ge(s.va_stored, 16)
                    act.wait_ge(s.vb_stored, 16)
                act.wait_ge(s.w_used, 4 * t + 4)
                act.activation(mk[:, t, :], PROJ[t % 2][:, 0, 0:NMEM], ACT.Copy).then_inc(proj_free[t % 2], 1)
            with act.Fori(0, 2) as i:
                for e in range(2):
                    tile_highs(4 + 2 * i + e)
                    act.wait_ge(s.w_used, 4 * (5 + 2 * i + e))
                    act.activation(mv_stage[:, :], PROJ[e][:, 0, 0:NMEM], ACT.Copy).then_inc(s.stage_ready, 1)
                    act.wait_ge(s.v_turned, 2 * i + e + 1)
                    act.activation(mv[:, :, bass.ds(2 * i + e, 1), :].rearrange("p k o d -> p k (o d)"),
                                   PROJ[e][:, 0, 0:NMEM].rearrange("p (k d) -> p k d", k=2), ACT.Copy)\
                       .then_inc(proj_free[e], 1)

            def values(t, stage, dst, count):
                p = PROJ[t % 2]
                act.wait_ge(s.w_used, 4 * t + 4)
                act.activation(stage[:, :], wide(p), ACT.Copy).then_inc(s.stage_ready, 1)
                act.wait_ge(s.v_turned, count)
                act.activation(dst[:, :, :].rearrange("p k d -> p (k d)"), wide(p), ACT.Copy)\
                   .then_inc(proj_free[t % 2], 1)

            tile_highs(T_AK)
            act.wait_ge(s.w_used, 4 * T_AK + 4)
            act.activation(kz[0:CHUNK, 0, :], wide(PG)[0:CHUNK, :], ACT.Copy)
            act.activation(ak[:, :], wide(PG), ACT.Copy).then_inc(s.pg_free, 1)
            act.wait_ge(s.pg_free, T_AK // 2 + 1)
            act.dma_start(kz[CHUNK:P, 1, :], ak[0:CHUNK, :]).then_inc(s.kz_moved, 16)
            tile_highs(T_AV)
            values(T_AV, av_stage, av, 5)
            for e in range(2):
                t = T_IQ + e
                tile_highs(t)
                act.wait_ge(s.w_used, 4 * t + 4)
                act.activation(iq[:, e, :], wide(PROJ[e]), ACT.Copy).then_inc(proj_free[e], 1)
            tile_highs(T_IK)
            act.wait_ge(s.w_used, 4 * T_IK + 4)
            act.activation(ikz[0:CHUNK, 0, :], wide(PG)[0:CHUNK, :], ACT.Copy).then_inc(s.ikz_copied, 1)
            act.activation(iwT[CHUNK:IKW, :], wide(PG)[CHUNK:IKW, :], ACT.Copy).then_inc(s.pg_free, 1)
            act.wait_ge(s.ikz_copied, 1)
            act.dma_start(ikz[CHUNK:P, 1, :], ikz[0:CHUNK, 0, :]).then_inc(s.ikz_moved, 16)

            act.wait_ge(s.iw_turned, 1)
            for slot in range(8):
                for u in range(3 * slot, 3 * slot + 3):
                    b = 2 + u // 4
                    act.wait_ge(s.idx_ready, u + 1)
                    if u >= 2:
                        act.wait_ge(s.idx_added, u - 1)
                    src = wide(L if u % 2 == 0 else TO)
                    act.activation(relu_s[:, u % 2, 0:P * (b + 1)], src[:, 0:P * (b + 1)], ACT.Relu, scale=0.125)\
                       .then_inc(s.relu_ready, 1)
                    if u % 4 == 1 and b > 2:
                        store_scores(act, b - 1)
                if slot % 2 == 0:
                    highs_ahead(T_Q0, slot // 2)
            store_scores(act, 7)
            act.wait_ge(s.w_used, 4 * T_Q0 + 4)
            act.activation(q0[:, :], wide(PQ), ACT.Copy).then_inc(s.pq_free, 1)
            act.wait_ge(s.isc_st0, 48)
            act.wait_ge(s.isc_st1, 48)

            def gate_exp(m, t):
                act.wait_ge(s.w_used, 4 * t + 4)
                act.activation(sg[:, :], wide(PG), ACT.Exp, scale=-1.0).then_inc(s.gate_exp, 1)

            def probs(g, b, kind):
                act.wait_ge(s.neg_ready, g + 1)
                if kind == "A":
                    k0 = P if b == 0 else 0
                    for e in range(2):
                        v = SA[:, b % 3, e, k0:257]
                        last = act.activation(v, v, ACT.Exp, scale=A_SCALE, bias=neg[:, b, e:e + 1],
                                              accum_out=den[:, b, e:e + 1])
                elif kind == "C":
                    last = act.activation(SA[:, b % 3, 0, 0:NMEM], L[:, b % 2, 0:NMEM], ACT.Exp, scale=BC_SCALE,
                                          bias=neg[:, b, 0:1], accum_out=den[:, b, 0:1])
                else:
                    v = SB[:, b % 2, 0:P * (b + 1)]
                    last = act.activation(v, v, ACT.Exp, scale=BC_SCALE, bias=neg[:, b, 0:1],
                                          accum_out=den[:, b, 0:1])
                last.then_inc(s.probs_ready, 1)

            def turned_probs(g, b, kind):
                act.wait_ge(s.pt_ready, g + 1)
                a, z = (0, 256) if kind == "C" else (256 if b == 0 else 0, 512)
                act.activation(PT[:, a:z], T[:, a:z], ACT.Copy).then_inc(s.pt_copied, 1)

            def head_out(g, b):
                act.wait_ge(s.ot_ready, g + 1)
                act.activation(oT[:, P * b:P * b + P], O[:, 0:P], ACT.Copy).then_inc(s.ot_copied, 1)

            def y_row(dst, m):
                return dst[bass.ds(m, 1), :, :].rearrange("o p t -> (o p) t").bitcast(F32)

            def y_store(m):
                act.wait_ge(s.y_low, m + 1)
                act.dma_start(y_row(yhi_dram, m), yhi_s[:, :].bitcast(F32)).then_inc(s.y_free, 16)
                act.dma_start(y_row(ylo_dram, m), ylo_s[:, :].bitcast(F32)).then_inc(s.y_free, 16)

            def mix(m, kind, pair=None, width=0, first=False):
                for slot in range(17):
                    if slot == 3 and not first:
                        y_store(m - 1)
                    if slot == 0 and kind == "C":
                        act.activation(mk_now[:, :], mk[:, bass.ds(m, 1), :].rearrange("p o n -> p (o n)"), ACT.Copy)
                        act.activation(mv_now[:, :, :], mv[:, :, bass.ds(m, 1), :].rearrange("p k o d -> p k (o d)"),
                                       ACT.Copy).then_inc(s.memkv_ready, 1)
                    if 4 <= slot <= 11:
                        turned_probs(8 * m + slot - 4, slot - 4, kind)
                    if 5 <= slot <= 12:
                        head_out(8 * m + slot - 5, slot - 5)
                    if 1 <= slot <= 8:
                        probs(8 * m + slot - 1, slot - 1, kind)
                    if slot == 1 and pair is not None:
                        act.wait_ge(s.mask_done, pair + 1)
                        act.dma_start(mask_dram[pair, :, 0:width], mask_s[:, 0:width]).then_inc(s.mask_stored, 16)
                        act.dma_start(W[:, 0:width], isc_dram[pair, :, 0:width]).then_inc(s.W_loaded, 16)
                    if slot % 2 == 0 and slot < 16:
                        c = slot // 2
                        highs_ahead(T_LOOP + 2 * m + c // 4, c % 4)
                    if slot == 8:
                        gate_exp(m, T_LOOP + 2 * m)
                act.wait_ge(s.w_used, 4 * (T_LOOP + 2 * m + 2))
                act.activation(q0[:, :], wide(PQ), ACT.Copy).then_inc(s.pq_free, 1)

            act.wait_ge(s.kz_moved, 16)
            for m in range(4):
                mix(m, "C", pair=m // 2 if m % 2 == 0 else None, width=512, first=m == 0)
            act.wait_ge(s.zeroed, 3)
            act.activation(kz1[CHUNK:P, 1, :], ak[CHUNK:P, :], ACT.Copy).then_inc(s.kz1_copied, 1)
            act.dma_start(kz1[0:CHUNK, 0, :], ak[CHUNK:P, :]).then_inc(s.kz1_moved, 16)
            for lo, width in ((2, 768), (4, 1024)):
                with act.Fori(lo, lo + 2) as pair:
                    mix(2 * pair, "A", pair, width)
                    mix(2 * pair + 1, "A")

            act.wait_ge(s.mask_done, 7)
            act.dma_start(mask_dram[6, :, :], mask_s[:, :]).then_inc(s.mask_stored, 16)
            tile_highs(T_B)
            act.wait_ge(s.w_used, 4 * T_B + 4)
            act.activation(bk0[:, :], wide(PG), ACT.Copy).then_inc(s.pg_free, 1)
            tile_highs(T_B + 1)

            def stage_values(t):
                act.wait_ge(s.w_used, 4 * t + 4)
                act.activation(bv_stage[:, :], wide(PQ), ACT.Copy).then_inc(s.stage_ready, 1)

            stage_values(T_B + 1)
            act.wait_ge(s.mask_stored, 16 * 7)

            def head(h, pos):
                m = 12 + h
                last = h == BH - 1

                def load_mask(b):
                    src = mask_dram[max(0, b - 1), :, P:3 * P] if b == 1 else mask_dram[max(0, b - 1), :, 0:P * (b + 1)]
                    act.dma_start(maskB[:, b % 2, 0:P * (b + 1)], src).then_inc((s.mask_ld0, s.mask_ld1)[b % 2], 16)

                act.wait_ge(s.S_max, 8 * m)
                if h == 0:
                    act.wait_ge(s.tb_built, 16)
                act.dma_start(biasB[:, :], tb_dram[h]).then_inc(s.biasB_loaded, 16)
                load_mask(0)
                load_mask(1)
                for slot in range(25 if last else 33):
                    if slot == 3:
                        y_store(m - 1)
                    if slot == 2:
                        act.wait_ge(s.v_turned, 6 + h)
                        act.activation((bv0, bv1)[h % 2][:, :, :].rearrange("p k d -> p (k d)"), wide(PQ), ACT.Copy)\
                           .then_inc(s.pq_free, 1)
                    for b in range(NB):
                        two = b >= 4
                        if slot == pos[b] + 4:
                            act.wait_ge(s.bpt_ready, 12 * h + (2 * b - 4 if two else b) + 1)
                            n = P * min(4, b + 1)
                            act.activation(PT[:, 0:n], T[:, 0:n], ACT.Copy).then_inc(s.bpt_copied, 1)
                        if slot == pos[b] + 5 and two:
                            act.wait_ge(s.bpt_ready, 12 * h + 2 * b - 4 + 2)
                            n = P * (b - 3)
                            act.activation(PT[:, 512:512 + n], T[:, 0:n], ACT.Copy).then_inc(s.bpt_copied, 1)
                        if slot == pos[b] + 6:
                            head_out(8 * m + b, b)
                        if slot == pos[b] + 1:
                            probs(8 * m + b, b, "B")
                            if b + 2 < NB:
                                load_mask(b + 2)
                    if last and slot == 8:
                        gate_exp(m, T_BHEAD + 4 * h)
                        act.activation(gate_last[:, :], wide(PG), ACT.Copy).then_inc(s.pg_free, 1)
                    if slot % 2 == 0 and slot < (8 if last else 32):
                        c = slot // 2
                        highs_ahead(T_BHEAD + 4 * h + c // 4, c % 4)
                    if last and 8 <= slot < 24:
                        k = slot - 8 + 3
                        high(T_ALL + k // 4, k % 4)
                    if slot == 8 and not last:
                        gate_exp(m, T_BHEAD + 4 * h)
                    if last and slot == 15:
                        y_last(0)
                    if slot == 16 and not last:
                        act.wait_ge(s.w_used, 4 * (T_BHEAD + 4 * h + 2))
                        act.activation((q0, q1)[(h + 1) % 2][:, :], wide(PQ), ACT.Copy).then_inc(s.pq_free, 1)
                    if slot == 24 and not last:
                        act.wait_ge(s.w_used, 4 * (T_BHEAD + 4 * h + 3))
                        act.activation((bk0, bk1)[(h + 1) % 2][:, :], wide(PG), ACT.Copy).then_inc(s.pg_free, 1)
                if last:
                    y_last(1)
                else:
                    stage_values(T_BHEAD + 4 * h + 3)

            def y_last(half):
                act.wait_ge(s.yf_ready, 16 + half)
                cols = slice(512 * half, 512 * half + 512)
                act.activation(y_hi[:, 15, cols], yf[:, cols], ACT.Copy).then_inc(s.y_high, 1)

            for h in range(BH - 1):
                head(h, B_POS)
            head(BH - 1, B_LAST)

            def roots(half):
                act.wait_ge(s.fin_ms, half + 1)
                act.activation(rms[:, 0:4], ms[:, 0:4], ACT.Sqrt).then_inc(s.fin_rt, 1)

            def store_out(half):
                for j in range(4):
                    act.wait_ge(s.fin_done, 4 * half + j + 1)
                    act.dma_start(out_v[4 * half + j], h_res[:, j, :]).then_inc(s.out_stored, 16)

            def squares(q, n):
                for j in range(4):
                    act.wait_ge(s.out_free, 8 + 4 * q + j + 1)
                    act.activation(sq_junk[:, 512 * j:512 * j + 512], h_res[:, j, bass.ds(n * 512, 512)], ACT.Square,
                                   accum_out=ssq[:, bass.ds(4 * j + n, 1)]).then_inc(s.sq_out, 1)

            def out_n(q, n, first=False, last=False):
                for k in range(3, 16 if last else 19):
                    high(T_ALL + 4 * q + k // 4, k % 4)
                    if k == 7:
                        squares(q - 1, 3 if first else n - 1)
                    if k == 8 and first:
                        roots(0)
                    if k == 12 and first:
                        store_out(0)

            with act.Fori(1, 4) as n:
                out_n(n, n)
            out_n(4, 0, first=True)
            with act.Fori(1, 3) as n:
                out_n(4 + n, n)
            out_n(7, 3, last=True)
            squares(7, 3)
            roots(1)
            store_out(1)
            act.wait_ge(s.out_stored, 16 * NB)

        @block.vector
        def _(dve):
            def carry():
                dve.memset(pace[:, :], 0.0)

            dve.memset(masked[:, :], MASKED).then_inc(s.ta_fill, 1)
            dve.wait_ge(s.rb_loaded, 32)
            dve.tensor_scalar(rbA[:, :], rbA[:, :], 1 / A_SCALE, None, ALU.mult)
            dve.tensor_scalar(rbB[:, :], rbB[:, :], 1 / BC_SCALE, None, ALU.mult).then_inc(s.rb_scaled, 1)
            dve.wait_ge(s.rb_scaled, 1)
            dve.memset(VA[:, VA_LEN - 1:VA_LEN], 0.0)
            dve.memset(VB[:, VB_LEN - 1:VB_LEN], 0.0)
            for first, last, r in bucket_edges():
                for V, rb, heads, zero in ((VA, rbA, AH, 255), (VB, rbB, BH, SEQ - 1)):
                    a, z = max(first + zero, 0), last + zero
                    if z > a:
                        ins = dve.tensor_copy(V[:, a:z], rb[:, r:r + 1].to_broadcast([heads, z - a]))
            ins.then_inc(s.v_built, 1)
            dve.memset(mask_s[CHUNK:P, :], 0.0)
            dve.memset(mask_s[0:CHUNK, 0:64], 0.0)
            dve.memset(mask_s[0:CHUNK, 64:128], MASKED)
            dve.memset(mask_s[0:CHUNK, 128:320], 0.0)
            dve.memset(mask_s[0:CHUNK, 320:384], MASKED)
            dve.memset(mask_s[0:CHUNK, 384:SEQ], 0.0).then_inc(s.mask_done, 1)

            def normed(j, e, raw, g):
                dve.wait_ge(s.sq_done, j + 1)
                dve.tensor_scalar(ms[:, e:e + 1], ssq[:, e:e + 1], 1.0 / D, EPS, ALU.mult, ALU.add)\
                   .then_inc(s.ms_done, 1)
                dve.wait_ge(s.rt_done, j + 1)
                dve.reciprocal(rstd[:, e:e + 1], rms[:, e:e + 1]).then_inc(s.rstd_done, 1)
                refine(slice(e, e + 1), 4 * j)
                dve.scalar_tensor_tensor(out=raw, in0=raw, scalar=rstd[:, e:e + 1], in1=g, op0=ALU.mult,
                                         op1=ALU.mult).then_inc(s.normed, 1)

            def refine(cols, done):
                dve.wait_ge(s.rstd_done, done + 1)
                dve.tensor_tensor(rfix[:, cols], rstd[:, cols], rstd[:, cols], ALU.mult).then_inc(s.rstd_done, 1)
                dve.wait_ge(s.rstd_done, done + 2)
                carry()
                dve.scalar_tensor_tensor(out=rfix[:, cols], in0=rfix[:, cols], scalar=-0.5, in1=ms[:, cols],
                                         op0=ALU.mult, op1=ALU.mult).then_inc(s.rstd_done, 1)
                dve.wait_ge(s.rstd_done, done + 3)
                carry()
                dve.scalar_tensor_tensor(out=rstd[:, cols], in0=rfix[:, cols], scalar=1.5, in1=rstd[:, cols],
                                         op0=ALU.add, op1=ALU.mult).then_inc(s.rstd_done, 1)
                dve.wait_ge(s.rstd_done, done + 4)

            def norm_low(j, e, hi, lo, col):
                for kg in range(4):
                    dve.wait_ge(s.tr_hi, 4 * j + kg + 1)
                    dve.tensor_tensor(lo[:, 4 * kg:4 * kg + 4, bass.ds(col, P)],
                                      bank[4 * e + kg].rearrange("p (k t) -> p k t", k=4),
                                      hi[:, 4 * kg:4 * kg + 4, bass.ds(col, P)].bitcast(F32), ALU.subtract)\
                       .then_inc(s.tr_lo, 1)

            dve.wait_ge(s.g_loaded, 32)
            normed(0, 0, mem_raw[:, 0, :], gmem_b[:, :])
            normed(1, 1, mem_raw[:, 1, :], gmem_b[:, :])
            norm_low(0, 0, memT_hi, memT_lo, 0)
            normed(2, 0, x_raw[:, 0, :], gx_b[:, :])
            norm_low(1, 1, memT_hi, memT_lo, P)
            with dve.Fori(0, 3) as i:
                normed(2 * i + 3, 1, x_raw[:, 1, :], gx_b[:, :])
                norm_low(2 * i + 2, 0, hn_hi, hn_lo, 2 * P * i)
                normed(2 * i + 4, 0, x_raw[:, 0, :], gx_b[:, :])
                norm_low(2 * i + 3, 1, hn_hi, hn_lo, 2 * P * i + P)
            normed(9, 1, x_raw[:, 1, :], gx_b[:, :])
            norm_low(8, 0, hn_hi, hn_lo, 6 * P)
            norm_low(9, 1, hn_hi, hn_lo, 7 * P)

            dve.wait_ge(s.const_loaded, 16)
            dve.tensor_scalar(sinks8[:, :], sinks8[:, :], 1 / A_SCALE, None, ALU.mult).then_inc(s.sink_ready, 1)

            dve.wait_ge(s.turned, 40)
            dve.memset(kz[CHUNK:P, 0, :], 0.0)
            dve.memset(kz[0:CHUNK, 1, :], 0.0).then_inc(s.zeroed, 1)
            dve.wait_ge(s.w_used, 4 * MEM_TILES)
            dve.memset(ikz[CHUNK:P, 0, :], 0.0)
            dve.memset(ikz[0:CHUNK, 1, :], 0.0).then_inc(s.zeroed, 1)

            dve.wait_ge(s.iw_turned, 1)
            dve.tensor_scalar(iw[:, :, :].rearrange("p b h -> p (b h)"), T[:, 0:4 * NB], 0.5, None, ALU.mult)\
               .then_inc(s.iw_ready, 1)
            dve.wait_ge(s.iw_ready, 1)
            for u in range(24):
                b, h = 2 + u // 4, u % 4
                w = P * (b + 1)
                dve.wait_ge(s.relu_ready, u + 1)
                if h == 0:
                    if b >= 4:
                        dve.wait_ge(isc_stored[b % 2], 16 * ((b - 2) // 2))
                    dve.tensor_scalar(acc[:, b % 2, 0:w], relu_s[:, u % 2, 0:w], iw[:, b, 0:1], 0.0,
                                      ALU.mult, ALU.add).then_inc(s.idx_added, 1)
                else:
                    dve.wait_ge(s.idx_added, u)
                    dve.scalar_tensor_tensor(out=acc[:, b % 2, 0:w], in0=relu_s[:, u % 2, 0:w],
                                             scalar=iw[:, b, h:h + 1], in1=acc[:, b % 2, 0:w],
                                             op0=ALU.mult, op1=ALU.add).then_inc(s.idx_added, 1)
                if h == 3:
                    dve.wait_ge(s.idx_added, u + 1)
                    if isc_width[b - 2] > w:
                        dve.memset(acc[:, b % 2, w:isc_width[b - 2]], MASKED)
                    if b == NB - 1:
                        dve.memset(acc[0:CHUNK, b % 2, w - CHUNK:w - 32], MASKED).then_inc(s.y_free, 32)
                        dve.memset(acc[0:CHUNK, b % 2, w - 32:w], MASKED).then_inc(s.isc_done, 1)
                    else:
                        dve.memset(acc[0:CHUNK, b % 2, w - CHUNK:w], MASKED).then_inc(s.isc_done, 1)

            def choose(pair, n, width):
                if n == 0:
                    dve.wait_ge(s.W_loaded, 16 * pair + 16)
                else:
                    dve.wait_ge(s.top_out, 32 * pair + n)
                carry()
                dve.max(top8[:, :], W[:, 0:width]).then_inc(s.top_max, 1)
                dve.wait_ge(s.top_max, 32 * pair + n + 1)
                carry()
                dve.match_replace(W[:, 0:width], top8[:, :], W[:, 0:width], TAKEN).then_inc(s.top_out, 1)
                if n == ROUNDS - 1:
                    dve.wait_ge(s.top_out, 32 * pair + ROUNDS)
                    dve.wait_ge(s.mask_stored, 16 * pair + 16)
                    dve.tensor_scalar(mask_s[:, 0:width], W[:, 0:width], BELOW_MASKED, MASKED, ALU.is_gt, ALU.mult)\
                       .then_inc(s.mask_done, 1)

            ROUNDS_AT = [[max(0, slot - 2) for slot in range(17)]]
            ROUNDS_AT.append([13 + slot + sum(slot > x for x in (5, 7, 11)) for slot in range(17)])
            ROUNDS_AT[0][16] = 13
            ROUNDS_AT[0] = [min(n, 13) for n in ROUNDS_AT[0]]
            assert ROUNDS_AT[0][16] == ROUNDS_AT[1][0] and ROUNDS_AT[1][16] == ROUNDS

            def negated(g, b, n, scale):
                dve.wait_ge(s.S_max, g + 1)
                dve.tensor_scalar(neg[:, b, 0:n], mx[:, b, 0:n], -scale, None, ALU.mult).then_inc(s.neg_ready, 1)

            def maxima(m, b, kind):
                g = 8 * m + b
                dve.wait_ge(s.logits_ready, g + 1)
                if kind == "C":
                    dve.tensor_reduce(mx[:, b, 0:1], L[:, b % 2, 0:NMEM], AX.X, ALU.max).then_inc(s.S_max, 1)
                    negated(g, b, 1, BC_SCALE)
                else:
                    k0 = P if b == 0 else 0
                    if b == 0:
                        dve.wait_ge(s.biasA_loaded, 16 * (m - 3))
                    dve.tensor_copy(SA[:, b % 3, :, 256:257].rearrange("p e o -> p (e o)"), sink_now[:, :])
                    for e in range(2):
                        last = dve.tensor_tensor_reduce(SA[:, b % 3, e, k0:256], L[:, b % 2, 256 * e + k0:256 * e + 256],
                                                        biasA[:, e, k0:256], 1.0, sink_now[:, e:e + 1], ALU.add,
                                                        ALU.max, mx[:, b, e:e + 1])
                    last.then_inc(s.S_max, 1)
                    negated(g, b, 2, A_SCALE)

            def reciprocals(g, b, n):
                dve.wait_ge(s.probs_ready, g + 1)
                dve.reciprocal(rec[:, b, 0:n], den[:, b, 0:n]).then_inc(s.recip_ready, 1)

            def silu(m, part, gate=wide(PG), done=s.pg_free):
                if part == 0:
                    dve.wait_ge(s.gate_exp, m + 1)
                    dve.tensor_scalar(sg[:, :], sg[:, :], 1.0, None, ALU.add).then_inc(s.gate_step, 1)
                elif part < 3:
                    if part == 1:
                        dve.wait_ge(s.gate_step, 3 * m + 1)
                    v = sg[:, 512 * part - 512:512 * part]
                    dve.reciprocal(v, v).then_inc(s.gate_step, 1)
                else:
                    dve.wait_ge(s.gate_step, 3 * m + 3)
                    dve.tensor_tensor(sg[:, :], gate, sg[:, :], ALU.mult).then_inc(done, 1)

            def mix(m, kind, pair, second, width):
                if kind == "A":
                    dve.wait_ge(s.S_max, 8 * m)
                    dve.tensor_copy(sink_now[:, :], sinks8[:, bass.ds(2 * (m - 4), 2)]).then_inc(s.sink_ready, 1)
                    dve.wait_ge(s.sink_ready, m - 2)
                for slot in range(16):
                    if slot < 8:
                        maxima(m, slot, kind)
                    for n in range(ROUNDS_AT[second][slot], ROUNDS_AT[second][slot + 1]):
                        choose(pair, n, width)
                    if 1 <= slot <= 8:
                        reciprocals(8 * m + slot - 1, slot - 1, 2 if kind == "A" else 1)
                    if 9 <= slot <= 12:
                        silu(m, slot - 9)

            for kind, lo, width in (("C", 0, 512), ("A", 2, 768), ("A", 4, 1024)):
                if lo == 2:
                    dve.wait_ge(s.sink_ready, 1)
                    dve.wait_ge(s.memkv_ready, 4)
                    dve.memset(kz1[CHUNK:P, 0, :], 0.0)
                    dve.memset(kz1[0:CHUNK, 1, :], 0.0).then_inc(s.zeroed, 1)
                with dve.Fori(lo, lo + 2) as pair:
                    mix(2 * pair, kind, pair, False, width)
                    mix(2 * pair + 1, kind, pair, True, width)

            def head(h, pos):
                m = 12 + h
                for slot in range(32):
                    if slot in pos:
                        b = pos.index(slot)
                        g, w = 8 * m + b, P * (b + 1)
                        dve.wait_ge(s.logits_ready, g + 1)
                        if b == 0:
                            dve.wait_ge(s.biasB_loaded, 16 * h + 16)
                        dve.tensor_tensor(SB[:, b % 2, 0:w], wide(L)[:, 0:w], biasB[:, SEQ - w:SEQ], ALU.add)\
                           .then_inc(s.S_biased, 1)
                        dve.wait_ge(s.S_biased, 8 * h + b + 1)
                        dve.wait_ge((s.mask_ld0, s.mask_ld1)[b % 2], 64 * h + 16 * (b // 2) + 16)
                        carry()
                        dve.tensor_tensor_reduce(SB[:, b % 2, 0:w], SB[:, b % 2, 0:w], maskB[:, b % 2, 0:w], 1.0,
                                                 MASKED, ALU.add, ALU.max, mx[:, b, 0:1]).then_inc(s.S_max, 1)
                        negated(g, b, 1, BC_SCALE)
                    if slot - 1 in pos:
                        b = pos.index(slot - 1)
                        reciprocals(8 * m + b, b, 1)
                    if 9 <= slot <= 12:
                        if pos is B_POS:
                            silu(m, slot - 9)
                        else:
                            silu(m, slot - 9, gate=gate_last[:, :], done=s.sg_ready)

            with dve.Fori(0, BH - 1) as h:
                head(h, B_POS)
            head(BH - 1, B_LAST)

            dve.wait_ge(s.ot_copied, 8 * 16)
            dve.memset(pace[:, :], 0.0).then_inc(s.out_free, 8)
            dve.wait_ge(s.y_low, 17)
            for half in range(2):
                if half == 1:
                    dve.wait_ge(s.out_stored, 64)
                with dve.Fori(0, 2) as i:
                    for e in range(2):
                        n = 2 * i + e
                        for j in range(4):
                            if j < 3:
                                dve.wait_ge(s.out_done, 12 * half + 3 * n + j + 1)
                            else:
                                dve.wait_ge(s.w_used, N_OUT + 64 * half + 16 * n + 16)
                            dve.wait_ge(xres_loaded[j], 64 * half + 16 * n + 16)
                            dve.tensor_tensor(h_res[:, j, bass.ds(n * 512, 512)], bank[4 * e + j], x_res[:, j, :],
                                              ALU.add).then_inc(s.out_free, 1)
                dve.wait_ge(s.sq_out, 16 * half + 16)
                dve.tensor_reduce(ssum[:, 0:4], ssq[:, :].rearrange("p (j n) -> p j n", j=4), AX.X, ALU.add)\
                   .then_inc(s.fin_sum, 1)
                dve.wait_ge(s.fin_sum, half + 1)
                dve.tensor_scalar(ms[:, 0:4], ssum[:, 0:4], 1.0 / D, EPS, ALU.mult, ALU.add).then_inc(s.fin_ms, 1)
                dve.wait_ge(s.fin_rt, half + 1)
                dve.reciprocal(rstd[:, 0:4], rms[:, 0:4]).then_inc(s.rstd_done, 1)
                refine(slice(0, 4), 40 + 4 * half)
                dve.wait_ge(s.gf_loaded, 16)
                for j in range(4):
                    dve.scalar_tensor_tensor(out=h_res[:, j, :], in0=h_res[:, j, :], scalar=rstd[:, j:j + 1],
                                             in1=gf_b[:, :], op0=ALU.mult, op1=ALU.mult).then_inc(s.fin_done, 1)

        @block.tensor
        def _(pe):
            def turn(u, b, srcs, inc):
                for i, src in enumerate(srcs):
                    last = pe.transpose(b[:, P * i:P * i + P], src, ident[:, :])
                last.then_inc(inc, 1)

            def norm_turn(j, e, raw, first=False):
                pe.wait_ge(s.normed, j + 1)
                for kg in range(4):
                    if not first:
                        pe.wait_ge(s.tr_lo, 4 * j + kg - 7)
                    turn(0, bank[4 * e + kg], [raw[:, P * (4 * kg + i):P * (4 * kg + i) + P] for i in range(4)], s.turned)

            pe.wait_ge(s.ident_ready, 1)
            norm_turn(0, 0, mem_raw[:, 0, :], first=True)
            norm_turn(1, 1, mem_raw[:, 1, :], first=True)
            with pe.Fori(1, 5) as i:
                norm_turn(2 * i, 0, x_raw[:, 0, :])
                norm_turn(2 * i + 1, 1, x_raw[:, 1, :])
            pe.wait_ge(s.tr_lo, 40)

            def three(dst, hi, lo, rhs_hi, rhs_lo, start, stop):
                for d, r in zip(dst, rhs_hi):
                    pe.matmul(d, hi, r, start=start, stop=False)
                for d, r in zip(dst, rhs_lo):
                    pe.matmul(d, hi, r, start=False, stop=False)
                for d, r in zip(dst, rhs_hi):
                    last = pe.matmul(d, lo, r, start=False, stop=stop)
                return last

            def begin(t, e, half_t):
                if not (isinstance(t, int) and t < 2):
                    pe.wait_ge(proj_free[e], half_t)

            def mem_tile(t, e, half_t):
                begin(t, e, half_t)
                for c in range(4):
                    pe.wait_ge(s.w_low, 4 * t + c + 1)
                    for i in range(4):
                        k = 4 * c + i
                        last = three([PROJ[e][:, 0, 0:NMEM]], w_hi[:, c, P * i:P * i + P], w_lo[:, c, P * i:P * i + P],
                                     [memT_hi[:, k, :]], [memT_lo[:, k, :]], k == 0, k == 15)
                    last.then_inc(s.w_used, 1)

            def slot_of(t, e, half_t, j, width=P):
                if j == 0:
                    begin(t, e, half_t)
                c = j // 2
                if j % 2 == 0:
                    pe.wait_ge(s.w_low, 4 * t + c + 1)
                for k in (2 * j, 2 * j + 1):
                    i = k % 4
                    last = three([PROJ[e][0:width, half, :] for half in range(2)],
                                 w_hi[:, c, P * i:P * i + width], w_lo[:, c, P * i:P * i + width],
                                 [hn_hi[:, k, 512 * half:512 * half + 512] for half in range(2)],
                                 [hn_lo[:, k, 512 * half:512 * half + 512] for half in range(2)], k == 0, k == 15)
                if j % 2 == 1:
                    last.then_inc(s.w_used, 1)

            def turn_values(e, stage, count, n=NB):
                pe.wait_ge(s.stage_ready, count)
                p = wide(PROJ[e])
                for i in range(n):
                    last = pe.transpose(p[:, P * i:P * i + P], stage[:, P * i:P * i + P], ident[:, :])
                last.then_inc(s.v_turned, 1)

            for t in range(CH):
                mem_tile(t, t % 2, t // 2)
            with pe.Fori(2, 4) as i:
                for e in range(2):
                    mem_tile(2 * i + e, e, i)
                    turn_values(e, mv_stage, 2 * i + e - 3, n=2)

            for t in (T_AK, T_AV, T_IQ, T_IQ + 1):
                for j in range(8):
                    slot_of(t, t % 2, t // 2, j)
                if t == T_AV:
                    turn_values(1, av_stage, 5)
            for j in range(8):
                slot_of(T_IK, 0, T_IK // 2, j, width=P)
            pe.wait_ge(s.pg_free, T_IK // 2 + 1)
            for b in range(NB):
                last = pe.transpose(T[:, 4 * b:4 * b + 4], iwT[CHUNK:IKW, P * b:P * b + P], ident[CHUNK:IKW, CHUNK:IKW])
            last.then_inc(s.iw_turned, 1)
            for j in range(8):
                slot_of(T_Q0, 1, T_Q0 // 2, j)
                if j == 0:
                    pe.wait_ge(s.ikz_copied, 1)
                    pe.wait_ge(s.ikz_moved, 16)
                    pe.wait_ge(s.zeroed, 2)
                for u in range(3 * j, 3 * j + 3):
                    b, h = 2 + u // 4, u % 4
                    if u == 1:
                        pe.wait_ge(s.iw_ready, 1)
                    if u >= 2:
                        pe.wait_ge(s.relu_ready, u - 1)
                    dst = wide(L if u % 2 == 0 else TO)
                    for a in range(0, P * (b + 1), 512):
                        z = min(a + 512, P * (b + 1))
                        last = pe.matmul(dst[:, a:z], iq[:, h // 2, P * b:P * b + P], ikz[:, h % 2, a:z],
                                         start=True, stop=True)
                    last.then_inc(s.idx_ready, 1)

            def logits(m, b, kind, group):
                if kind == "C":
                    if b == 0:
                        pe.wait_ge(s.pq_free, m + 7)
                        pe.wait_ge(s.memkv_ready, m + 1)
                    if b >= 2:
                        pe.wait_ge(s.probs_ready, 8 * m + b - 1)
                    last = pe.matmul(L[:, b % 2, 0:NMEM], q0[:, P * b:P * b + P], mk_now[:, :], start=True, stop=True)
                else:
                    if b == 0:
                        pe.wait_ge(s.pq_free, m + 7)
                    if b >= 2:
                        pe.wait_ge(s.S_max, 8 * m + b - 1)
                    k0 = P if b == 0 else 0
                    a = P * (b - 1) + k0
                    dst = L[:, b % 2, :].rearrange("p (e k) -> p e k", e=2)[:, :, k0:256]
                    last = pe.matmul(dst, q0[:, P * b:P * b + P], (kz, kz1)[group][:, :, a:P * (b + 1)], start=True, stop=True)
                last.then_inc(s.logits_ready, 1)

            def turn_probs(m, b, kind):
                pe.wait_ge(s.norm_ready, 8 * m + b + 1)
                for kt in range(1 if kind == "A" and b == 0 else 0, 2):
                    for e in range(2 if kind == "A" else 1):
                        i = 2 * kt + e if kind == "A" else kt
                        last = pe.transpose(T[:, P * i:P * i + P], SA[:, b % 3, e, P * kt:P * kt + P], ident[:, :])
                last.then_inc(s.pt_ready, 1)

            def weigh(m, b, kind, group):
                pe.wait_ge(s.pt_copied, 8 * m + b + 1)
                if b >= 1:
                    pe.wait_ge(s.ot_copied, 8 * m + b)
                if kind == "C":
                    for kt in range(2):
                        last = pe.matmul(O[:, 0:P], mv_now[:, kt, :], PT[:, P * kt:P * kt + P], start=kt == 0, stop=kt == 1)
                else:
                    kts = (1,) if b == 0 else (0, 1)
                    for e in range(2):
                        for kt in kts:
                            i = 2 * kt + e
                            last = pe.matmul(O[CHUNK * e:CHUNK * e + CHUNK, 0:P],
                                             av[:, b - 1 + kt, CHUNK * group:CHUNK * group + CHUNK],
                                             PT[:, P * i:P * i + P], start=kt == kts[0], stop=kt == 1)
                last.then_inc(s.ot_ready, 1)

            def mix(m, kind, group):
                for slot in range(16):
                    t = T_LOOP + 2 * m + slot // 8
                    slot_of(t, slot // 8, m + 7, slot % 8)
                    if 4 <= slot <= 11:
                        weigh(m, slot - 4, kind, group)
                    if 3 <= slot <= 10:
                        turn_probs(m, slot - 3, kind)
                    if slot <= 7:
                        logits(m, slot, kind, group)

            with pe.Fori(0, 4) as m:
                mix(m, "C", 0)
            pe.wait_ge(s.kz_moved, 16)
            pe.wait_ge(s.zeroed, 1)
            with pe.Fori(4, 8) as m:
                mix(m, "A", 0)
            pe.wait_ge(s.kz1_copied, 1)
            pe.wait_ge(s.kz1_moved, 16)
            with pe.Fori(8, 12) as m:
                mix(m, "A", 1)

            for t in (T_B, T_B + 1):
                for j in range(8):
                    slot_of(t, t % 2, t // 2, j)

            def out_step(q, e, half, k):
                if half == 0 and q == 0:
                    if k < 15:
                        pe.wait_ge(y_loaded[k], 32)
                    else:
                        pe.wait_ge(s.y_low, 16)
                pe.wait_ge(s.w_low, N_OUT + 16 * q + k + 1)
                c = k % 4
                for j in range(4):
                    dst = bank[4 * e + j]
                    cols = slice(512 * half + P * j, 512 * half + P * j + P)
                    pe.matmul(dst, y_hi[:, k, cols], w_hi[:, c, :], start=k == 0, stop=False)
                    pe.matmul(dst, y_hi[:, k, cols], w_lo[:, c, :], start=False, stop=False)
                    last = pe.matmul(dst, y_lo[:, k, cols], w_hi[:, c, :], start=False, stop=k == 15)
                    if k == 15 and j < 3:
                        last.then_inc(s.out_done, 1)
                last.then_inc(s.w_used, 1)

            def head(h, pos):
                m = 12 + h
                q, bk, bv = (q0, q1)[h % 2], (bk0, bk1)[h % 2], (bv0, bv1)[h % 2]
                for slot in range(24 if h == BH - 1 else 32):
                    if h < BH - 1 or slot < 8:
                        t = T_BHEAD + 4 * h + slot // 8
                        slot_of(t, t % 2, t // 2, slot % 8)
                    if slot == 1:
                        turn_values(1, bv_stage, 6 + h)
                    for b in range(NB):
                        if slot == pos[b] + 5:
                            pe.wait_ge(s.bpt_copied, 12 * h + (2 * b - 2 if b >= 4 else b + 1))
                            if b >= 1:
                                pe.wait_ge(s.ot_copied, 8 * m + b)
                            else:
                                pe.wait_ge(s.pq_free, 20 + 2 * h)
                            for kt in range(b + 1):
                                last = pe.matmul(O[:, 0:P], bv[:, kt, :], PT[:, P * kt:P * kt + P], start=kt == 0, stop=kt == b)
                            last.then_inc(s.ot_ready, 1)
                    for b in range(4, NB):
                        if slot == pos[b] + 4:
                            pe.wait_ge(s.bpt_copied, 12 * h + 2 * b - 3)
                            for kt in range(4, b + 1):
                                last = pe.transpose(T[:, P * (kt - 4):P * (kt - 3)], SB[:, b % 2, P * kt:P * kt + P], ident[:, :])
                            last.then_inc(s.bpt_ready, 1)
                    for b in range(NB):
                        if slot == pos[b] + 3:
                            pe.wait_ge(s.norm_ready, 8 * m + b + 1)
                            for kt in range(min(4, b + 1)):
                                last = pe.transpose(T[:, P * kt:P * kt + P], SB[:, b % 2, P * kt:P * kt + P], ident[:, :])
                            last.then_inc(s.bpt_ready, 1)
                    if slot in pos:
                        b = pos.index(slot)
                        if b == 0:
                            pe.wait_ge(s.pq_free, 19 if h == 0 else 19 + 2 * h)
                            pe.wait_ge(s.pg_free, 20 + 2 * h)
                        else:
                            pe.wait_ge(s.S_biased, 8 * h + b)
                        for a in range(0, P * (b + 1), 512):
                            z = min(a + 512, P * (b + 1))
                            last = pe.matmul(wide(L)[:, a:z], q[:, P * b:P * b + P], bk[:, a:z], start=True, stop=True)
                        last.then_inc(s.logits_ready, 1)
                    if h == BH - 1 and slot >= 8:
                        if slot == 8:
                            pe.wait_ge(s.pg_free, 27)
                        out_step(0, 0, 0, slot - 8)

            for h in range(BH - 1):
                head(h, B_POS)
            head(BH - 1, B_LAST)

            def out_tile(q, e, half):
                pe.wait_ge(s.out_free, 4 * q + 4)
                for k in range(16):
                    out_step(q, e, half, k)

            for q in range(1, 4):
                out_tile(q, q % 2, 0)
            for k in range(15):
                pe.wait_ge(y_loaded[k], 64)
            pe.wait_ge(s.y_low, 17)
            with pe.Fori(2, 4) as i:
                for e in range(2):
                    out_tile(2 * i + e, e, 1)


_INS = ["x", "mem", "g_norm", "w_in", "sinks", "rel_bias", "g_mem", "w_mem_kv", "w_out", "g_final"]
_OUTS = [((1, SEQ, D), "float32")]


def kernel(**inputs):
    import numpy as _np
    import concourse.bacc as _bacc
    from concourse import mybir as _mybir
    from concourse.bass_utils import run_bass_kernel_spmd as _run

    nc = _bacc.Bacc("TRN2", target_bir_lowering=False, num_devices=1, dynamic_dma_scratch_size=256)
    arrays, args = {}, []
    for name in _INS:
        a = _np.ascontiguousarray(inputs[name])
        arrays[f"in_{name}_dram"] = a
        args.append(nc.dram_tensor(f"in_{name}_dram", a.shape, _mybir.dt.from_np(a.dtype), kind="ExternalInput").ap())
    for i, (shape, dtype) in enumerate(_OUTS):
        dt = _mybir.dt.from_np(_np.dtype(dtype))
        args.append(nc.dram_tensor(f"out_{i}_dram", shape, dt, kind="ExternalOutput").ap())
    hybrid_layer(nc, *args)
    r = _run(nc, [arrays], core_ids=[0])
    got = tuple(r.results[0][f"out_{i}_dram"] for i in range(len(_OUTS)))
    return got[0]
```

```python
import math
from contextlib import ExitStack

import concourse.bass as bass
from concourse import mybir

F32 = mybir.dt.float32
F32R = mybir.dt.float32r
BF16 = mybir.dt.bfloat16
ALU = mybir.AluOpType
ACT = mybir.ActivationFunctionType
AX = mybir.AxisListType

P = 128
SEQ, D = 1024, 2048
KT = D // P
NB = SEQ // P
NMEM = 256
EPS = 1e-6
CHUNK = 64
TOPK = 256
ROUNDS = TOPK // 8
NBUCKET, MAXDIST = 32, 1024
AH, BH, CH = 16, 4, 4
A_SCALE = 64 ** -0.5
BC_SCALE = 128 ** -0.5
MASKED = -3.0e38
TAKEN = -3.3e38
BELOW_MASKED = -3.2e38

C_AQ, C_AK, C_AV = 0, 1024, 1152
C_BQ, C_BK, C_BV = 1280, 1792, 2304
C_IQ, C_IK = 2816, 3072
C_CQ, C_GATE = 3140, 3652
IKW = 68

MEM_TILES = 8
T_AK, T_AV, T_IQ, T_IK, T_Q0 = 8, 9, 10, 12, 13
T_LOOP = 14
T_B = T_LOOP + 24
T_BHEAD = T_B + 2
T_ALL = T_BHEAD + 13
N_OUT = 4 * T_ALL
N_TAIL = N_OUT + 96
UNITS_AT = (0, 4, 4, 4, 3, 3, 3, 3)
B_POS = [0, 3, 6, 10, 14, 18, 22, 26]
SHIFT = {"C": 0, "A": 1}
B_LAST = [0, 2, 4, 6, 9, 12, 15, 18]


def bucket_edges():
    half, exact = NBUCKET // 2, NBUCKET // 4

    def bucket(rel):
        n = abs(rel)
        if n < exact:
            b = n
        else:
            b = min(half - 1, exact + int(math.log(n / exact) / math.log(MAXDIST / exact) * (half - exact)))
        return b + (half if rel > 0 else 0)

    out, first = [], -(SEQ - 1)
    for rel in range(-(SEQ - 1) + 1, P + 1):
        if rel == P or bucket(rel) != bucket(first):
            out.append((first, rel, bucket(first)))
            first = rel
    return out


def mix_tile(m):
    return m + 12 if m < 4 else m - 4


class Semaphores:

    def __init__(self, sem):
        self.const_loaded = sem("const_loaded")
        self.rb_loaded = sem("rb_loaded")
        self.rb_scaled = sem("rb_scaled")
        self.v_built = sem("v_built")
        self.va_stored = sem("va_stored")
        self.vb_stored = sem("vb_stored")
        self.ta_built = sem("ta_built")
        self.tb_built = sem("tb_built")
        self.ta_fill = sem("ta_fill")
        self.ta_done = sem("ta_done")
        self.ident_zero = sem("ident_zero")
        self.ident_ready = sem("ident_ready")
        self.mem_loaded0 = sem("mem_loaded0")
        self.mem_loaded1 = sem("mem_loaded1")
        self.gm_loaded = sem("gm_loaded")
        self.gx_loaded = sem("gx_loaded")
        self.sq_done = sem("sq_done")
        self.ms_done = sem("ms_done")
        self.rt_done = sem("rt_done")
        self.rstd_done = sem("rstd_done")
        self.normed = sem("normed")
        self.turned = sem("turned")
        self.tr_hi = sem("tr_hi")
        self.tr_lo = sem("tr_lo")
        self.w_high = sem("w_high")
        self.w_low = sem("w_low")
        self.w_used = sem("w_used")
        self.pg_free = sem("pg_free")
        self.pq_free = sem("pq_free")
        self.stage_ready = sem("stage_ready")
        self.v_turned = sem("v_turned")
        self.stack_high = sem("stack_high")
        self.stack_low = sem("stack_low")
        self.k1_low = sem("k1_low")
        self.iwT_ready = sem("iwT_ready")
        self.iw_turned = sem("iw_turned")
        self.iw_ready = sem("iw_ready")
        self.idx_ready = sem("idx_ready")
        self.relu_ready = sem("relu_ready")
        self.idx_added = sem("idx_added")
        self.isc_done = sem("isc_done")
        self.isc_st0 = sem("isc_st0")
        self.isc_st1 = sem("isc_st1")
        self.mask_done = sem("mask_done")
        self.mask_stored = sem("mask_stored")
        self.W_loaded = sem("W_loaded")
        self.top_max = sem("top_max")
        self.top_out = sem("top_out")
        self.gate_exp = sem("gate_exp")
        self.gate_step = sem("gate_step")
        self.sg_ready = sem("sg_ready")
        self.biasA_loaded = sem("biasA_loaded")
        self.sink_ready = sem("sink_ready")
        self.memkv_ready = sem("memkv_ready")
        self.logits_ready = sem("logits_ready")
        self.S_biased = sem("S_biased")
        self.S_max = sem("S_max")
        self.neg_ready = sem("neg_ready")
        self.probs_ready = sem("probs_ready")
        self.recip_ready = sem("recip_ready")
        self.norm_ready = sem("norm_ready")
        self.pt_ready = sem("pt_ready")
        self.pt_copied = sem("pt_copied")
        self.ot_ready = sem("ot_ready")
        self.ot_copied = sem("ot_copied")
        self.yf_ready = sem("yf_ready")
        self.y_high = sem("y_high")
        self.y_low = sem("y_low")
        self.y_free = sem("y_free")
        self.biasB_loaded = sem("biasB_loaded")
        self.mask_ld0 = sem("mask_ld0")
        self.mask_ld1 = sem("mask_ld1")
        self.bpt_ready = sem("bpt_ready")
        self.bpt_copied = sem("bpt_copied")
        self.out_done = sem("out_done")
        self.fin_sum = sem("fin_sum")
        self.out_free = sem("out_free")
        self.sq_out = sem("sq_out")
        self.fin_ms = sem("fin_ms")
        self.fin_rt = sem("fin_rt")
        self.fin_done = sem("fin_done")
        self.out_stored = sem("out_stored")
        self.gf_loaded = sem("gf_loaded")


def hybrid_layer(nc, x, mem, g_norm, w_in, sinks, rel_bias, g_mem, w_mem_kv, w_out, g_final, out):
    ctx = ExitStack()
    with ctx:
        def dram(name, shape, dt=F32):
            return nc.dram_tensor(name, shape, dt, kind="Internal").ap()

        VA_LEN, VB_LEN = 384, 1152
        va_dram = dram("va_dram", (AH, VA_LEN))
        vb_dram = dram("vb_dram", (BH, VB_LEN))
        ta_dram = dram("ta_dram", (AH, P, 256))
        tb_dram = dram("tb_dram", (BH, P, SEQ))
        isc_dram = dram("isc_dram", (6, P, SEQ))
        mask_dram = dram("mask_dram", (7, P, SEQ), BF16)
        yhi_dram = dram("yhi_dram", (16, P, SEQ), F32R)
        ylo_dram = dram("ylo_dram", (16, P, SEQ), F32R)

        base = (nc.sbuf_base + 127) // 128 * 128
        end = [base]

        def at(name, shape, dt, offset):
            return nc.alloc_sbuf_tensor_at(name, shape, dt, offset=offset)

        def take(nbytes):
            end[0] += nbytes
            return end[0] - nbytes

        KB = 1024
        R1 = take(128 * KB)
        hn_hi = at("hn_hi", [P, KT, SEQ], F32R, R1)
        hn_lo = at("hn_lo", [P, KT, SEQ], F32R, R1 + 64 * KB)
        mem_raw = at("mem_raw", [P, 2, D], F32, R1 + 96 * KB)
        gmem_b = at("gmem_b", [P, D], F32, R1 + 112 * KB)
        y_hi = at("y_hi", [P, KT, SEQ], F32R, R1)
        y_lo = at("y_lo", [P, KT, SEQ], F32R, R1 + 64 * KB)
        R2 = take(24 * KB)
        w_raw = at("w_raw", [P, 4, 512], F32, R2)
        w_hi = at("w_hi", [P, 4, 512], F32R, R2 + 8 * KB)
        w_lo = at("w_lo", [P, 4, 512], F32R, R2 + 16 * KB)
        R3 = take(32 * KB)
        memT_hi = at("memT_hi", [P, KT, NMEM], F32R, R3)
        memT_lo = at("memT_lo", [P, KT, NMEM], F32R, R3 + 16 * KB)
        SA = at("SA", [P, 3, 2, 257], F32, R3)
        SB = at("SB", [P, 2, SEQ], F32, R3)
        acc = at("acc", [P, 2, SEQ], F32, R3)
        VA = at("VA", [AH, VA_LEN], F32, R3 + 4 * KB)
        rbA = at("rbA", [AH, NBUCKET], F32, R3 + 6 * KB)
        rbB = at("rbB", [BH, NBUCKET], F32, R3 + 6 * KB + 128)
        VB = at("VB", [BH, VB_LEN], F32, R3 + 8 * KB)
        av_stage = at("av_stage", [P, SEQ], F32, R3)
        PT = at("PT", [P, SEQ], F32, R3 + 8 * KB)
        relu_s = at("relu_s", [P, 2, SEQ], F32, R3 + 8 * KB)
        W = at("W", [P, SEQ], F32, R3 + 12 * KB)
        iwT = at("iwT", [P, SEQ], F32, R3 + 12 * KB)
        bv_stage = at("bv_stage", [P, SEQ], F32, R3 + 12 * KB)
        oT = at("oT", [P, SEQ], F32, R3 + 16 * KB)
        yf = at("yf", [P, SEQ], F32, R3 + 20 * KB)
        yhi_s = at("yhi_s", [P, SEQ], F32R, R3 + 24 * KB)
        ylo_s = at("ylo_s", [P, SEQ], F32R, R3 + 28 * KB)
        ik_hh = at("ik_hh", [P, SEQ], F32R, R3 + 24 * KB)
        ik_ll = at("ik_ll", [P, SEQ], F32R, R3 + 28 * KB)
        h_res = at("h_res", [P, 4, D], F32, R3)
        R4 = take(16 * KB)
        x_raw = at("x_raw", [P, 2, D], F32, R4)
        q0 = at("q0", [P, SEQ], F32, R4)
        gate_last = at("gate_last", [P, SEQ], F32, R4)
        q1 = at("q1", [P, SEQ], F32, R4 + 4 * KB)
        bk1 = at("bk1", [P, SEQ], F32, R4 + 8 * KB)
        ak = at("ak", [P, SEQ], F32, R4 + 12 * KB)
        biasB = at("biasB", [P, SEQ], F32, R4 + 12 * KB)
        x_res = at("x_res", [P, 4, 512], F32, R4)
        R5 = take(16 * KB)
        mk = at("mk", [P, CH, NMEM], F32, R5)
        bk0 = at("bk0", [P, SEQ], F32, R5)
        mv = at("mv", [P, 2, CH, P], F32, R5 + 4 * KB)
        bv0 = at("bv0", [P, NB, P], F32, R5 + 4 * KB)
        gx_b = at("gx_b", [P, D], F32, R5 + 8 * KB)
        av = at("av", [P, NB, P], F32, R5 + 8 * KB)
        bv1 = at("bv1", [P, NB, P], F32, R5 + 8 * KB)
        sg = at("sg", [P, SEQ], F32, R5 + 12 * KB)
        gf_b = at("gf_b", [P, D], F32, R5)
        R6 = take(6 * KB)
        k_hh = [at("k_hh0", [P, SEQ], F32R, R4 + 4 * KB), at("k_hh1", [P, SEQ], F32R, R5)]
        k_ll = [at("k_ll0", [P, SEQ], F32R, R4 + 8 * KB), at("k_ll1", [P, SEQ], F32R, R5 + 4 * KB)]
        q_hl = [at("q_hl0", [P, SEQ], F32R, R4), at("q_hl1", [P, SEQ], F32R, R3 + 8 * KB)]
        iq_hl = [at("iq_hl0", [P, SEQ], F32R, R3 + 16 * KB), at("iq_hl1", [P, SEQ], F32R, R3 + 20 * KB),
                 at("iq_hl2", [P, SEQ], F32R, R5 + 12 * KB), at("iq_hl3", [P, SEQ], F32R, R6)]
        PT_A = at("PT_A", [P, 512], F32, R6)
        biasA = at("biasA", [P, 2, 256], F32, R6 + 2 * KB)
        maskB = at("maskB", [P, 2, SEQ], BF16, R6)
        mask_s = at("mask_s", [P, SEQ], BF16, R6 + 4 * KB)
        mk_now = at("mk_now", [P, NMEM], F32, R6)
        mv_now = at("mv_now", [P, 2, P], F32, R6 + KB)
        sq_junk = at("sq_junk", [P, D], BF16, R6)
        ident = at("ident", [P, P], F32, take(512))
        sinks8 = at("sinks8", [P, AH], F32, take(64))
        sink_now = at("sink_now", [P, 2], F32, take(32))
        mx = at("mx", [P, NB, 2], F32, take(64))
        neg = at("neg", [P, NB, 2], F32, take(64))
        den = at("den", [P, NB, 2], F32, take(64))
        rec = at("rec", [P, NB, 2], F32, take(64))
        iw = at("iw", [P, NB, 4], F32, take(128))
        top8 = at("top8", [P, 8], F32, take(32))
        ssq = at("ssq", [P, 16], F32, take(64))
        rms = at("rms", [P, 16], F32, take(64))
        rstd = at("rstd", [P, 16], F32, take(64))
        rfix = at("rfix", [P, 4], F32, take(32))
        pace = at("pace", [P, 1], F32, take(32))
        ssum = at("ssum", [P, 4], F32, take(32))
        ms = at("ms", [P, 4], F32, take(32))
        masked = at("masked", [CHUNK, CHUNK], F32, take(256))
        assert end[0] <= nc.sbuf_usable_end, (end[0], nc.sbuf_usable_end)

        def pb(name):
            return ctx.enter_context(nc.psum_tensor(name, [P, 2, 512], F32))

        PG, PQ, L, TO = pb("PG"), pb("PQ"), pb("L"), pb("TO")
        PROJ = (PG, PQ)
        T, O = TO[:, 0, :], TO[:, 1, :]
        bank = [t[:, i, :] for t in (PG, PQ, L, TO) for i in range(2)]

        def half_rows(e):
            return slice(CHUNK * e, CHUNK * e + CHUNK)

        ST_K0, ST_IQ, ST_IK, ST_K1 = 2, (4, 6), 8, 10

        def tail_chunk(n):
            k = n // 2
            if n % 2 == 0:
                return w_hi[:, k % 4, :], w_lo[:, k % 4, :]
            return y_hi[:, k, 0:512], y_lo[:, k, 0:512]

        def norm_bank(j, kg):
            return bank[kg] if isinstance(j, int) and j == 0 else bank[4 + kg]

        def wide(t):
            return t[:, :, :].rearrange("p a b -> p (a b)")

        s = Semaphores(lambda n: ctx.enter_context(nc.semaphore(n)))
        w_loaded = [ctx.enter_context(nc.semaphore(f"w_loaded{i}")) for i in range(4)]
        x_loaded = [ctx.enter_context(nc.semaphore(f"x_loaded{i}")) for i in range(2)]
        xres_loaded = [ctx.enter_context(nc.semaphore(f"xres_loaded{i}")) for i in range(4)]
        y_loaded = [ctx.enter_context(nc.semaphore(f"y_loaded{i}")) for i in range(15)]
        proj_free = (s.pg_free, s.pq_free)

        w_in_v = w_in[0].rearrange("(c k p) n -> c p k n", k=4, p=P)
        w_mem_v = w_mem_kv[0].rearrange("(c k p) n -> c p k n", k=4, p=P)
        x_v = x[0].rearrange("(t p) d -> t p d", p=P)
        mem_v = mem[0].rearrange("(t p) d -> t p d", p=P)
        out_v = out[0].rearrange("(t p) d -> t p d", p=P)
        w_out_v = w_out[0].rearrange("(m p) n -> m p n", p=P)

        block = ctx.enter_context(nc.Block())

        @block.sync
        def _(sp):
            def chunk(n, c, src, k=4, width=P, first=False):
                if not first:
                    sp.wait_ge(s.w_low, n - 3)
                dst = w_raw[:, c, 0:512].rearrange("p (k n) -> p k n", k=k)[:, :, 0:width]
                sp.dma_start(dst, src).then_inc(w_loaded[c], 16)

            def tile(t, view, col, width=P, first=False):
                for c in range(4):
                    chunk(4 * t + c, c, view[c, :, :, bass.ds(col, width)], width=width, first=first)

            sp.dma_start(mem_raw[:, 0, :], mem_v[0]).then_inc(s.mem_loaded0, 16)
            sp.dma_start(gmem_b[:, :], g_mem[0:1, :].to_broadcast([P, D])).then_inc(s.gm_loaded, 16)
            sp.dma_start(mem_raw[:, 1, :], mem_v[1]).then_inc(s.mem_loaded1, 16)
            sp.dma_start(x_raw[:, 0, :], x_v[0]).then_inc(x_loaded[0], 16)
            sp.dma_start(gx_b[:, :], g_norm[0:1, :].to_broadcast([P, D])).then_inc(s.gx_loaded, 16)
            tile(0, w_mem_v, 0, first=True)
            sp.dma_start(x_raw[:, 1, :], x_v[1]).then_inc(x_loaded[1], 16)
            for t in range(1, MEM_TILES):
                for c in range(4):
                    if c == 1 and t < 7:
                        sp.wait_ge(s.turned, 4 * t + 8)
                        sp.dma_start(x_raw[:, (t + 1) % 2, :], x_v[t + 1]).then_inc(x_loaded[(t + 1) % 2], 16)
                    if t < CH:
                        chunk(4 * t + c, c, w_mem_v[c, :, :, t * P:t * P + P])
                    else:
                        k = 4 * (t - CH) + c
                        chunk(4 * t + c, c, w_mem_kv[0, P * k:P * k + P, CH * P:], k=1, width=512)
            tile(T_AK, w_in_v, C_AK)
            sp.wait_ge(s.w_used, 4 * MEM_TILES)
            with nc.allow_non_contiguous_dma(reason="a few hundred elements"):
                sp.dma_start(rbA[:, :], rel_bias[:, 0:AH].rearrange("n h -> h n")).then_inc(s.rb_loaded, 16)
                sp.dma_start(rbB[:, :], rel_bias[:, AH:AH + BH].rearrange("n h -> h n")).then_inc(s.rb_loaded, 16)
            sp.dma_start(sinks8[:, :], sinks[0:1, :].to_broadcast([P, AH])).then_inc(s.const_loaded, 16)
            tile(T_AV, w_in_v, C_AV)
            sp.wait_ge(s.v_built, 1)
            sp.dma_start(va_dram, VA[:, :]).then_inc(s.va_stored, 16)
            sp.dma_start(vb_dram, VB[:, :]).then_inc(s.vb_stored, 16)
            tile(T_IQ, w_in_v, C_IQ)
            sp.wait_ge(s.va_stored, 16)
            skew = bass.AP(va_dram.tensor, va_dram.offset + P - 1, [[VA_LEN, AH], [-1, P], [1, 256]])
            sp.dma_start(ta_dram, skew).then_inc(s.ta_built, 16)
            sp.wait_ge(s.vb_stored, 16)
            skew = bass.AP(vb_dram.tensor, vb_dram.offset + P - 1, [[VB_LEN, BH], [-1, P], [1, SEQ]])
            sp.dma_start(tb_dram, skew).then_inc(s.tb_built, 16)
            tile(T_IQ + 1, w_in_v, C_IQ + P)
            sp.wait_ge(s.ta_built, 16)
            sp.wait_ge(s.ta_fill, 1)
            neg_src = masked[:, :].rearrange("p (o k) -> p o k", o=1).to_broadcast([CHUNK, AH, CHUNK])
            ta_w = ta_dram.rearrange("h p k -> p h k")
            sp.dma_start(ta_w[0:CHUNK, :, 192:256], neg_src).then_inc(s.ta_done, 16)
            sp.dma_start(ta_w[CHUNK:P, :, 0:CHUNK], neg_src).then_inc(s.ta_done, 16)
            tile(T_IK, w_in_v, C_IK, width=IKW)
            tile(T_Q0, w_in_v, C_CQ)
            with sp.Fori(0, 3) as i:
                tile(T_LOOP + 2 * i, w_in_v, C_GATE + 12 * P + i * P)
                tile(T_LOOP + 1 + 2 * i, w_in_v, C_CQ + P + i * P)
            tile(T_LOOP + 6, w_in_v, C_GATE + 15 * P)
            tile(T_LOOP + 7, w_in_v, C_AQ)
            sp.wait_ge(s.ta_done, 32)

            def window_bias(i):
                sp.wait_ge(s.S_max, 8 * i + 32)
                sp.dma_start(biasA[:, :, :], ta_dram[bass.ds(2 * i, 2), :, :].rearrange("h p k -> p h k"))\
                  .then_inc(s.biasA_loaded, 16)

            with sp.Fori(0, 7) as i:
                tile(T_LOOP + 8 + 2 * i, w_in_v, C_GATE + i * P)
                window_bias(i)
                tile(T_LOOP + 9 + 2 * i, w_in_v, C_AQ + P + i * P)
            tile(T_LOOP + 22, w_in_v, C_GATE + 7 * P)
            window_bias(7)
            tile(T_LOOP + 23, w_in_v, C_BQ)
            tile(T_B, w_in_v, C_BK)
            tile(T_B + 1, w_in_v, C_BV)
            with sp.Fori(0, 3) as h:
                tile(T_BHEAD + 4 * h, w_in_v, C_GATE + 8 * P + h * P)
                tile(T_BHEAD + 4 * h + 1, w_in_v, C_BQ + P + h * P)
                tile(T_BHEAD + 4 * h + 2, w_in_v, C_BK + P + h * P)
                tile(T_BHEAD + 4 * h + 3, w_in_v, C_BV + P + h * P)
            tile(T_BHEAD + 12, w_in_v, C_GATE + 11 * P)

            def load_y(half, m):
                cols = slice(512 * half, 512 * half + 512)
                sp.dma_start(y_hi[:, m, cols].bitcast(F32), yhi_dram[m, :, cols].bitcast(F32)).then_inc(y_loaded[m], 16)
                sp.dma_start(y_lo[:, m, cols].bitcast(F32), ylo_dram[m, :, cols].bitcast(F32)).then_inc(y_loaded[m], 16)

            def load_residual(q, col, half):
                for j in range(4):
                    if not (isinstance(q, int) and q == 0):
                        sp.wait_ge(s.out_free, 8 + 4 * (q - 1) + j + 1)
                    sp.dma_start(x_res[:, j, :], x_v[4 * half + j, :, bass.ds(col, 512)]).then_inc(xres_loaded[j], 16)

            def out_chunk(q, m, col):
                chunk(N_OUT + 16 * q + m, m % 4, w_out_v[mix_tile(m), :, bass.ds(col, 512)], k=1, width=512)

            for m in range(16):
                out_chunk(0, m, 0)
                if m in (0, 14):
                    sp.wait_ge(s.y_free, 32 * (15 if m == 0 else 16))
                if m < 15:
                    if m % 4 == 0:
                        sp.wait_ge(s.w_used, 4 * T_ALL - 4 + m // 4 + 1)
                    load_y(0, m)
            sp.wait_ge(s.logits_ready, 8 * 16)
            sp.wait_ge(s.sg_ready, 1)
            load_residual(0, 0, 0)

            def out_loads(q, col, half, y_from=15):
                for m in range(16):
                    if m == 8:
                        load_residual(q, col, half)
                    out_chunk(q, m, col)
                    if m % 2 == 0 and y_from + m // 2 < 15:
                        load_y(1, y_from + m // 2)

            out_loads(1, 512, 0, y_from=0)
            out_loads(2, 1024, 0, y_from=8)
            sp.dma_start(gf_b[:, :], bass.AP(g_final.tensor, g_final.offset, [[0, P], [1, D]]))\
              .then_inc(s.gf_loaded, 16)
            out_loads(3, 1536, 0)
            with sp.Fori(1, 3) as n:
                out_loads(3 + n, n * 512 - 512, 1)
            for m in range(16):
                if m == 8:
                    load_residual(6, 1024, 1)
                for u in range(2):
                    chunk(N_TAIL + 2 * m + u, (2 * m + u) % 4, w_out_v[mix_tile(m), :, bass.ds(1024 + 512 * u, 512)],
                          k=1, width=512)
            load_residual(7, 1536, 1)

        @block.gpsimd
        def _(pool):
            pool.memset(ident[:, :], 0.0).then_inc(s.ident_zero, 1)
            pool.wait_ge(s.ident_zero, 1)
            pool.affine_select(out=ident[:, :], in_=ident[:, :], compare_op=ALU.not_equal, fill=1.0, base=0,
                               pattern=[[-1, P]], channel_multiplier=1).then_inc(s.ident_ready, 1)

            def low(n, c):
                pool.wait_ge(s.w_high, n + 1)
                pool.tensor_tensor(w_lo[:, c, :], w_raw[:, c, :], w_hi[:, c, :].bitcast(F32), ALU.subtract)\
                    .then_inc(s.w_low, 1)

            for n in range(3):
                low(n, n % 4)
            with pool.Fori(0, T_LOOP) as t:
                for c in range(4):
                    low(4 * t + c + 3, (c + 3) % 4)

            def normalise(g, b, kind):
                pool.wait_ge(s.recip_ready, g + 1)
                if kind == "A":
                    k0 = P if b == 0 else 0
                    for e in range(2):
                        v = SA[:, b % 3, e, k0:256]
                        last = pool.tensor_tensor(v, v, rec[:, b, e:e + 1].to_broadcast([P, 256 - k0]), ALU.mult)
                else:
                    w = NMEM if kind == "C" else P * (b + 1)
                    v = SA[:, b % 3, 0, 0:w] if kind == "C" else SB[:, b % 2, 0:w]
                    last = pool.tensor_tensor(v, v, rec[:, b, 0:1].to_broadcast([P, w]), ALU.mult)
                last.then_inc(s.norm_ready, 1)

            def gated(m, pg_count):
                pool.wait_ge(s.ot_copied, 8 * m + 8)
                pool.wait_ge(s.pg_free, pg_count)
                pool.tensor_tensor(yf[:, :], oT[:, :], sg[:, :], ALU.mult).then_inc(s.yf_ready, 1)
                pool.wait_ge(s.y_free, 32 * m + 32)
                pool.tensor_tensor(yhi_s[:, :], oT[:, :], sg[:, :], ALU.mult).then_inc(s.y_high, 1)

            def y_low(m):
                pool.wait_ge(s.y_high, m + 1)
                pool.tensor_tensor(ylo_s[:, :], yf[:, :], yhi_s[:, :].bitcast(F32), ALU.subtract)\
                    .then_inc(s.y_low, 1)

            def mix(m, kind):
                for slot in range(16):
                    if slot % 2 == 0:
                        low(4 * T_LOOP + 8 * m + slot // 2 + 3, (slot // 2 + 3) % 4)
                    if 0 <= slot - SHIFT[kind] - 1 < NB:
                        b = slot - SHIFT[kind] - 1
                        normalise(8 * m + b, b, kind)
                    if slot == 13:
                        gated(m, m + 8)
                    if slot == 15:
                        y_low(m)

            with pool.Fori(0, 4) as m:
                mix(m, "C")
            pool.wait_ge(s.stack_high, ST_K1)
            pool.wait_ge(s.y_low, 4)
            for e in range(2):
                if e == 1:
                    pool.wait_ge(s.k1_low, 1)
                last = pool.tensor_tensor(k_ll[1][half_rows(e), :], ak[CHUNK:P, :],
                                          k_hh[1][CHUNK:P, :].bitcast(F32), ALU.subtract)
                last.then_inc(s.k1_low, 1)
            pool.wait_ge(s.k1_low, 2)
            with pool.Fori(4, 12) as m:
                mix(m, "A")
            for n in range(4 * T_B, 4 * T_BHEAD):
                low(n + 3, (n + 3) % 4)

            def head(h, pos, last=False):
                m = 12 + h
                for slot in range(24 if last else 32):
                    if slot % 2 == 0 and slot < (8 if last else 32):
                        low(4 * T_BHEAD + 16 * h + slot // 2 + 3, (slot // 2 + 3) % 4)
                    if last and slot >= 8:
                        low(N_OUT + slot - 8 + 3, (slot - 8 + 3) % 4)
                    if slot - 1 in pos:
                        b = pos.index(slot - 1)
                        normalise(8 * m + b, b, "B")
                    if last and slot == 14:
                        y_last(0)
                if last:
                    y_last(1)
                else:
                    gated(m, 21 + 2 * h)
                    y_low(m)

            def y_last(half):
                cols = slice(512 * half, 512 * half + 512)
                pool.wait_ge(s.ot_copied, 8 * 15 + 4 + 4 * half)
                pool.wait_ge(s.sg_ready, 1)
                pool.tensor_tensor(yf[:, cols], oT[:, cols], sg[:, cols], ALU.mult).then_inc(s.yf_ready, 1)
                pool.wait_ge(s.y_high, 16 + half)
                pool.tensor_tensor(y_lo[:, 15, cols], yf[:, cols], y_hi[:, 15, cols].bitcast(F32), ALU.subtract)\
                    .then_inc(s.y_low, 1)

            with pool.Fori(0, BH - 1) as h:
                head(h, B_POS)
            head(BH - 1, B_LAST, last=True)
            low(N_OUT + 19, 3)
            with pool.Fori(N_OUT // 4 + 5, N_TAIL // 4) as t:
                for c in range(4):
                    low(4 * t + c, c)
            for n in range(32):
                pool.wait_ge(s.w_high, N_TAIL + n + 1)
                hi, lo = tail_chunk(n)
                pool.tensor_tensor(lo, w_raw[:, n % 4, :], hi.bitcast(F32), ALU.subtract).then_inc(s.w_low, 1)

        isc_stored = (s.isc_st0, s.isc_st1)
        isc_width = [512, 512, 768, 768, 1024, 1024]

        def store_scores(act, b):
            act.wait_ge(s.isc_done, b - 1)
            w = isc_width[b - 2]
            act.dma_start(isc_dram[b - 2, :, 0:w], acc[:, b % 2, 0:w]).then_inc(isc_stored[b % 2], 16)

        @block.scalar
        def _(act):
            def norm_root(j, e, raw):
                act.activation(sq_junk[:, :], raw, ACT.Square, accum_out=ssq[:, e:e + 1]).then_inc(s.sq_done, 1)
                act.wait_ge(s.ms_done, j + 1)
                act.activation(rms[:, e:e + 1], ms[:, e:e + 1], ACT.Sqrt).then_inc(s.rt_done, 1)

            def norm_high(j, dst, col):
                for kg in range(4):
                    act.wait_ge(s.turned, 4 * j + kg + 1)
                    act.activation(dst[:, 4 * kg:4 * kg + 4, bass.ds(col, P)],
                                   norm_bank(j, kg).rearrange("p (k t) -> p k t", k=4), ACT.Copy).then_inc(s.tr_hi, 1)

            act.wait_ge(s.mem_loaded0, 16)
            norm_root(0, 0, mem_raw[:, 0, :])
            act.wait_ge(s.mem_loaded1, 16)
            norm_root(1, 1, mem_raw[:, 1, :])
            norm_high(0, memT_hi, 0)
            act.wait_ge(x_loaded[0], 16)
            norm_root(2, 0, x_raw[:, 0, :])
            norm_high(1, memT_hi, P)
            act.wait_ge(x_loaded[1], 16)
            norm_root(3, 1, x_raw[:, 1, :])

            def high(t, c, first=False):
                act.wait_ge(w_loaded[c], 16 * t + 16)
                if not first:
                    act.wait_ge(s.w_used, 4 * t + c - 3)
                act.activation(w_hi[:, c, :], w_raw[:, c, :], ACT.Copy).then_inc(s.w_high, 1)

            def highs_ahead(t, c):
                if c == 0:
                    high(t, 3)
                else:
                    high(t + 1, c - 1)

            for c in range(4):
                high(0, c, first=True)

            def tile_highs(t, first=0):
                for c in range(first, 4):
                    highs_ahead(t, c)

            def x_high(i, e):
                norm_high(2 * i + 2 + e, hn_hi, 2 * P * i + P * e)

            def next_highs(i, e, root=True):
                for c in range(4):
                    high(2 * i + e + 1, c)
                    if c == 0 and root:
                        act.wait_ge(x_loaded[e], 16 * i + 32)
                        norm_root(2 * i + e + 4, e, x_raw[:, e, :])

            with act.Fori(0, 2) as i:
                for e in range(2):
                    t = 2 * i + e
                    x_high(i, e)
                    next_highs(i, e)
                    act.wait_ge(s.w_used, 4 * t + 4)
                    act.activation(mk[:, bass.ds(t, 1), :].rearrange("p o n -> p (o n)"), PROJ[e][:, 0, 0:NMEM],
                                   ACT.Copy).then_inc(proj_free[e], 1)

            for t in range(4, MEM_TILES):
                x_high(t // 2, t % 2)
                next_highs(t // 2, t % 2, root=t < 6)
            act.wait_ge(s.w_used, 4 * MEM_TILES)
            for e in range(2):
                act.activation(mv[:, e, :, :].rearrange("p h d -> p (h d)"), PROJ[e][:, 0, :], ACT.Copy)\
                   .then_inc(proj_free[e], 2)

            tile_highs(T_AK, 1)
            act.wait_ge(s.w_used, 4 * T_AK + 4)
            act.activation(ak[:, :], wide(PG), ACT.Copy).then_inc(s.pg_free, 1)
            act.wait_ge(s.pg_free, T_AK // 2 + 1)

            def high_twice(dst, src):
                for e in range(2):
                    act.activation(dst[half_rows(e), :], src, ACT.Copy).then_inc(s.stack_high, 1)

            def high_pair(dst, src):
                for e in range(2):
                    act.activation(dst[e][half_rows(e), :], src[half_rows(e), :], ACT.Copy).then_inc(s.stack_high, 1)

            high_twice(k_hh[0], ak[0:CHUNK, :])
            tile_highs(T_AV)
            act.wait_ge(s.w_used, 4 * T_AV + 4)
            act.activation(av_stage[:, :], wide(PQ), ACT.Copy).then_inc(s.stage_ready, 1)
            highs_ahead(T_IQ, 0)
            highs_ahead(T_IQ, 1)
            act.wait_ge(s.v_turned, 1)
            act.activation(av[:, :, :].rearrange("p k d -> p (k d)"), wide(PQ), ACT.Copy).then_inc(s.pq_free, 1)
            for e in range(2):
                t = T_IQ + e
                tile_highs(t, 2 if e == 0 else 0)
                act.wait_ge(s.w_used, 4 * t + 4)
                high_pair(iq_hl[2 * e:2 * e + 2], wide(PROJ[e]))
            tile_highs(T_IK)
            act.wait_ge(s.w_used, 4 * T_IK + 4)
            high_twice(ik_hh, wide(PG)[0:CHUNK, :])
            act.wait_ge(s.vb_stored, 16)
            act.activation(iwT[CHUNK:IKW, :], wide(PG)[CHUNK:IKW, :], ACT.Copy).then_inc(s.iwT_ready, 1)

            act.wait_ge(s.iw_turned, 1)
            for slot in range(8):
                for u in range(sum(UNITS_AT[:slot]), sum(UNITS_AT[:slot + 1])):
                    b = 2 + u // 4
                    act.wait_ge(s.idx_ready, u + 1)
                    if u >= 2:
                        act.wait_ge(s.idx_added, u - 1)
                    src = wide(L if u % 2 == 0 else TO)
                    act.activation(relu_s[:, u % 2, 0:P * (b + 1)], src[:, 0:P * (b + 1)], ACT.Relu, scale=0.125)\
                       .then_inc(s.relu_ready, 1)
                    if u % 4 == 1 and b > 2:
                        store_scores(act, b - 1)
                if slot % 2 == 0:
                    highs_ahead(T_Q0, slot // 2)
            def gate_exp(m, t):
                act.wait_ge(s.w_used, 4 * t + 4)
                act.activation(sg[:, :], wide(PG), ACT.Exp, scale=-1.0).then_inc(s.gate_exp, 1)

            def probs(g, b, kind):
                act.wait_ge(s.neg_ready, g + 1)
                if kind == "A":
                    k0 = P if b == 0 else 0
                    for e in range(2):
                        v = SA[:, b % 3, e, k0:257]
                        last = act.activation(v, v, ACT.Exp, scale=A_SCALE, bias=neg[:, b, e:e + 1],
                                              accum_out=den[:, b, e:e + 1])
                elif kind == "C":
                    last = act.activation(SA[:, b % 3, 0, 0:NMEM], L[:, b % 2, 0:NMEM], ACT.Exp, scale=BC_SCALE,
                                          bias=neg[:, b, 0:1], accum_out=den[:, b, 0:1])
                else:
                    v = SB[:, b % 2, 0:P * (b + 1)]
                    last = act.activation(v, v, ACT.Exp, scale=BC_SCALE, bias=neg[:, b, 0:1],
                                          accum_out=den[:, b, 0:1])
                last.then_inc(s.probs_ready, 1)

            def turned_probs(g, b, kind):
                act.wait_ge(s.pt_ready, g + 1)
                a, z = (0, 256) if kind == "C" else (256 if b == 0 else 0, 512)
                act.activation((PT if kind == "C" else PT_A)[:, a:z], T[:, a:z], ACT.Copy).then_inc(s.pt_copied, 1)

            def head_out(g, b):
                act.wait_ge(s.ot_ready, g + 1)
                act.activation(oT[:, P * b:P * b + P], O[:, 0:P], ACT.Copy).then_inc(s.ot_copied, 1)

            def y_row(dst, m):
                return dst[bass.ds(m, 1), :, :].rearrange("o p t -> (o p) t").bitcast(F32)

            def y_store(m):
                act.wait_ge(s.y_low, m + 1)
                act.dma_start(y_row(yhi_dram, m), yhi_s[:, :].bitcast(F32)).then_inc(s.y_free, 16)
                act.dma_start(y_row(ylo_dram, m), ylo_s[:, :].bitcast(F32)).then_inc(s.y_free, 16)

            def mix(m, kind, pair=None, width=0, first=False, scores_slot=1):
                act.wait_ge(s.w_used, 4 * (T_LOOP + 2 * m))
                if kind == "C":
                    act.activation(q0[:, :], wide(PQ), ACT.Copy).then_inc(s.pq_free, 1)
                else:
                    high_pair(q_hl, wide(PQ))
                o = SHIFT[kind]
                for slot in range(17):
                    if slot == 3 and not first:
                        y_store(m - 1)
                    if slot == 0 and kind == "C":
                        act.activation(mk_now[:, :], mk[:, bass.ds(m, 1), :].rearrange("p o n -> p (o n)"), ACT.Copy)
                        act.activation(mv_now[:, :, :], mv[:, :, bass.ds(m, 1), :].rearrange("p k o d -> p k (o d)"),
                                       ACT.Copy).then_inc(s.memkv_ready, 1)
                    if 0 <= slot - o - 4 < NB:
                        turned_probs(8 * m + slot - o - 4, slot - o - 4, kind)
                    if 0 <= slot - o - 5 < NB:
                        head_out(8 * m + slot - o - 5, slot - o - 5)
                    if slot == 1 and first:
                        store_scores(act, 7)
                        act.wait_ge(s.isc_st0, 48)
                        act.wait_ge(s.isc_st1, 48)
                    if 0 <= slot - o - 1 < NB:
                        probs(8 * m + slot - o - 1, slot - o - 1, kind)
                    if slot == scores_slot and pair is not None:
                        act.wait_ge(s.mask_done, pair + 1)
                        act.dma_start(mask_dram[pair, :, 0:width], mask_s[:, 0:width]).then_inc(s.mask_stored, 16)
                        act.dma_start(W[:, 0:width], isc_dram[pair, :, 0:width]).then_inc(s.W_loaded, 16)
                    if slot % 2 == 0 and slot < 16:
                        c = slot // 2
                        highs_ahead(T_LOOP + 2 * m + c // 4, c % 4)
                    if slot == 8:
                        gate_exp(m, T_LOOP + 2 * m)

            for m in range(4):
                mix(m, "C", pair=m // 2 if m % 2 == 0 else None, width=512, first=m == 0)
            high_twice(k_hh[1], ak[CHUNK:P, :])
            with act.Fori(2, 4) as pair:
                mix(2 * pair, "A", pair, 768)
                mix(2 * pair + 1, "A")
            mix(8, "A", 4, 1024)
            mix(9, "A")
            mix(10, "A", 5, 1024, scores_slot=5)
            mix(11, "A")

            act.wait_ge(s.w_used, 4 * T_B)
            act.activation(q0[:, :], wide(PQ), ACT.Copy).then_inc(s.pq_free, 1)
            tile_highs(T_B)
            act.wait_ge(s.w_used, 4 * T_B + 4)
            act.activation(bk0[:, :], wide(PG), ACT.Copy).then_inc(s.pg_free, 1)
            tile_highs(T_B + 1)

            def stage_values(t):
                act.wait_ge(s.w_used, 4 * t + 4)
                act.activation(bv_stage[:, :], wide(PQ), ACT.Copy).then_inc(s.stage_ready, 1)

            act.wait_ge(s.mask_done, 7)
            act.dma_start(mask_dram[6, :, :], mask_s[:, :]).then_inc(s.mask_stored, 16)
            stage_values(T_B + 1)
            act.wait_ge(s.mask_stored, 16 * 7)

            def head(h, pos):
                m = 12 + h
                last = h == BH - 1

                def load_mask(b):
                    src = mask_dram[max(0, b - 1), :, P:3 * P] if b == 1 else mask_dram[max(0, b - 1), :, 0:P * (b + 1)]
                    act.dma_start(maskB[:, b % 2, 0:P * (b + 1)], src).then_inc((s.mask_ld0, s.mask_ld1)[b % 2], 16)

                act.wait_ge(s.S_max, 8 * m)
                if h == 0:
                    act.wait_ge(s.tb_built, 16)
                act.dma_start(biasB[:, :], tb_dram[h]).then_inc(s.biasB_loaded, 16)
                load_mask(0)
                load_mask(1)
                for slot in range(25 if last else 33):
                    if last and slot == 8:
                        act.wait_ge(s.w_used, 4 * (T_BHEAD + 4 * h + 1))
                        act.activation(gate_last[:, :], wide(PG), ACT.Copy).then_inc(s.pg_free, 1)
                        act.wait_ge(s.pg_free, 27)
                        act.activation(sg[:, :], gate_last[:, :], ACT.Exp, scale=-1.0).then_inc(s.gate_exp, 1)
                    if slot == 3:
                        y_store(m - 1)
                    if slot == 2:
                        act.wait_ge(s.v_turned, 2 + h)
                        act.activation((bv0, bv1)[h % 2][:, :, :].rearrange("p k d -> p (k d)"), wide(PQ), ACT.Copy)\
                           .then_inc(s.pq_free, 1)
                    for b in range(NB):
                        two = b >= 4
                        if slot == pos[b] + 4:
                            act.wait_ge(s.bpt_ready, 12 * h + (2 * b - 4 if two else b) + 1)
                            n = P * min(4, b + 1)
                            act.activation(PT[:, 0:n], T[:, 0:n], ACT.Copy).then_inc(s.bpt_copied, 1)
                        if slot == pos[b] + 5 and two:
                            act.wait_ge(s.bpt_ready, 12 * h + 2 * b - 4 + 2)
                            n = P * (b - 3)
                            act.activation(PT[:, 512:512 + n], T[:, 0:n], ACT.Copy).then_inc(s.bpt_copied, 1)
                        if slot == pos[b] + 6:
                            head_out(8 * m + b, b)
                        if slot == pos[b] + 1:
                            probs(8 * m + b, b, "B")
                            if b + 2 < NB:
                                load_mask(b + 2)
                    if slot % 2 == 0 and slot < (8 if last else 32):
                        c = slot // 2
                        highs_ahead(T_BHEAD + 4 * h + c // 4, c % 4)
                    if last and 8 <= slot < 24:
                        k = slot - 8 + 3
                        high(T_ALL + k // 4, k % 4)
                    if slot == 8 and not last:
                        gate_exp(m, T_BHEAD + 4 * h)
                    if last and slot == 15:
                        y_last(0)
                    if slot == 16 and not last:
                        act.wait_ge(s.w_used, 4 * (T_BHEAD + 4 * h + 2))
                        act.activation((q0, q1)[(h + 1) % 2][:, :], wide(PQ), ACT.Copy).then_inc(s.pq_free, 1)
                    if slot == 24 and not last:
                        act.wait_ge(s.w_used, 4 * (T_BHEAD + 4 * h + 3))
                        act.activation((bk0, bk1)[(h + 1) % 2][:, :], wide(PG), ACT.Copy).then_inc(s.pg_free, 1)
                if last:
                    y_last(1)
                else:
                    stage_values(T_BHEAD + 4 * h + 3)

            def y_last(half):
                act.wait_ge(s.yf_ready, 16 + half)
                cols = slice(512 * half, 512 * half + 512)
                act.activation(y_hi[:, 15, cols], yf[:, cols], ACT.Copy).then_inc(s.y_high, 1)

            for h in range(BH - 1):
                head(h, B_POS)
            head(BH - 1, B_LAST)

            def root(count, cols):
                act.wait_ge(s.fin_ms, count)
                act.activation(rms[:, cols], ms[:, cols], ACT.Sqrt).then_inc(s.fin_rt, 1)

            def store(count, t, j, cols=slice(0, D)):
                act.wait_ge(s.fin_done, count)
                act.dma_start(out_v[t, :, cols], h_res[:, j, cols]).then_inc(s.out_stored, 16)

            def square(q, n, j):
                act.wait_ge(s.out_free, 8 + 4 * q + j + 1)
                act.activation(sq_junk[:, 512 * j:512 * j + 512], h_res[:, j, bass.ds(n * 512, 512)], ACT.Square,
                               accum_out=ssq[:, bass.ds(4 * j + n, 1)]).then_inc(s.sq_out, 1)

            def out_n(q, n, first=False, last=False):
                for k in range(3, 16 if last else 19):
                    high(T_ALL + 4 * q + k // 4, k % 4)
                    if k == 7:
                        for j in range(4):
                            square(q - 1, 3 if first else n - 1, j)
                    if k == 8 and first:
                        root(1, slice(0, 4))
                    if k == 12 and first:
                        for j in range(4):
                            store(j + 1, j, j)

            with act.Fori(1, 4) as n:
                out_n(n, n)
            out_n(4, 0, first=True)
            out_n(5, 1, last=True)
            for n in range(32):
                act.wait_ge(w_loaded[n % 4], 16 * (N_TAIL + n - n % 4) // 4 + 16)
                if n % 2 == 0:
                    act.wait_ge(s.w_used, N_TAIL + n // 2 - 3)
                act.activation(tail_chunk(n)[0], w_raw[:, n % 4, :], ACT.Copy).then_inc(s.w_high, 1)
                if n == 10:
                    for j in range(4):
                        square(5, 1, j)
            for j in range(4):
                square(6, 2, j)
            act.wait_ge(s.sq_out, 28)
            for j in range(4):
                square(7, 3, j)
                root(2 + j, slice(j, j + 1))
                if j < 3:
                    store(5 + j, 4 + j, j)
                else:
                    for i in range(2):
                        store(8 + i, 7, 3, slice(1024 * i, 1024 * i + 1024))
            act.wait_ge(s.out_stored, 16 * 9)

        @block.vector
        def _(dve):
            def carry():
                dve.memset(pace[:, :], 0.0)

            dve.memset(masked[:, :], MASKED).then_inc(s.ta_fill, 1)

            def normed(j, e, raw, g):
                dve.wait_ge(s.sq_done, j + 1)
                dve.tensor_scalar(ms[:, e:e + 1], ssq[:, e:e + 1], 1.0 / D, EPS, ALU.mult, ALU.add)\
                   .then_inc(s.ms_done, 1)
                dve.wait_ge(s.rt_done, j + 1)
                dve.reciprocal(rstd[:, e:e + 1], rms[:, e:e + 1]).then_inc(s.rstd_done, 1)
                refine(slice(e, e + 1), 4 * j)
                dve.scalar_tensor_tensor(out=raw, in0=raw, scalar=rstd[:, e:e + 1], in1=g, op0=ALU.mult,
                                         op1=ALU.mult).then_inc(s.normed, 1)

            def refine(cols, done):
                dve.wait_ge(s.rstd_done, done + 1)
                dve.tensor_tensor(rfix[:, cols], rstd[:, cols], rstd[:, cols], ALU.mult).then_inc(s.rstd_done, 1)
                dve.wait_ge(s.rstd_done, done + 2)
                carry()
                dve.scalar_tensor_tensor(out=rfix[:, cols], in0=rfix[:, cols], scalar=-0.5, in1=ms[:, cols],
                                         op0=ALU.mult, op1=ALU.mult).then_inc(s.rstd_done, 1)
                dve.wait_ge(s.rstd_done, done + 3)
                carry()
                dve.scalar_tensor_tensor(out=rstd[:, cols], in0=rfix[:, cols], scalar=1.5, in1=rstd[:, cols],
                                         op0=ALU.add, op1=ALU.mult).then_inc(s.rstd_done, 1)
                dve.wait_ge(s.rstd_done, done + 4)

            def norm_low(j, hi, lo, col):
                for kg in range(4):
                    dve.wait_ge(s.tr_hi, 4 * j + kg + 1)
                    dve.tensor_tensor(lo[:, 4 * kg:4 * kg + 4, bass.ds(col, P)],
                                      norm_bank(j, kg).rearrange("p (k t) -> p k t", k=4),
                                      hi[:, 4 * kg:4 * kg + 4, bass.ds(col, P)].bitcast(F32), ALU.subtract)\
                       .then_inc(s.tr_lo, 1)

            dve.wait_ge(s.gm_loaded, 16)
            normed(0, 0, mem_raw[:, 0, :], gmem_b[:, :])
            normed(1, 1, mem_raw[:, 1, :], gmem_b[:, :])
            norm_low(0, memT_hi, memT_lo, 0)
            dve.wait_ge(s.gx_loaded, 16)
            normed(2, 0, x_raw[:, 0, :], gx_b[:, :])
            norm_low(1, memT_hi, memT_lo, P)
            with dve.Fori(0, 3) as i:
                normed(2 * i + 3, 1, x_raw[:, 1, :], gx_b[:, :])
                norm_low(2 * i + 2, hn_hi, hn_lo, 2 * P * i)
                normed(2 * i + 4, 0, x_raw[:, 0, :], gx_b[:, :])
                norm_low(2 * i + 3, hn_hi, hn_lo, 2 * P * i + P)
            normed(9, 1, x_raw[:, 1, :], gx_b[:, :])
            norm_low(8, hn_hi, hn_lo, 6 * P)
            norm_low(9, hn_hi, hn_lo, 7 * P)

            def low_twice(count, dst, src, high):
                dve.wait_ge(s.stack_high, count)
                for e in range(2):
                    last = dve.tensor_tensor(dst[half_rows(e), :], src, high.bitcast(F32), ALU.subtract)
                    last.then_inc(s.stack_low, 1)

            def low_pair(count, dst, src, free):
                for e in range(2):
                    dve.wait_ge(s.stack_high, count - 1 + e)
                    rows = half_rows(e)
                    last = dve.tensor_tensor(dst[e][half_rows(1 - e), :], src[rows, :], dst[e][rows, :].bitcast(F32),
                                             ALU.subtract)
                    last.then_inc(*((s.stack_low, 1) if e == 0 else (free, 1)))

            low_twice(ST_K0, k_ll[0], ak[0:CHUNK, :], k_hh[0][0:CHUNK, :])

            dve.wait_ge(s.const_loaded, 16)
            dve.tensor_scalar(sinks8[:, :], sinks8[:, :], 1 / A_SCALE, None, ALU.mult).then_inc(s.sink_ready, 1)

            dve.wait_ge(s.rb_loaded, 32)
            dve.tensor_scalar(rbA[:, :], rbA[:, :], 1 / A_SCALE, None, ALU.mult)
            dve.tensor_scalar(rbB[:, :], rbB[:, :], 1 / BC_SCALE, None, ALU.mult).then_inc(s.rb_scaled, 1)
            dve.wait_ge(s.rb_scaled, 1)
            dve.memset(VA[:, VA_LEN - 1:VA_LEN], 0.0)
            dve.memset(VB[:, VB_LEN - 1:VB_LEN], 0.0)
            for first, last, r in bucket_edges():
                for V, rb, heads, zero in ((VA, rbA, AH, 255), (VB, rbB, BH, SEQ - 1)):
                    a, z = max(first + zero, 0), last + zero
                    if z > a:
                        ins = dve.tensor_copy(V[:, a:z], rb[:, r:r + 1].to_broadcast([heads, z - a]))
            ins.then_inc(s.v_built, 1)
            dve.memset(mask_s[CHUNK:P, :], 0.0)
            dve.memset(mask_s[0:CHUNK, 0:64], 0.0)
            dve.memset(mask_s[0:CHUNK, 64:128], MASKED)
            dve.memset(mask_s[0:CHUNK, 128:320], 0.0)
            dve.memset(mask_s[0:CHUNK, 320:384], MASKED)
            dve.memset(mask_s[0:CHUNK, 384:SEQ], 0.0).then_inc(s.mask_done, 1)


            for e in range(2):
                low_pair(ST_IQ[e], iq_hl[2 * e:2 * e + 2], wide(PROJ[e]), proj_free[e])
            low_twice(ST_IK, ik_ll, wide(PG)[0:CHUNK, :], ik_hh[0:CHUNK, :])
            dve.wait_ge(s.iwT_ready, 1)
            dve.memset(pace[:, :], 0.0).then_inc(s.pg_free, 1)
            dve.wait_ge(s.va_stored, 16)
            dve.wait_ge(s.iw_turned, 1)
            dve.tensor_scalar(iw[:, :, :].rearrange("p b h -> p (b h)"), T[:, 0:4 * NB], 0.5, None, ALU.mult)\
               .then_inc(s.iw_ready, 1)
            dve.wait_ge(s.iw_ready, 1)
            for u in range(24):
                b, h = 2 + u // 4, u % 4
                w = P * (b + 1)
                dve.wait_ge(s.relu_ready, u + 1)
                if h == 0:
                    if b >= 4:
                        dve.wait_ge(isc_stored[b % 2], 16 * ((b - 2) // 2))
                    dve.tensor_scalar(acc[:, b % 2, 0:w], relu_s[:, u % 2, 0:w], iw[:, b, 0:1], 0.0,
                                      ALU.mult, ALU.add).then_inc(s.idx_added, 1)
                else:
                    dve.wait_ge(s.idx_added, u)
                    dve.scalar_tensor_tensor(out=acc[:, b % 2, 0:w], in0=relu_s[:, u % 2, 0:w],
                                             scalar=iw[:, b, h:h + 1], in1=acc[:, b % 2, 0:w],
                                             op0=ALU.mult, op1=ALU.add).then_inc(s.idx_added, 1)
                if h == 3:
                    dve.wait_ge(s.idx_added, u + 1)
                    if isc_width[b - 2] > w:
                        dve.memset(acc[:, b % 2, w:isc_width[b - 2]], MASKED)
                    if b == NB - 1:
                        dve.memset(acc[0:CHUNK, b % 2, w - CHUNK:w - 32], MASKED).then_inc(s.y_free, 32)
                        dve.memset(acc[0:CHUNK, b % 2, w - 32:w], MASKED).then_inc(s.isc_done, 1)
                    else:
                        dve.memset(acc[0:CHUNK, b % 2, w - CHUNK:w], MASKED).then_inc(s.isc_done, 1)

            def choose(pair, n, width):
                if n == 0:
                    dve.wait_ge(s.W_loaded, 16 * pair + 16)
                else:
                    dve.wait_ge(s.top_out, 32 * pair + n)
                carry()
                dve.max(top8[:, :], W[:, 0:width]).then_inc(s.top_max, 1)
                dve.wait_ge(s.top_max, 32 * pair + n + 1)
                carry()
                dve.match_replace(W[:, 0:width], top8[:, :], W[:, 0:width], TAKEN).then_inc(s.top_out, 1)
                if n == ROUNDS - 1:
                    dve.wait_ge(s.top_out, 32 * pair + ROUNDS)
                    dve.wait_ge(s.mask_stored, 16 * pair + 16)
                    dve.tensor_scalar(mask_s[:, 0:width], W[:, 0:width], BELOW_MASKED, MASKED, ALU.is_gt, ALU.mult)\
                       .then_inc(s.mask_done, 1)

            def schedule(counts, pair, done, width):
                return [[(pair, done + sum(counts[:slot]) + i, width) for i in range(c)] for slot, c in enumerate(counts)]

            FIRST = [0, 0, 1, 1, 2, 1, 2, 1, 1] + [0] * 3 + [1, 1, 1, 2]
            SECOND = [1, 1, 1, 2, 1, 2, 1, 2, 1] + [0] * 2 + [1, 1, 2, 1, 1]
            assert sum(FIRST + SECOND) == ROUNDS
            TILE8 = [0, 0, 1, 1, 1, 1, 2, 1, 1] + [0] * 3 + [1, 1, 1, 2]
            TILE9 = [1, 1, 1, 1, 1, 2, 1, 1, 1] + [0] * 3 + [1, 1, 1, 2]
            TILE10 = [1, 1, 1, 1] + [0] * 12
            TILE10_LATE = [0] * 7 + [1, 1] + [0] * 3 + [1] * 4
            TILE11 = [1] * 9 + [0] * 3 + [1] * 4
            assert sum(TILE8 + TILE9 + TILE10) == ROUNDS

            def negated(g, b, n, scale):
                dve.wait_ge(s.S_max, g + 1)
                dve.tensor_scalar(neg[:, b, 0:n], mx[:, b, 0:n], -scale, None, ALU.mult).then_inc(s.neg_ready, 1)

            def maxima(m, b, kind):
                g = 8 * m + b
                dve.wait_ge(s.logits_ready, g + 1)
                if kind == "C":
                    dve.tensor_reduce(mx[:, b, 0:1], L[:, b % 2, 0:NMEM], AX.X, ALU.max).then_inc(s.S_max, 1)
                    negated(g, b, 1, BC_SCALE)
                else:
                    k0 = P if b == 0 else 0
                    if b == 0:
                        dve.wait_ge(s.biasA_loaded, 16 * (m - 3))
                    dve.tensor_copy(SA[:, b % 3, :, 256:257].rearrange("p e o -> p (e o)"), sink_now[:, :])
                    for e in range(2):
                        last = dve.tensor_tensor_reduce(SA[:, b % 3, e, k0:256], L[:, b % 2, 256 * e:256 * e + 256 - k0],
                                                        biasA[:, e, k0:256], 1.0, sink_now[:, e:e + 1], ALU.add,
                                                        ALU.max, mx[:, b, e:e + 1])
                    last.then_inc(s.S_max, 1)
                    negated(g, b, 2, A_SCALE)

            def reciprocals(g, b, n):
                dve.wait_ge(s.probs_ready, g + 1)
                dve.reciprocal(rec[:, b, 0:n], den[:, b, 0:n]).then_inc(s.recip_ready, 1)

            def silu(m, part, gate=wide(PG), done=s.pg_free):
                if part == 0:
                    dve.wait_ge(s.gate_exp, m + 1)
                    dve.tensor_scalar(sg[:, :], sg[:, :], 1.0, None, ALU.add).then_inc(s.gate_step, 1)
                elif part < 3:
                    if part == 1:
                        dve.wait_ge(s.gate_step, 3 * m + 1)
                    v = sg[:, 512 * part - 512:512 * part]
                    dve.reciprocal(v, v).then_inc(s.gate_step, 1)
                else:
                    dve.wait_ge(s.gate_step, 3 * m + 3)
                    dve.tensor_tensor(sg[:, :], gate, sg[:, :], ALU.mult).then_inc(done, 1)

            def mix(m, kind, rounds):
                if kind == "A":
                    low_pair(ST_K1 + 2 * (m - 4) + 2, q_hl, wide(PQ), s.pq_free)
                    dve.wait_ge(s.S_max, 8 * m)
                    dve.tensor_copy(sink_now[:, :], sinks8[:, bass.ds(2 * (m - 4), 2)]).then_inc(s.sink_ready, 1)
                    dve.wait_ge(s.sink_ready, m - 2)
                for slot in range(16):
                    if 0 <= slot - SHIFT[kind] < NB:
                        maxima(m, slot - SHIFT[kind], kind)
                    if 0 <= slot - SHIFT[kind] - 1 < NB:
                        b = slot - SHIFT[kind] - 1
                        reciprocals(8 * m + b, b, 2 if kind == "A" else 1)
                    for pair, n, width in rounds[slot]:
                        choose(pair, n, width)
                    if 9 <= slot <= 12:
                        silu(m, slot - 9)

            for kind, lo, width in (("C", 0, 512), ("A", 2, 768)):
                if lo == 2:
                    dve.wait_ge(s.sink_ready, 1)
                with dve.Fori(lo, lo + 2) as pair:
                    mix(2 * pair, kind, schedule(FIRST, pair, 0, width))
                    mix(2 * pair + 1, kind, schedule(SECOND, pair, sum(FIRST), width))
            mix(8, "A", schedule(TILE8, 4, 0, 7 * P))
            mix(9, "A", schedule(TILE9, 4, sum(TILE8), 7 * P))
            both = zip(schedule(TILE10, 4, sum(TILE8 + TILE9), 7 * P), schedule(TILE10_LATE, 5, 0, 8 * P))
            mix(10, "A", [a + b for a, b in both])
            mix(11, "A", schedule(TILE11, 5, sum(TILE10_LATE), 8 * P))
            for n in range(sum(TILE10_LATE + TILE11), ROUNDS):
                choose(5, n, 8 * P)

            def head(h, pos):
                m = 12 + h
                for slot in range(32):
                    if slot in pos:
                        b = pos.index(slot)
                        g, w = 8 * m + b, P * (b + 1)
                        dve.wait_ge(s.logits_ready, g + 1)
                        if b == 0:
                            dve.wait_ge(s.biasB_loaded, 16 * h + 16)
                        dve.tensor_tensor(SB[:, b % 2, 0:w], wide(L)[:, 0:w], biasB[:, SEQ - w:SEQ], ALU.add)\
                           .then_inc(s.S_biased, 1)
                        dve.wait_ge(s.S_biased, 8 * h + b + 1)
                        dve.wait_ge((s.mask_ld0, s.mask_ld1)[b % 2], 64 * h + 16 * (b // 2) + 16)
                        carry()
                        dve.tensor_tensor_reduce(SB[:, b % 2, 0:w], SB[:, b % 2, 0:w], maskB[:, b % 2, 0:w], 1.0,
                                                 MASKED, ALU.add, ALU.max, mx[:, b, 0:1]).then_inc(s.S_max, 1)
                        negated(g, b, 1, BC_SCALE)
                    if slot - 1 in pos:
                        b = pos.index(slot - 1)
                        reciprocals(8 * m + b, b, 1)
                    if 9 <= slot <= 12:
                        if pos is B_POS:
                            silu(m, slot - 9)
                        else:
                            silu(m, slot - 9, gate=gate_last[:, :], done=s.sg_ready)

            with dve.Fori(0, BH - 1) as h:
                head(h, B_POS)
            head(BH - 1, B_LAST)

            dve.wait_ge(s.ot_copied, 8 * 16)
            dve.memset(pace[:, :], 0.0).then_inc(s.out_free, 8)
            dve.wait_ge(s.y_low, 17)
            def add_residual(half, n, e, j):
                if j < 3:
                    dve.wait_ge(s.out_done, 12 * half + 3 * n + j + 1)
                else:
                    dve.wait_ge(s.w_used, N_OUT + 64 * half + 16 * n + 16)
                dve.wait_ge(xres_loaded[j], 64 * half + 16 * n + 16)
                dve.tensor_tensor(h_res[:, j, bass.ds(n * 512, 512)], bank[4 * e + j], x_res[:, j, :],
                                  ALU.add).then_inc(s.out_free, 1)

            def final_root(count, sums, js, refined):
                cols = slice(js.start, js.stop)
                dve.wait_ge(s.sq_out, sums)
                dve.tensor_reduce(ssum[:, cols], ssq[:, 4 * js.start:4 * js.stop].rearrange("p (j n) -> p j n", n=4),
                                  AX.X, ALU.add).then_inc(s.fin_sum, 1)
                dve.wait_ge(s.fin_sum, count)
                dve.tensor_scalar(ms[:, cols], ssum[:, cols], 1.0 / D, EPS, ALU.mult, ALU.add).then_inc(s.fin_ms, 1)
                dve.wait_ge(s.fin_rt, count)
                dve.reciprocal(rstd[:, cols], rms[:, cols]).then_inc(s.rstd_done, 1)
                refine(cols, refined)

            def scale(j, cols=slice(0, D)):
                dve.scalar_tensor_tensor(out=h_res[:, j, cols], in0=h_res[:, j, cols], scalar=rstd[:, j:j + 1],
                                         in1=gf_b[:, cols], op0=ALU.mult, op1=ALU.mult).then_inc(s.fin_done, 1)

            with dve.Fori(0, 2) as i:
                for e in range(2):
                    for j in range(4):
                        add_residual(0, 2 * i + e, e, j)
            final_root(1, 16, range(0, 4), 40)
            dve.wait_ge(s.gf_loaded, 16)
            for j in range(4):
                scale(j)
            dve.wait_ge(s.out_stored, 64)
            for n in range(3):
                for j in range(4):
                    add_residual(1, n, n % 2, j)
            for j in range(4):
                add_residual(1, 3, 1, j)
                final_root(2 + j, 16 + 12 + j + 1, range(j, j + 1), 44 + 4 * j)
                if j < 3:
                    scale(j)
                else:
                    for i in range(2):
                        scale(j, slice(1024 * i, 1024 * i + 1024))

        @block.tensor
        def _(pe):
            def turn(b, srcs, inc):
                for i, src in enumerate(srcs):
                    last = pe.transpose(b[:, P * i:P * i + P], src, ident[:, :])
                last.then_inc(inc, 1)

            def norm_turn(j, raw):
                pe.wait_ge(s.normed, j + 1)
                for kg in range(4):
                    if not (isinstance(j, int) and j < 2):
                        pe.wait_ge(s.tr_lo, 4 * j + kg - 3)
                    turn(norm_bank(j, kg), [raw[:, P * (4 * kg + i):P * (4 * kg + i) + P] for i in range(4)], s.turned)

            pe.wait_ge(s.ident_ready, 1)
            norm_turn(0, mem_raw[:, 0, :])
            norm_turn(1, mem_raw[:, 1, :])

            def three(dst, hi, lo, rhs_hi, rhs_lo, start, stop):
                for d, r in zip(dst, rhs_hi):
                    pe.matmul(d, hi, r, start=start, stop=False)
                for d, r in zip(dst, rhs_lo):
                    pe.matmul(d, hi, r, start=False, stop=False)
                for d, r in zip(dst, rhs_hi):
                    last = pe.matmul(d, lo, r, start=False, stop=stop)
                return last

            def begin(t, e, half_t):
                if not (isinstance(t, int) and t < 2):
                    pe.wait_ge(proj_free[e], half_t)

            def mem_tile(t, e, half_t):
                begin(t, e, half_t)
                for c in range(4):
                    pe.wait_ge(s.w_low, 4 * t + c + 1)
                    for i in range(4):
                        k = 4 * c + i
                        last = three([PROJ[e][:, 0, 0:NMEM]], w_hi[:, c, P * i:P * i + P], w_lo[:, c, P * i:P * i + P],
                                     [memT_hi[:, k, :]], [memT_lo[:, k, :]], k == 0, k == 15)
                    last.then_inc(s.w_used, 1)

            def mem_values(t):
                if t == CH:
                    for e in range(2):
                        pe.wait_ge(proj_free[e], 2)
                for c in range(4):
                    pe.wait_ge(s.w_low, 4 * t + c + 1)
                    k = 4 * (t - CH) + c
                    for e in range(2):
                        last = three([PROJ[e][:, 0, :]], memT_hi[:, k, P * e:P * e + P], memT_lo[:, k, P * e:P * e + P],
                                     [w_hi[:, c, :]], [w_lo[:, c, :]], k == 0, k == KT - 1)
                    last.then_inc(s.w_used, 1)

            def slot_of(t, e, half_t, j, width=P):
                if j == 0:
                    begin(t, e, half_t)
                c = j // 2
                if j % 2 == 0:
                    pe.wait_ge(s.w_low, 4 * t + c + 1)
                for k in (2 * j, 2 * j + 1):
                    i = k % 4
                    last = three([PROJ[e][0:width, half, :] for half in range(2)],
                                 w_hi[:, c, P * i:P * i + width], w_lo[:, c, P * i:P * i + width],
                                 [hn_hi[:, k, 512 * half:512 * half + 512] for half in range(2)],
                                 [hn_lo[:, k, 512 * half:512 * half + 512] for half in range(2)], k == 0, k == 15)
                if j % 2 == 1:
                    last.then_inc(s.w_used, 1)

            def turn_values(e, stage, count):
                pe.wait_ge(s.stage_ready, count)
                p = wide(PROJ[e])
                for i in range(NB):
                    last = pe.transpose(p[:, P * i:P * i + P], stage[:, P * i:P * i + P], ident[:, :])
                last.then_inc(s.v_turned, 1)

            for t in range(MEM_TILES):
                norm_turn(t + 2, x_raw[:, t % 2, :])
                if t < CH:
                    mem_tile(t, t % 2, t // 2)
                else:
                    mem_values(t)
            pe.wait_ge(s.tr_lo, 40)

            for t in (T_AK, T_AV, T_IQ, T_IQ + 1):
                for j in range(8):
                    slot_of(t, t % 2, t // 2, j)
                    if t == T_IQ and j == 1:
                        turn_values(1, av_stage, 1)
            for j in range(8):
                slot_of(T_IK, 0, T_IK // 2, j, width=P)
            for j in range(8):
                slot_of(T_Q0, 1, T_Q0 // 2, j)
                if j == 1:
                    pe.wait_ge(s.pg_free, T_IK // 2 + 1)
                    for b in range(NB):
                        last = pe.transpose(T[:, 4 * b:4 * b + 4], iwT[CHUNK:IKW, P * b:P * b + P], ident[CHUNK:IKW, CHUNK:IKW])
                    last.then_inc(s.iw_turned, 1)
                    pe.wait_ge(s.stack_low, 6)
                for u in range(sum(UNITS_AT[:j]), sum(UNITS_AT[:j + 1])):
                    b, h = 2 + u // 4, u % 4
                    if u == 1:
                        pe.wait_ge(s.iw_ready, 1)
                    if u >= 2:
                        pe.wait_ge(s.relu_ready, u - 1)
                    dst = wide(L if u % 2 == 0 else TO)
                    for a in range(0, P * (b + 1), 512):
                        z = max(min(a + 512, P * (b + 1)), a + 256)
                        for part, keys in enumerate((ik_hh, ik_ll)):
                            last = pe.matmul(dst[:, a:z], iq_hl[h][:, P * b:P * b + P], keys[:, a:z],
                                             start=part == 0, stop=part == 1)
                    last.then_inc(s.idx_ready, 1)

            def logits(m, b, kind, group):
                if kind == "C":
                    if b == 0:
                        pe.wait_ge(s.pq_free, m + 7)
                        pe.wait_ge(s.memkv_ready, m + 1)
                    if b >= 2:
                        pe.wait_ge(s.probs_ready, 8 * m + b - 1)
                    last = pe.matmul(L[:, b % 2, 0:NMEM], q0[:, P * b:P * b + P], mk_now[:, :], start=True, stop=True)
                else:
                    if b == 0:
                        pe.wait_ge(s.pq_free, m + 7)
                    if b >= 2:
                        pe.wait_ge(s.S_max, 8 * m + b - 1)
                    a = P * max(b - 1, 0)
                    for e in range(2):
                        for part, keys in enumerate((k_hh, k_ll)):
                            last = pe.matmul(L[:, b % 2, 256 * e:256 * e + 256], q_hl[e][:, P * b:P * b + P],
                                             keys[group][:, a:a + 256], start=part == 0, stop=part == 1)
                last.then_inc(s.logits_ready, 1)

            def turn_probs(m, b, kind):
                pe.wait_ge(s.norm_ready, 8 * m + b + 1)
                for kt in range(1 if kind == "A" and b == 0 else 0, 2):
                    for e in range(2 if kind == "A" else 1):
                        i = 2 * kt + e if kind == "A" else kt
                        last = pe.transpose(T[:, P * i:P * i + P], SA[:, b % 3, e, P * kt:P * kt + P], ident[:, :])
                last.then_inc(s.pt_ready, 1)

            def weigh(m, b, kind, group):
                pe.wait_ge(s.pt_copied, 8 * m + b + 1)
                if b >= 1:
                    pe.wait_ge(s.ot_copied, 8 * m + b)
                if kind == "C":
                    for kt in range(2):
                        last = pe.matmul(O[:, 0:P], mv_now[:, kt, :], PT[:, P * kt:P * kt + P], start=kt == 0, stop=kt == 1)
                else:
                    kts = (1,) if b == 0 else (0, 1)
                    for e in range(2):
                        for kt in kts:
                            i = 2 * kt + e
                            last = pe.matmul(O[CHUNK * e:CHUNK * e + CHUNK, 0:P],
                                             av[:, b - 1 + kt, CHUNK * group:CHUNK * group + CHUNK],
                                             PT_A[:, P * i:P * i + P], start=kt == kts[0], stop=kt == 1)
                last.then_inc(s.ot_ready, 1)

            def mix(m, kind, group):
                for slot in range(16):
                    t = T_LOOP + 2 * m + slot // 8
                    slot_of(t, slot // 8, m + 7, slot % 8)
                    b = slot - SHIFT[kind]
                    if 0 <= b - 4 < NB:
                        weigh(m, b - 4, kind, group)
                    if 0 <= b - 3 < NB:
                        turn_probs(m, b - 3, kind)
                    if 0 <= b < NB:
                        logits(m, b, kind, group)

            with pe.Fori(0, 4) as m:
                mix(m, "C", 0)
            with pe.Fori(4, 8) as m:
                mix(m, "A", 0)
            pe.wait_ge(s.k1_low, 2)
            with pe.Fori(8, 12) as m:
                mix(m, "A", 1)

            for t in (T_B, T_B + 1):
                for j in range(8):
                    slot_of(t, t % 2, t // 2, j)

            def out_step(q, e, half, k):
                if half == 0 and q == 0:
                    if k < 15:
                        pe.wait_ge(y_loaded[k], 32)
                    else:
                        pe.wait_ge(s.y_low, 16)
                pe.wait_ge(s.w_low, N_TAIL + 2 * k + 1 if q == 6 else N_OUT + 16 * q + k + 1)
                c = k % 4
                for j in range(4):
                    dst = bank[4 * e + j]
                    cols = slice(512 * half + P * j, 512 * half + P * j + P)
                    pe.matmul(dst, y_hi[:, k, cols], w_hi[:, c, :], start=k == 0, stop=False)
                    pe.matmul(dst, y_hi[:, k, cols], w_lo[:, c, :], start=False, stop=False)
                    last = pe.matmul(dst, y_lo[:, k, cols], w_hi[:, c, :], start=False, stop=k == 15)
                    if k == 15 and j < 3:
                        last.then_inc(s.out_done, 1)
                last.then_inc(s.w_used, 1)

            def head(h, pos):
                m = 12 + h
                q, bk, bv = (q0, q1)[h % 2], (bk0, bk1)[h % 2], (bv0, bv1)[h % 2]
                for slot in range(24 if h == BH - 1 else 32):
                    if h < BH - 1 or slot < 8:
                        t = T_BHEAD + 4 * h + slot // 8
                        slot_of(t, t % 2, t // 2, slot % 8)
                    if slot == 1:
                        turn_values(1, bv_stage, 2 + h)
                    for b in range(NB):
                        if slot == pos[b] + 5:
                            pe.wait_ge(s.bpt_copied, 12 * h + (2 * b - 2 if b >= 4 else b + 1))
                            if b >= 1:
                                pe.wait_ge(s.ot_copied, 8 * m + b)
                            else:
                                pe.wait_ge(s.pq_free, 20 + 2 * h)
                            for kt in range(b + 1):
                                last = pe.matmul(O[:, 0:P], bv[:, kt, :], PT[:, P * kt:P * kt + P], start=kt == 0, stop=kt == b)
                            last.then_inc(s.ot_ready, 1)
                    for b in range(4, NB):
                        if slot == pos[b] + 4:
                            pe.wait_ge(s.bpt_copied, 12 * h + 2 * b - 3)
                            for kt in range(4, b + 1):
                                last = pe.transpose(T[:, P * (kt - 4):P * (kt - 3)], SB[:, b % 2, P * kt:P * kt + P], ident[:, :])
                            last.then_inc(s.bpt_ready, 1)
                    for b in range(NB):
                        if slot == pos[b] + 3:
                            pe.wait_ge(s.norm_ready, 8 * m + b + 1)
                            for kt in range(min(4, b + 1)):
                                last = pe.transpose(T[:, P * kt:P * kt + P], SB[:, b % 2, P * kt:P * kt + P], ident[:, :])
                            last.then_inc(s.bpt_ready, 1)
                    if slot in pos:
                        b = pos.index(slot)
                        if b == 0:
                            pe.wait_ge(s.pq_free, 19 if h == 0 else 19 + 2 * h)
                            pe.wait_ge(s.pg_free, 20 + 2 * h)
                        else:
                            pe.wait_ge(s.S_biased, 8 * h + b)
                        for a in range(0, P * (b + 1), 512):
                            z = min(a + 512, P * (b + 1))
                            last = pe.matmul(wide(L)[:, a:z], q[:, P * b:P * b + P], bk[:, a:z], start=True, stop=True)
                        last.then_inc(s.logits_ready, 1)
                    if h == BH - 1 and slot >= 8:
                        if slot == 8:
                            pe.wait_ge(s.pg_free, 27)
                        out_step(0, 0, 0, slot - 8)

            for h in range(BH - 1):
                head(h, B_POS)
            head(BH - 1, B_LAST)

            def out_tile(q, e, half):
                pe.wait_ge(s.out_free, 4 * q + 4)
                for k in range(16):
                    out_step(q, e, half, k)

            for q in range(1, 4):
                out_tile(q, q % 2, 0)
            for k in range(15):
                pe.wait_ge(y_loaded[k], 64)
            pe.wait_ge(s.y_low, 17)
            for q in range(4, 7):
                out_tile(q, q % 2, 1)
            pe.wait_ge(s.out_free, 32)
            for j in range(4):
                cols = slice(512 + P * j, 512 + P * j + P)
                for k in range(16):
                    if j == 0:
                        pe.wait_ge(s.w_low, N_TAIL + 2 * k + 2)
                    high, low = tail_chunk(2 * k + 1)
                    last = three([bank[4 + j]], y_hi[:, k, cols], y_lo[:, k, cols], [high], [low], k == 0, k == 15)
                last.then_inc(*((s.out_done, 1) if j < 3 else (s.w_used, 16)))


_INS = ["x", "mem", "g_norm", "w_in", "sinks", "rel_bias", "g_mem", "w_mem_kv", "w_out", "g_final"]
_OUTS = [((1, SEQ, D), "float32")]


def kernel(**inputs):
    import numpy as _np
    import concourse.bacc as _bacc
    from concourse import mybir as _mybir
    from concourse.bass_utils import run_bass_kernel_spmd as _run

    nc = _bacc.Bacc("TRN2", target_bir_lowering=False, num_devices=1, dynamic_dma_scratch_size=256)
    arrays, args = {}, []
    for name in _INS:
        a = _np.ascontiguousarray(inputs[name])
        arrays[f"in_{name}_dram"] = a
        args.append(nc.dram_tensor(f"in_{name}_dram", a.shape, _mybir.dt.from_np(a.dtype), kind="ExternalInput").ap())
    for i, (shape, dtype) in enumerate(_OUTS):
        dt = _mybir.dt.from_np(_np.dtype(dtype))
        args.append(nc.dram_tensor(f"out_{i}_dram", shape, dt, kind="ExternalOutput").ap())
    hybrid_layer(nc, *args)
    r = _run(nc, [arrays], core_ids=[0])
    got = tuple(r.results[0][f"out_{i}_dram"] for i in range(len(_OUTS)))
    return got[0]
```
